# Optimizing a Trainium2 kernel written in Bass

```python
import math
import jax, jax.numpy as jnp
from jax import lax
import numpy as np

D_MODEL = 1024
BATCH = 1
SEQ = 1024
DEPTH = 1
DEC_BATCH = 8
DEC_SEQ = 1
PAST_LEN = 1024
PAGE_SIZE = 128

MIX_WIDTH = D_MODEL
FOX_HEADS = 8
FOX_HEAD_DIM = 64
FOX_WIDTH = FOX_HEADS * FOX_HEAD_DIM
GDN_HEADS = 4
GDN_HEAD_DIM = 128
GDN_WIDTH = GDN_HEADS * GDN_HEAD_DIM
GDN_CONV = 4
GDN_CHUNK = 64
FFN_DIM = 2816
FFN_CONV = 3
Q_BLOCK = 128
EPS = 1e-6
NEG_BIG = -1e30
FORGET_BIAS_INIT = 2.0
IN_SECTIONS = (FOX_WIDTH, FOX_WIDTH, FOX_WIDTH, FOX_HEADS,
               GDN_WIDTH, GDN_WIDTH, GDN_WIDTH, GDN_HEADS, GDN_HEADS, GDN_WIDTH)
IN_WIDTH = sum(IN_SECTIONS)
SPLIT_POINTS = tuple(sum(IN_SECTIONS[:i + 1]) for i in range(len(IN_SECTIONS) - 1))
GDN_QKV_SPLIT = (GDN_WIDTH, 2 * GDN_WIDTH)

kernel_name = 'fox_gdn_parallel_heads_convffn_step'

def rms_norm(x, g):
    xf = x.astype(jnp.float32)
    y = xf * lax.rsqrt(jnp.mean(xf * xf, axis=-1, keepdims=True) + EPS)
    return (y * g.astype(jnp.float32)).astype(x.dtype)

def l2_normalize(x):
    xf = x.astype(jnp.float32)
    return xf * lax.rsqrt(jnp.sum(xf * xf, axis=-1, keepdims=True) + EPS)

def gather_pages(pool, page_table):
    pages = pool[page_table]
    b, n_pages = page_table.shape
    return pages.reshape((b, n_pages * pool.shape[1]) + pool.shape[2:])

def causal_depthwise_conv(x, ctx, w, b=None):
    width = w.shape[0]
    t = x.shape[1]
    xc = jnp.concatenate([ctx.astype(x.dtype), x], axis=1)
    y = xc[:, 0:t] * w[0]
    for i in range(1, width):
        y = y + xc[:, i:i + t] * w[i]
    if b is not None:
        y = y + b
    return y, xc[:, -(width - 1):]

def fox_attention(q, k, v, cq, ck, q_pos, k_pos):
    b, tq, h, dh = q.shape
    blk = min(Q_BLOCK, tq)
    n_blk = -(-tq // blk)
    pad = n_blk * blk - tq
    q = jnp.pad(q, ((0, 0), (0, pad), (0, 0), (0, 0)))
    cq = jnp.pad(cq, ((0, 0), (0, pad), (0, 0)))
    q_pos = jnp.pad(q_pos, (0, pad), mode='edge')
    qb = q.reshape(b, n_blk, blk, h, dh).transpose(1, 0, 2, 3, 4)
    cqb = cq.reshape(b, n_blk, blk, h).transpose(1, 0, 3, 2)
    pb = q_pos.reshape(n_blk, blk)
    ck_t = jnp.transpose(ck, (0, 2, 1))
    scale = dh ** -0.5

    def one_block(args):
        q_blk, cq_blk, p_blk = args
        s = jnp.einsum('bqhd,bkhd->bhqk', q_blk, k,
                       preferred_element_type=jnp.float32) * scale
        s = s + (cq_blk[..., :, None] - ck_t[:, :, None, :])
        mask = k_pos[None, :] <= p_blk[:, None]
        s = jnp.where(mask, s, NEG_BIG)
        p = jax.nn.softmax(s, axis=-1)
        return jnp.einsum('bhqk,bkhd->bqhd', p.astype(v.dtype), v)

    out = lax.map(one_block, (qb, cqb, pb))
    return out.transpose(1, 0, 2, 3, 4).reshape(b, n_blk * blk, h, dh)[:, :tq]

def gated_delta_chunked(q, k, v, g, beta, s0):
    b, t, h, dk = q.shape
    dv = v.shape[-1]
    c = min(GDN_CHUNK, t)
    n = -(-t // c)
    pad = n * c - t
    f32 = jnp.float32
    q = q.astype(f32) * (dk ** -0.5)
    k = k.astype(f32)
    v = v.astype(f32)
    pad4 = ((0, 0), (0, pad), (0, 0), (0, 0))
    pad3 = ((0, 0), (0, pad), (0, 0))
    q, k, v = jnp.pad(q, pad4), jnp.pad(k, pad4), jnp.pad(v, pad4)
    g, beta = jnp.pad(g, pad3), jnp.pad(beta, pad3)

    def chunks(x):
        return x.reshape(b, n, c, h, x.shape[-1]).transpose(0, 3, 1, 2, 4)

    qc, kc, vc = chunks(q), chunks(k), chunks(v)
    gc = g.reshape(b, n, c, h).transpose(0, 3, 1, 2)
    bc = beta.reshape(b, n, c, h).transpose(0, 3, 1, 2)
    gcum = jnp.cumsum(gc, axis=-1)
    diff = gcum[..., :, None] - gcum[..., None, :]
    lower = jnp.tril(jnp.ones((c, c), dtype=bool))
    strict = jnp.tril(jnp.ones((c, c), dtype=bool), -1)
    decay = jnp.where(lower, jnp.exp(jnp.where(lower, diff, 0.0)), 0.0)
    kk = jnp.einsum('bhnid,bhnjd->bhnij', kc, kc)
    a_mat = jnp.where(strict, bc[..., :, None] * kk * decay, 0.0)
    lhs = a_mat + jnp.eye(c, dtype=f32)
    rhs = jnp.concatenate([vc * bc[..., None], kc * (bc * jnp.exp(gcum))[..., None]], axis=-1)
    sol = lax.linalg.triangular_solve(lhs, rhs, left_side=True, lower=True, unit_diagonal=True)
    u, w = sol[..., :dv], sol[..., dv:]
    qk = jnp.einsum('bhnid,bhnjd->bhnij', qc, kc) * decay
    q_dec = qc * jnp.exp(gcum)[..., None]
    k_dec = kc * jnp.exp(gcum[..., -1:] - gcum)[..., None]
    g_last = jnp.exp(gcum[..., -1])

    def step(s, xs):
        u_i, w_i, qk_i, qd_i, kd_i, gl_i = xs
        v_new = u_i - jnp.einsum('bhcd,bhde->bhce', w_i, s)
        o = jnp.einsum('bhcd,bhde->bhce', qd_i, s) + jnp.einsum('bhij,bhje->bhie', qk_i, v_new)
        s = s * gl_i[..., None, None] + jnp.einsum('bhcd,bhce->bhde', kd_i, v_new)
        return s, o

    xs = tuple(jnp.moveaxis(x, 2, 0) for x in (u, w, qk, q_dec, k_dec, g_last))
    s_final, o = lax.scan(step, s0.astype(f32), xs)
    o = o.transpose(1, 0, 3, 2, 4).reshape(b, n * c, h, dv)[:, :t]
    return o, s_final.astype(s0.dtype)

def decoder_layer(x, past_k, past_v, past_lf, s0, gdn_ctx, ffn_ctx,
                  norm_mix, w_in, b_forget, gdn_a_log, gdn_dt_bias, w_gdn_conv,
                  gdn_out_norm, w_out, norm_ffn, w_up, w_ffn_conv, b_ffn_conv, w_down):
    b, t, _ = x.shape
    p_len = past_k.shape[1]
    f32 = jnp.float32
    h = rms_norm(x, norm_mix)
    proj = h @ w_in
    fq, fk, fv, ff, gq, gk, gv, ga, gb, gz = jnp.split(proj, SPLIT_POINTS, axis=-1)

    fq = fq.reshape(b, t, FOX_HEADS, FOX_HEAD_DIM)
    fk = fk.reshape(b, t, FOX_HEADS, FOX_HEAD_DIM)
    fv = fv.reshape(b, t, FOX_HEADS, FOX_HEAD_DIM)
    lf = jax.nn.log_sigmoid(ff.astype(f32) + b_forget.astype(f32))
    k_all = jnp.concatenate([past_k.astype(fk.dtype), fk], axis=1)
    v_all = jnp.concatenate([past_v.astype(fv.dtype), fv], axis=1)
    cum = jnp.cumsum(jnp.concatenate([past_lf.astype(f32), lf], axis=1), axis=1)
    pos = jnp.arange(p_len + t)
    fox_out = fox_attention(fq, k_all, v_all, cum[:, p_len:], cum, pos[p_len:], pos)

    qkv = jnp.concatenate([gq, gk, gv], axis=-1)
    qkv_c, new_gdn_ctx = causal_depthwise_conv(qkv, gdn_ctx, w_gdn_conv)
    qkv_c = jax.nn.silu(qkv_c)
    cq, ck, cv = jnp.split(qkv_c, GDN_QKV_SPLIT, axis=-1)
    cq = l2_normalize(cq.reshape(b, t, GDN_HEADS, GDN_HEAD_DIM))
    ck = l2_normalize(ck.reshape(b, t, GDN_HEADS, GDN_HEAD_DIM))
    cv = cv.reshape(b, t, GDN_HEADS, GDN_HEAD_DIM)
    beta = jax.nn.sigmoid(gb.astype(f32))
    g = -jnp.exp(gdn_a_log.astype(f32)) * jax.nn.softplus(ga.astype(f32) + gdn_dt_bias.astype(f32))
    o, new_s = gated_delta_chunked(cq, ck, cv, g, beta, s0)
    o = rms_norm(o, gdn_out_norm) * jax.nn.silu(gz.reshape(b, t, GDN_HEADS, GDN_HEAD_DIM).astype(f32))

    mix = jnp.concatenate([fox_out.reshape(b, t, FOX_WIDTH),
                           o.reshape(b, t, GDN_WIDTH).astype(x.dtype)], axis=-1)
    x = x + mix @ w_out

    h2 = rms_norm(x, norm_ffn)
    gate, up = jnp.split(h2 @ w_up, 2, axis=-1)
    gate_c, new_ffn_ctx = causal_depthwise_conv(gate, ffn_ctx, w_ffn_conv, b_ffn_conv)
    x = x + (jax.nn.silu(gate_c) * up) @ w_down
    return x, (fk, fv, lf, new_s, new_gdn_ctx, new_ffn_ctx)

def setup_inputs(seed: int = 0) -> dict:
    key = jax.random.key(seed)
    ks = jax.random.split(key, 24)
    f32 = jnp.float32
    n_pages = PAST_LEN // PAGE_SIZE
    n_pool = (5 * DEC_BATCH * n_pages) // 4

    def nrm(k, shape, scale):
        return jax.random.normal(k, shape, f32) * scale

    x_prompt = nrm(ks[0], (BATCH, SEQ, D_MODEL), 1.0)
    x_sample = nrm(ks[1], (DEC_BATCH, DEC_SEQ, D_MODEL), 1.0)
    cache_k = nrm(ks[2], (DEPTH, n_pool, PAGE_SIZE, FOX_HEADS, FOX_HEAD_DIM), 1.0)
    cache_v = nrm(ks[3], (DEPTH, n_pool, PAGE_SIZE, FOX_HEADS, FOX_HEAD_DIM), 1.0)
    cache_logf = jax.nn.log_sigmoid(FORGET_BIAS_INIT + nrm(ks[4], (DEPTH, n_pool, PAGE_SIZE, FOX_HEADS), 1.0))
    state_gdn = nrm(ks[5], (DEPTH, DEC_BATCH, GDN_HEADS, GDN_HEAD_DIM, GDN_HEAD_DIM), GDN_HEAD_DIM ** -0.5)
    state_gdn_conv = nrm(ks[6], (DEPTH, DEC_BATCH, GDN_CONV - 1, 3 * GDN_WIDTH), 1.0)
    state_ffn_conv = nrm(ks[7], (DEPTH, DEC_BATCH, FFN_CONV - 1, FFN_DIM), 1.0)
    page_table = jax.random.permutation(ks[8], n_pool)[: DEC_BATCH * n_pages]
    page_table = page_table.reshape(DEC_BATCH, n_pages).astype(jnp.int32)

    norm_mix = 1.0 + nrm(ks[9], (DEPTH, D_MODEL), 0.02)
    w_in = nrm(ks[10], (DEPTH, D_MODEL, IN_WIDTH), D_MODEL ** -0.5)
    b_forget = FORGET_BIAS_INIT + nrm(ks[11], (DEPTH, FOX_HEADS), 0.5)
    gdn_a_log = jnp.log(jax.random.uniform(ks[12], (DEPTH, GDN_HEADS), f32, 1.0, 16.0))
    dt = jnp.exp(jax.random.uniform(ks[13], (DEPTH, GDN_HEADS), f32, math.log(1e-3), math.log(1e-1)))
    gdn_dt_bias = dt + jnp.log(-jnp.expm1(-dt))
    w_gdn_conv = nrm(ks[14], (DEPTH, GDN_CONV, 3 * GDN_WIDTH), GDN_CONV ** -0.5)
    gdn_out_norm = 1.0 + nrm(ks[15], (DEPTH, GDN_HEAD_DIM), 0.02)
    w_out = nrm(ks[16], (DEPTH, MIX_WIDTH, D_MODEL), MIX_WIDTH ** -0.5)
    norm_ffn = 1.0 + nrm(ks[17], (DEPTH, D_MODEL), 0.02)
    w_up = nrm(ks[18], (DEPTH, D_MODEL, 2 * FFN_DIM), D_MODEL ** -0.5)
    w_ffn_conv = nrm(ks[19], (DEPTH, FFN_CONV, FFN_DIM), FFN_CONV ** -0.5)
    b_ffn_conv = nrm(ks[20], (DEPTH, FFN_DIM), 0.02)
    w_down = nrm(ks[21], (DEPTH, FFN_DIM, D_MODEL), FFN_DIM ** -0.5)
    norm_final = 1.0 + nrm(ks[22], (D_MODEL,), 0.02)
    return {
        'x_prompt': x_prompt, 'x_sample': x_sample,
        'cache_k': cache_k, 'cache_v': cache_v, 'cache_logf': cache_logf,
        'state_gdn': state_gdn, 'state_gdn_conv': state_gdn_conv, 'state_ffn_conv': state_ffn_conv,
        'page_table': page_table,
        'norm_mix': norm_mix, 'w_in': w_in, 'b_forget': b_forget,
        'gdn_a_log': gdn_a_log, 'gdn_dt_bias': gdn_dt_bias, 'w_gdn_conv': w_gdn_conv,
        'gdn_out_norm': gdn_out_norm, 'w_out': w_out, 'norm_ffn': norm_ffn,
        'w_up': w_up, 'w_ffn_conv': w_ffn_conv, 'b_ffn_conv': b_ffn_conv,
        'w_down': w_down, 'norm_final': norm_final,
    }

def reference(x_prompt, x_sample, cache_k, cache_v, cache_logf, state_gdn, state_gdn_conv,
              state_ffn_conv, page_table, norm_mix, w_in, b_forget, gdn_a_log, gdn_dt_bias,
              w_gdn_conv, gdn_out_norm, w_out, norm_ffn, w_up, w_ffn_conv, b_ffn_conv,
              w_down, norm_final):
    yp, ys = x_prompt, x_sample
    bp = x_prompt.shape[0]
    new_p, new_s = [], []
    for layer in range(DEPTH):
        params = (norm_mix[layer], w_in[layer], b_forget[layer], gdn_a_log[layer],
                  gdn_dt_bias[layer], w_gdn_conv[layer], gdn_out_norm[layer], w_out[layer],
                  norm_ffn[layer], w_up[layer], w_ffn_conv[layer], b_ffn_conv[layer], w_down[layer])
        yp, st_p = decoder_layer(
            yp,
            jnp.zeros((bp, 0, FOX_HEADS, FOX_HEAD_DIM), yp.dtype),
            jnp.zeros((bp, 0, FOX_HEADS, FOX_HEAD_DIM), yp.dtype),
            jnp.zeros((bp, 0, FOX_HEADS), jnp.float32),
            jnp.zeros((bp, GDN_HEADS, GDN_HEAD_DIM, GDN_HEAD_DIM), jnp.float32),
            jnp.zeros((bp, GDN_CONV - 1, 3 * GDN_WIDTH), yp.dtype),
            jnp.zeros((bp, FFN_CONV - 1, FFN_DIM), yp.dtype),
            *params)
        ys, st_s = decoder_layer(
            ys,
            gather_pages(cache_k[layer], page_table),
            gather_pages(cache_v[layer], page_table),
            gather_pages(cache_logf[layer], page_table),
            state_gdn[layer], state_gdn_conv[layer], state_ffn_conv[layer],
            *params)
        new_p.append(st_p)
        new_s.append(st_s)
    y_prompt = rms_norm(yp, norm_final)
    y_sample = rms_norm(ys, norm_final)
    k_p, v_p, lf_p, s_p, gc_p, fc_p = [jnp.stack(t, axis=0) for t in zip(*new_p)]
    k_s, v_s, lf_s, s_s, gc_s, fc_s = [jnp.stack(t, axis=0) for t in zip(*new_s)]
    return (y_prompt, y_sample, k_p, v_p, lf_p, s_p, gc_p, fc_p, k_s, v_s, lf_s, s_s, gc_s, fc_s)


_drawn_inputs = setup_inputs


def setup_inputs(seed=0):
    import zlib

    import numpy as np

    out = dict(_drawn_inputs(seed))
    spreads = {}
    factors = {'gdn_out_norm': 6.423, 'norm_ffn': 2.8, 'b_ffn_conv': 5.979, 'norm_final': 2.829}
    for name, (base, spread) in spreads.items():
        noise = np.random.default_rng([zlib.crc32(name.encode()), seed]).standard_normal(out[name].shape)
        drawn = base * np.exp(spread * noise) if base else spread * noise
        out[name] = __import__('jax').numpy.asarray(drawn.astype(out[name].dtype))
    for name, factor in factors.items():
        out[name] = (out[name] * factor).astype(out[name].dtype)
    return out
```

```python
from contextlib import ExitStack

import concourse.bass as bass
from concourse import mybir

ALU = mybir.AluOpType
ACT = mybir.ActivationFunctionType
AX = mybir.AxisListType
F32 = mybir.dt.float32
F32R = mybir.dt.float32r
I32 = mybir.dt.int32
RMAX = bass.bass_isa.ReduceOp.max
ds = bass.ds

P = 128
D = 1024
KC = D // P
SEQ = 1024
NBLK = SEQ // P
DEC = 8
TOK = SEQ + DEC
GRP = TOK // 3
NG = TOK // GRP
FH, FD = 8, 64
FW = FH * FD
GH, GD = 4, 128
GW = GH * GD
PAGES = 8
TAPS = 4
EXT = (TAPS - 1) + SEQ + TAPS * DEC
CONV = EXT - (TAPS - 1)
FFN = 2816
FT = FFN // P
FTAPS = 3
FEXT = (FTAPS - 1) + SEQ + FTAPS * DEC
FCONV = FEXT - (FTAPS - 1)
EPS = 1e-6
NEG_BIG = -1e30
SCALE = FD ** -0.5
LN_GSCALE = -0.5 * 4.852030263919617
STEPS = 4
R_F, R_A, R_B, GROWS = 0, 32, 64, 96
C_FQ, C_FK, C_FV, C_FF = 0, FW, 2 * FW, 3 * FW
C_GQ = C_FF + FH
C_GK, C_GV = C_GQ + GW, C_GQ + 2 * GW
C_GA = C_GQ + 3 * GW
C_GZ = C_GA + 2 * GH
TILE_COL = (C_FQ, C_FK, C_FV, C_GQ, C_GK, C_GV, C_GZ)
NTILE = len(TILE_COL)


class OnChip:

    def __init__(self, sem, mixer_sem, sb, ps, x_dram, mix_dram, gate_dram, ident, ones, head_ones, later,
                 causal, level_mask, norms, gconv, fconv, out_norm, hi, lo, logf_n,
                 beta_n, gcum_n, page_ids, dec_bias, dec_gates):
        self.sem = sem
        self.mixer_sem = mixer_sem
        self.sb = sb
        self.ps = ps
        self.x_dram = x_dram
        self.mix_dram = mix_dram
        self.gate_dram = gate_dram
        self.ident = ident
        self.ones = ones
        self.head_ones = head_ones
        self.later = later
        self.causal = causal
        self.level_mask = level_mask
        self.norms = norms
        self.gconv = gconv
        self.fconv = fconv
        self.out_norm = out_norm
        self.hi = hi
        self.lo = lo
        self.logf_n = logf_n
        self.beta_n = beta_n
        self.gcum_n = gcum_n
        self.page_ids = page_ids
        self.dec_bias = dec_bias
        self.dec_gates = dec_gates


def groups(width, n):
    step = width // n
    return [(g * step, step) for g in range(n)]


def program(nc, t):
    stack = ExitStack()
    mixer_sems = []

    def sem(name):
        return stack.enter_context(nc.semaphore(name))

    def mixer_sem(name):
        mixer_sems.append(nc.alloc_semaphore(name))
        return mixer_sems[-1]

    def sb(name, shape, dt=F32, scope=None):
        return (scope or stack).enter_context(nc.sbuf_tensor(name, shape, dt))

    with stack:
        ps = stack.enter_context(nc.psum_tensor("ps", [P, 8, 512], F32))
        x_dram = nc.dram_tensor("x_scratch", [P, KC, TOK], F32, kind="Internal").ap()
        mix_dram = nc.dram_tensor("mix_scratch", [KC, P, TOK], F32, kind="Internal").ap()
        gate_dram = nc.dram_tensor("gate_scratch", [GROWS, SEQ], F32, kind="Internal").ap()

        ident = sb("ident", [P, P])
        ones = sb("ones", [P, P])
        head_ones = sb("head_ones", [P, 2, P])
        later = sb("later", [P, P])
        causal = sb("causal", [P, P])
        level_mask = sb("level_mask", [P, 7, P])
        norms = sb("norms", [P, KC, 3])
        gconv = sb("gconv", [P, 3 * GH, 28])
        fconv = sb("fconv", [P, FT, 20])
        out_norm = sb("out_norm", [P, 1])
        hi = sb("act_hi", [P, KC, TOK], F32R)
        lo = sb("act_lo", [P, KC, TOK], F32R)
        logf_n = sb("logf_n", [P, NBLK + 1, FH])
        beta_n = sb("beta_n", [P, NBLK, GH])
        gcum_n = sb("gcum_n", [P, NBLK, GH])
        page_ids = sb("page_ids", [1, DEC * PAGES], I32)
        dec_bias = sb("dec_bias", [P, DEC * PAGES, FH])
        dec_gates = sb("dec_gates", [P, 2, GH, DEC])

        v = OnChip(sem, mixer_sem, sb, ps, x_dram, mix_dram, gate_dram, ident, ones, head_ones, later,
                   causal, level_mask, norms, gconv, fconv, out_norm, hi, lo,
                   logf_n, beta_n, gcum_n, page_ids, dec_bias, dec_gates)

        setup(nc, t, v)
        gates(nc, t, v)
        mixer(nc, t, v)
        nc.clear_and_free_semaphores(mixer_sems)
        nc.all_engine_barrier()
        out_projection(nc, t, v)
        ffn_up_down(nc, t, v)
        finish(nc, t, v)


def split_piece(pe, out, w_hi, w_lo, a_hi, a_lo, k, first, last):
    pe.matmul(out, w_hi, a_hi, start=first, stop=False)
    pe.matmul(out, w_hi, a_lo, start=False, stop=False)
    return pe.matmul(out, w_lo, a_hi, start=False, stop=last)


def setup(nc, t, v):
    with ExitStack() as scope:
        def sb(name, shape, dt=F32):
            return v.sb(name, shape, dt, scope)

        xT = sb("xT0", [P, KC, TOK])
        xn = sb("x_rows", [P, 2, D])
        vec_rows = sb("vec_rows", [3, D])
        gconv_rows = sb("gconv_rows", [28, 3 * GW])
        fconv_rows = sb("fconv_rows", [20, FFN])
        sq = sb("sq0", [P, KC, GRP])
        rstd = sb("rstd0", [P, TOK])
        tmp = sb("h_tmp0", [P, 2, TOK])
        ps = v.ps
        x_loaded = [v.sem("x_loaded0"), v.sem("x_loaded1")]
        params_loaded, consts_ready = v.sem("params_loaded"), v.sem("consts_ready")
        x_turned, x_copied = v.sem("x_turned"), v.sem("x_copied")
        par_turned, par_copied = v.sem("par_turned"), v.sem("par_copied")
        x_saved = v.sem("x_saved")
        S = norm_signals(v, "n0")
        rows = [(i, P) for i in range(NBLK)] + [(NBLK, DEC)]

        block = scope.enter_context(nc.Block())

        @block.sync
        def _(sp):
            for i in range(2):
                sp.dma_start(xn[:, i], t["x_prompt"][0, i * P:(i + 1) * P]).then_inc(x_loaded[i], 16)
            sp.dma_start(vec_rows[0:1, :], t["norm_mix"]).then_inc(params_loaded, 16)
            sp.dma_start(vec_rows[1:2, :], t["norm_ffn"]).then_inc(params_loaded, 16)
            sp.dma_start(vec_rows[2:3, :], t["norm_final"].rearrange("(a d) -> a d", a=1)).then_inc(params_loaded, 16)
            sp.dma_start(gconv_rows[0:4, :], t["w_gdn_conv"][0]).then_inc(params_loaded, 16)
            sp.dma_start(gconv_rows[4:28, :], t["state_gdn_conv"][0].rearrange("b i c -> (b i) c")).then_inc(params_loaded, 16)
            sp.dma_start(fconv_rows[0:3, :], t["w_ffn_conv"][0]).then_inc(params_loaded, 16)
            sp.dma_start(fconv_rows[3:4, :], t["b_ffn_conv"]).then_inc(params_loaded, 16)
            sp.dma_start(fconv_rows[4:20, :], t["state_ffn_conv"][0].rearrange("b i c -> (b i) c")).then_inc(params_loaded, 16)
            sp.dma_start(v.out_norm[:], t["gdn_out_norm"].rearrange("a d -> d a")).then_inc(params_loaded, 16)
            sp.dma_start(v.page_ids[:], t["page_table"].rearrange("b p -> (b p)").rearrange("(a n) -> a n", a=1)).then_inc(params_loaded, 16)
            with sp.Fori(1, NBLK // 2) as it:
                for i in range(2):
                    sp.wait_ge(x_turned, it * 2 + i - 1)
                    sp.dma_start(xn[:, i], t["x_prompt"][0, ds((it * 2 + i) * P, P)]).then_inc(x_loaded[i], 16)
            sp.wait_ge(x_turned, NBLK - 1)
            sp.dma_start(xn[0:DEC, 0], t["x_sample"].rearrange("b a d -> (b a) d")).then_inc(x_loaded[0], 16)
            sp.wait_ge(x_copied, NBLK + 1)
            sp.dma_start(v.x_dram, xT[:]).then_inc(x_saved, 16)
            sp.wait_ge(x_saved, 16)

        @block.gpsimd
        def _(pool):
            pool.memset(v.ident[:], 0.0)
            pool.memset(v.ones[:], 1.0)
            pool.memset(v.later[:], 1.0)
            pool.memset(v.causal[:], 0.0)
            pool.memset(v.head_ones[:], 0.0)
            pool.memset(v.level_mask[:], 0.0)
            pool.drain()
            pool.memset(v.head_ones[0:FD, 0], 1.0)
            pool.drain()
            pool.memset(v.head_ones[FD:P, 1], 1.0)
            pool.drain()
            for l in range(7):
                b = 1 << l
                m = v.level_mask[:, l].rearrange("p (n w) -> p n w", w=2 * b)
                pool.memset(m[:, :, b:2 * b], 1.0)
            pool.affine_select(out=v.ident[:], in_=v.ident[:], compare_op=ALU.not_equal, fill=1.0, base=0,
                               pattern=[[-1, P]], channel_multiplier=1)
            pool.affine_select(out=v.later[:], in_=v.later[:], compare_op=ALU.is_ge, fill=0.0, base=-1,
                               pattern=[[-1, P]], channel_multiplier=1)
            pool.affine_select(out=v.causal[:], in_=v.causal[:], compare_op=ALU.is_ge, fill=NEG_BIG / SCALE, base=0,
                               pattern=[[-1, P]], channel_multiplier=1)
            pool.drain()
            for l in range(7):
                b = 1 << l
                m = v.level_mask[:, l].rearrange("p (n w) -> p n w", w=2 * b)
                n = P // (2 * b)
                pool.affine_select(out=m, in_=m, compare_op=ALU.is_ge, fill=0.0, base=0,
                                   pattern=[[-2 * b, n], [0, 2 * b]], channel_multiplier=1)
                pool.drain()
                pool.affine_select(out=m, in_=m, compare_op=ALU.is_ge, fill=0.0, base=b - 1,
                                   pattern=[[2 * b, n], [0, 2 * b]], channel_multiplier=-1)
            pool.drain()
            pool.drain().then_inc(consts_ready, 1)

        def turn(pe, i, slot, n, last_of):
            for k in range(KC):
                mm = pe.transpose(ps[:, 2 * slot + k // 4, (k % 4) * P:(k % 4) * P + n],
                                  xn[0:n, slot, k * P:(k + 1) * P], v.ident[0:n, 0:n])
            mm.then_inc(x_turned, 1)

        @block.tensor
        def _(pe):
            pe.wait_ge(consts_ready, 1)
            for i in range(2):
                pe.wait_ge(x_loaded[i], 16)
                turn(pe, i, i, P, None)
            with pe.Fori(1, NBLK // 2) as it:
                for i in range(2):
                    pe.wait_ge(x_loaded[i], it * 16 + 16)
                    pe.wait_ge(x_copied, it * 2 + i - 1)
                    turn(pe, i, i, P, None)
            pe.wait_ge(x_loaded[0], 16 * (NBLK // 2 + 1))
            pe.wait_ge(x_copied, NBLK - 1)
            turn(pe, NBLK, 0, DEC, None)
            pe.wait_ge(params_loaded, 160)
            for k in range(KC):
                pe.transpose(ps[:, 4, k * 3:k * 3 + 3], vec_rows[0:3, k * P:(k + 1) * P], v.ident[0:3, 0:3])
            for k in range(3 * GH):
                pe.transpose(ps[:, 5, k * 28:k * 28 + 28], gconv_rows[:, k * P:(k + 1) * P], v.ident[0:28, 0:28])
            for k in range(FT):
                mm = pe.transpose(ps[:, 6, k * 20:k * 20 + 20], fconv_rows[:, k * P:(k + 1) * P], v.ident[0:20, 0:20])
            mm.then_inc(par_turned, 1)
            norm_pe(pe, v, S, sq)

        def copy_out(dve, slot, n, cols):
            for half in range(2):
                src = ps[:, 2 * slot + half].rearrange("p (k t) -> p k t", k=4)[:, :, 0:n]
                ins = dve.tensor_copy(xT[:, 4 * half:4 * half + 4, cols], src)
            ins.then_inc(x_copied, 1)

        @block.vector
        def _(dve):
            with dve.Fori(0, NBLK // 2) as it:
                for i in range(2):
                    dve.wait_ge(x_turned, it * 2 + i + 1)
                    copy_out(dve, i, P, ds((it * 2 + i) * P, P))
            dve.wait_ge(x_turned, NBLK + 1)
            copy_out(dve, 0, DEC, slice(SEQ, TOK))
            dve.wait_ge(par_turned, 1)
            dve.tensor_copy(v.norms[:].rearrange("p k n -> p (k n)"), ps[:, 4, 0:3 * KC])
            dve.tensor_copy(v.gconv[:].rearrange("p k n -> p (k n)"), ps[:, 5, 0:28 * 3 * GH])
            dve.tensor_copy(v.fconv[:].rearrange("p k n -> p (k n)"), ps[:, 6, 0:20 * FT])
            dve.drain()
            norm_dve(dve, v, S, xT, rstd, tmp, 0, v.lo)

        @block.scalar
        def _(act):
            act.wait_ge(x_copied, NBLK + 1)
            norm_act(act, v, S, xT, sq, rstd, tmp)


def norm_signals(v, name):
    return {k: v.sem(f"{name}_{k}") for k in ("squared", "summed", "rstd", "normed", "hi", "lo")}


def norm_act(act, v, S, xT, sq, rstd, tmp):
    for g in range(NG):
        if g:
            act.wait_ge(S["summed"], g)
        act.activation(sq[:], xT[:, :, g * GRP:(g + 1) * GRP], ACT.Square).then_inc(S["squared"], 1)
    act.wait_ge(S["summed"], NG)
    for g in range(NG):
        act.activation(rstd[:, g * GRP:(g + 1) * GRP], v.ps[:, g, 0:GRP], ACT.Ln, scale=1.0 / D, bias=EPS)
    act.drain()
    act.activation(rstd[:], rstd[:], ACT.Exp, scale=-0.5).then_inc(S["rstd"], 1)
    if tmp is not None:
        for k in range(KC):
            act.wait_ge(S["normed"], k + 1)
            act.activation(v.hi[:, k], tmp[:, k % 2], ACT.Copy).then_inc(S["hi"], 1)


def norm_pe(pe, v, S, sq):
    for g in range(NG):
        pe.wait_ge(S["squared"], g + 1)
        for k in range(KC):
            mm = pe.matmul(v.ps[:, g, 0:GRP], v.ones[:], sq[:, k], start=(k == 0), stop=(k == KC - 1))
        mm.then_inc(S["summed"], 1)


def norm_dve(dve, v, S, xT, rstd, tmp, which, lo):
    dve.wait_ge(S["rstd"], 1)
    for k in range(KC + 1):
        if k < KC:
            dve.scalar_tensor_tensor(out=tmp[:, k % 2], in0=xT[:, k], scalar=v.norms[:, k, which:which + 1],
                                     in1=rstd[:], op0=ALU.mult, op1=ALU.mult).then_inc(S["normed"], 1)
        if k >= 1:
            dve.wait_ge(S["hi"], k)
            dve.tensor_tensor(lo[:, k - 1], tmp[:, (k - 1) % 2], v.hi[:, k - 1].bitcast(F32),
                              ALU.subtract).then_inc(S["lo"], 1)
            dve.drain()


def gates(nc, t, v):
    with ExitStack() as scope:
        def sb(name, shape, dt=F32):
            return v.sb(name, shape, dt, scope)

        w_raw = sb("wg_raw", [P, KC, FH + 2 * GH])
        w_hi = sb("wg_hi", [P, KC, GROWS], F32R)
        w_lo = sb("wg_lo", [P, KC, GROWS], F32R)
        sign, bias, coef = sb("g_sign", [GROWS, 1]), sb("g_bias", [GROWS, 1]), sb("g_coef", [GROWS, 1])
        y, mag, gate = sb("g_y", [GROWS, TOK]), sb("g_mag", [GROWS, TOK]), sb("g_gate", [GROWS, TOK])
        run, keep = sb("g_run", [GROWS, SEQ]), sb("g_keep", [GROWS, SEQ])
        past = sb("past_logf", [P, DEC * PAGES, FH])
        dsel = sb("dec_sel", [GROWS, P])
        total = sb("dec_total", [P, DEC, FH])
        ps = v.ps
        w_loaded, b_loaded, past_loaded = v.sem("wg_loaded"), v.sem("gbias_loaded"), v.sem("past_loaded")
        prepared, bias_set = v.sem("g_prepared"), v.sem("g_bias_zeroed")
        split_hi, split_lo = v.sem("wg_split_hi"), v.sem("wg_split_lo")
        summed, y_ready, mag_ready = v.sem("g_summed"), v.sem("g_y_ready"), v.sem("g_mag_ready")
        coef_ready, gate_ready, beta_ready = v.sem("g_coef_ready"), v.sem("g_gate_ready"), v.sem("g_beta_ready")
        run_ready, turned, sel_ready = v.sem("g_run_ready"), v.sem("g_turned"), v.sem("g_sel_ready")
        dec_done, gates_out, stored, eg_done, dec_copied = v.sem("g_dec_done"), v.sem("g_gates_out"), v.sem("g_stored"), v.sem("g_eg_done"), v.sem("g_dec_copied")
        w_view = t["w_in"][0].rearrange("(k p) n -> p k n", p=P)
        NPG = DEC * PAGES

        block = scope.enter_context(nc.Block())

        @block.sync
        def _(sp):
            sp.dma_start(w_raw[:, :, 0:FH], w_view[:, :, C_FF:C_FF + FH]).then_inc(w_loaded, 16)
            sp.dma_start(w_raw[:, :, FH:], w_view[:, :, C_GA:C_GA + 2 * GH]).then_inc(w_loaded, 16)
            sp.wait_ge(bias_set, 1)
            sp.dma_start(bias[R_F:R_F + FH, :], t["b_forget"].rearrange("a h -> h a")).then_inc(b_loaded, 16)
            sp.dma_start(bias[R_A:R_A + GH, :], t["gdn_dt_bias"].rearrange("a h -> h a")).then_inc(b_loaded, 16)
            sp.dma_start(coef[R_A:R_A + GH, :], t["gdn_a_log"].rearrange("a h -> h a")).then_inc(b_loaded, 16)
            with sp.Fori(0, NPG) as n:
                page = sp.value_load(v.page_ids[0:1, ds(n, 1)], min_val=0, max_val=t["cache_logf"].shape[1] - 1)
                sp.dma_start(past[:, ds(n, 1), :].rearrange("p a h -> p (a h)"),
                             t["cache_logf"][0, ds(page, 1)].rearrange("a p h -> p (a h)")).then_inc(past_loaded, 16)
            sp.wait_ge(run_ready, 1)
            sp.dma_start(v.gate_dram, run[:]).then_inc(stored, 16)
            sp.wait_ge(gates_out, 1)
            sp.dma_start(t["new_logf_prompt"][0, 0].rearrange("(c p) h -> p c h", p=P),
                         v.logf_n[:, 0:NBLK]).then_inc(stored, 16)
            sp.dma_start(t["new_logf_sample"][0].rearrange("b a h -> b (a h)"),
                         v.logf_n[0:DEC, NBLK]).then_inc(stored, 16)
            sp.wait_ge(stored, 48)

        @block.gpsimd
        def _(pool):
            pool.memset(bias[:], 0.0)
            pool.memset(coef[:], 0.0)
            pool.drain()
            pool.drain().then_inc(bias_set, 1)
            pool.memset(sign[:], -1.0)
            pool.memset(keep[:], 1.0)
            pool.memset(dsel[:], 0.0)
            pool.drain()
            pool.memset(sign[R_A:R_A + 32, :], 1.0)
            pool.drain()
            pool.memset(keep[R_A:R_A + 32, :].rearrange("p (c i) -> p c i", c=NBLK)[:, :, 0:1], 0.0)
            pool.drain()
            pool.memset(w_hi[:].bitcast(F32), 0.0)
            pool.memset(w_lo[:].bitcast(F32), 0.0)
            pool.drain()
            pool.drain().then_inc(prepared, 1)

        cols = [(0, FH, R_F), (FH, GH, R_A), (FH + GH, GH, R_B)]

        @block.scalar
        def _(act):
            act.wait_ge(w_loaded, 32)
            act.wait_ge(prepared, 1)
            for a, n, r in cols:
                ins = act.activation(w_hi[:, :, r:r + n], w_raw[:, :, a:a + n], ACT.Copy)
            ins.then_inc(split_hi, 1)
            act.wait_ge(y_ready, 1)
            act.activation(mag[:], y[:], ACT.Abs)
            act.drain()
            act.activation(mag[:], mag[:], ACT.Exp, scale=-1.0)
            act.wait_ge(b_loaded, 48)
            act.activation(coef[R_A:R_A + 32, :], coef[R_A:R_A + 32, :], ACT.Exp).then_inc(coef_ready, 1)
            act.drain()
            act.activation(mag[:], mag[:], ACT.Ln, bias=1.0).then_inc(mag_ready, 1)
            act.wait_ge(gate_ready, 1)
            act.activation(gate[R_B:R_B + 32, :], gate[R_B:R_B + 32, :], ACT.Exp).then_inc(beta_ready, 1)
            act.wait_ge(dec_copied, 1)
            act.activation(v.dec_gates[:, 0], v.dec_gates[:, 0], ACT.Exp).then_inc(eg_done, 1)
            act.wait_ge(eg_done, 1)

        @block.tensor
        def _(pe):
            pe.wait_ge(split_lo, 1)
            for g in range(NG):
                for k in range(KC):
                    mm = split_piece(pe, ps[0:GROWS, 3 + g, 0:GRP], w_hi[:, k], w_lo[:, k],
                                     v.hi[:, k, g * GRP:(g + 1) * GRP], v.lo[:, k, g * GRP:(g + 1) * GRP],
                                     k, k == 0, k == KC - 1)
            mm.then_inc(summed, 1)
            pe.wait_ge(past_loaded, 16 * NPG)
            past_flat = past[:].rearrange("p n h -> p (n h)")
            pe.matmul(ps[:, 0, 0:512], v.later[:], past_flat, start=True, stop=True)
            pe.matmul(ps[:, 1, 0:512], v.ones[:], past_flat, start=True, stop=True)
            pe.wait_ge(sel_ready, 1)
            pe.matmul(ps[:, 2, 0:P], v.ones[0:GROWS, :], dsel[:], start=True, stop=True).then_inc(dec_done, 1)
            for c in range(NBLK):
                pe.transpose(ps[:, 6 + c // 4, (c % 4) * GROWS:(c % 4 + 1) * GROWS], gate[:, c * P:(c + 1) * P],
                             v.ident[0:GROWS, 0:GROWS])
            pe.transpose(ps[0:DEC, 3, 0:GROWS], gate[:, SEQ:TOK], v.ident[0:GROWS, 0:GROWS])
            for c in range(NBLK):
                mm = pe.transpose(ps[:, 4 + c // 4, (c % 4) * GROWS:(c % 4 + 1) * GROWS], run[:, c * P:(c + 1) * P],
                                  v.ident[0:GROWS, 0:GROWS])
            mm.then_inc(turned, 1)

        @block.vector
        def _(dve):
            dve.wait_ge(split_hi, 1)
            for a, n, r in cols:
                ins = dve.tensor_tensor(w_lo[:, :, r:r + n], w_raw[:, :, a:a + n], w_hi[:, :, r:r + n].bitcast(F32), ALU.subtract)
            ins.then_inc(split_lo, 1)
            dve.wait_ge(summed, 1)
            dve.wait_ge(b_loaded, 48)
            for g in range(NG):
                ins = dve.tensor_scalar(y[:, g * GRP:(g + 1) * GRP], ps[0:GROWS, 3 + g, 0:GRP], bias[:], sign[:], ALU.add, ALU.mult)
            ins.then_inc(y_ready, 1)
            dve.wait_ge(coef_ready, 1)
            dve.tensor_scalar(coef[R_A:R_A + 32, :], coef[R_A:R_A + 32, :], -1.0, None, ALU.mult)
            dve.memset(coef[R_F:R_F + 32, :], -1.0)
            dve.memset(coef[R_B:R_B + 32, :], -1.0)
            dve.wait_ge(mag_ready, 1)
            dve.scalar_tensor_tensor(out=gate[:], in0=y[:], scalar=0.0, in1=mag[:], op0=ALU.max, op1=ALU.add)
            dve.drain()
            dve.tensor_scalar(gate[:], gate[:], coef[:], None, ALU.mult).then_inc(gate_ready, 1)
            dve.drain()
            dve.tensor_tensor_scan(run[0:64, :], keep[0:64, :], gate[0:64, 0:SEQ], 0.0, ALU.mult, ALU.add)
            dve.wait_ge(beta_ready, 1)
            dve.tensor_copy(run[R_B:R_B + 32, :], gate[R_B:R_B + 32, 0:SEQ])
            dve.drain()
            dve.tensor_scalar(run[R_F:R_F + 32, :], run[R_F:R_F + 32, :], -1.0 / SCALE, None, ALU.mult).then_inc(run_ready, 1)
            for r, n in ((R_F, FH), (R_A, GH), (R_B, GH)):
                g_row = gate[r:r + n, SEQ:TOK]
                if r == R_F:
                    out = dsel[r:r + n, 0:64].rearrange("p (b h) -> p b h", b=DEC)
                    a = g_row.unsqueeze(2).broadcast_to([n, DEC, n])
                    b = v.ident[r:r + n, r:r + n].unsqueeze(1).broadcast_to([n, DEC, n])
                else:
                    at = 64 if r == R_A else 96
                    out = dsel[r:r + n, at:at + 32].rearrange("p (h b) -> p h b", h=GH)
                    a = g_row.unsqueeze(1).broadcast_to([n, GH, DEC])
                    b = v.ident[r:r + n, r:r + n].unsqueeze(2).broadcast_to([n, GH, DEC])
                ins = dve.tensor_tensor(out, a, b, ALU.mult)
            ins.then_inc(sel_ready, 1)
            dve.wait_ge(dec_done, 1)
            dve.tensor_copy(v.dec_gates[:].rearrange("p n h b -> p (n h b)"), ps[:, 2, 64:128]).then_inc(dec_copied, 1)
            dve.tensor_copy(total[:].rearrange("p b h -> p (b h)"), ps[:, 2, 0:64])
            within = ps[:, 0].rearrange("p (b g h) -> p b g h", b=DEC, g=PAGES)
            whole = ps[:, 1].rearrange("p (b g h) -> p b g h", b=DEC, g=PAGES)
            bias_v = v.dec_bias[:].rearrange("p (b g) h -> p b g h", b=DEC)
            for pg in reversed(range(PAGES)):
                dve.drain()
                dve.tensor_tensor(bias_v[:, :, pg, :], total[:], within[:, :, pg, :], ALU.add)
                if pg:
                    dve.drain()
                    dve.tensor_tensor(total[:], total[:], whole[:, :, pg, :], ALU.add)
            dve.wait_ge(turned, 1)
            for half in range(2):
                rows_n = ps[:, 6 + half, 0:4 * GROWS].rearrange("p (c r) -> p c r", c=4)
                dve.tensor_copy(v.logf_n[:, 4 * half:4 * half + 4, :], rows_n[:, :, R_F:R_F + FH])
                dve.tensor_copy(v.beta_n[:, 4 * half:4 * half + 4, :], rows_n[:, :, R_B:R_B + GH])
                dve.tensor_copy(v.gcum_n[:, 4 * half:4 * half + 4, :],
                                ps[:, 4 + half, 0:4 * GROWS].rearrange("p (c r) -> p c r", c=4)[:, :, R_A:R_A + GH])
            dve.tensor_copy(v.logf_n[0:DEC, NBLK, :], ps[0:DEC, 3, R_F:R_F + FH]).then_inc(gates_out, 1)


class Count:

    def __init__(self, sem, per, credit=0):
        self.sem, self.per, self.credit = sem, per, credit

    def at(self, j, n):
        return j * self.per + (n + self.credit)


def mixer(nc, t, v):
    with ExitStack() as scope:
        def sb(name, shape, dt=F32):
            return v.sb(name, shape, dt, scope)

        ps = v.ps
        w_raw = sb("wm_raw", [P, 2, KC, P])
        w_hi = sb("wm_hi", [P, 2, KC, P], F32R)
        w_lo = sb("wm_lo", [P, 2, KC, P], F32R)
        qT, kT, vT = sb("qT", [P, TOK]), sb("kT", [P, TOK]), sb("vT", [P, TOK])
        ext = sb("gdn_ext", [P, 3, EXT])
        z_silu = sb("z_silu", [P, TOK])
        mix = sb("mix", [P, TOK])
        small = sb("mix_small", [P, 640])
        region = sb("region", [P, 16544])
        at = [0]

        def view(width):
            at[0] += width
            assert at[0] <= 16544
            return region[:, at[0] - width:at[0]]

        def blocks(ap):
            return ap.rearrange("p (c i) -> p c i", i=P)

        k_nat, v_nat = blocks(view(SEQ)), blocks(view(SEQ))
        ck_row = view(2 * SEQ).rearrange("p (h s) -> p h s", h=2)
        ck_diag = view(2 * SEQ).rearrange("p (h s) -> p h s", h=2)
        prob = view(2 * SEQ).rearrange("p (u s) -> p u s", u=2)
        probT = view(2 * SEQ).rearrange("p (u c i) -> p u c i", u=2, i=P)
        o_nat = k_nat
        v_past = view(4 * SEQ).rearrange("p (b g d) -> p b g d", b=4, d=P)
        k_past = view(2 * SEQ).rearrange("p (b g d) -> p b g d", b=2, d=P)
        at[0] = 0
        conv = view(3 * CONV).rearrange("p (y e) -> p y e", y=3)
        rs_qk = view(2 * CONV).rearrange("p (y e) -> p y e", y=2)
        slots = [view(SEQ) for _ in range(11)]
        decayT, k_dec, k_beta, v_beta, aT, qkT, gc_row, beta_row, eg_row, k_scaled, s_dec = slots
        squares = region[:, 5 * CONV:7 * CONV].rearrange("p (y e) -> p y e", y=2)
        levelT = [blocks(decayT), blocks(gc_row)]
        inv, invT, z_mat = blocks(k_scaled), blocks(beta_row), blocks(eg_row)
        wT = blocks(conv[:, 1, 0:SEQ])
        oT = rs_qk[:, 1, 0:TOK]
        o_sq, o_rstd = region[:, 5 * CONV:5 * CONV + TOK], region[:, 5 * CONV + 2 * SEQ:5 * CONV + 2 * SEQ + TOK]
        state = sb("state", [P, GD])
        v_new = sb("v_new", [P, 2, GD])

        off = [0]

        def sm(n):
            off[0] += n
            assert off[0] <= 640
            return small[:, off[0] - n:off[0]]

        kv_dec = sb("kv_dec", [DEC, 2, P])
        neg_max, row_sum, row_inv, max_part = sm(16), sm(16), sm(16), sm(16)
        bias_j = sm(2 * DEC * PAGES).rearrange("p (b g h) -> p b g h", b=DEC, g=PAGES)
        score = sm(64).rearrange("p (b g h) -> p b g h", b=4, g=PAGES)
        d_max, d_all, d_self, d_pself, d_den = (sm(8).rearrange("p (b h) -> p b h", b=4) for _ in range(5))
        qk_self = sm(DEC)
        conv_j = sm(3 * 28).rearrange("p (y n) -> p y n", y=3)
        gs = sm(7 * NBLK).rearrange("p (n c) -> p n c", n=7)
        BETA, GCUM, GLAST, EG, KB, KD, EGL = range(7)
        dg = sm(2 * DEC).rearrange("p (n b) -> p n b", n=2)
        kq = sm(2 * DEC).rearrange("p (b n) -> p b n", n=2)
        kq_dot, kq_prod, delta, d_tmp = sm(DEC), sm(DEC), sm(DEC), sm(DEC)
        tail = sb("conv_tail", [P, 3, TAPS - 1 + DEC])
        tail_rows = sb("conv_tail_rows", [TAPS - 1 + DEC, 3, P])
        nat_dec = v_beta[0:DEC, 0:2 * P].rearrange("p (n d) -> p n d", n=2)
        delta_diag = blocks(k_beta[0:DEC, :])

        C = {}

        def count(name, per, credit=0):
            C[name] = Count(v.mixer_sem("m_" + name), per, credit)
            return C[name]

        step_done = {e: count("step_" + e, 1, 1) for e in ("pe", "act", "dve", "pool")}
        w_loaded = [count("w_loaded0", 64), count("w_loaded1", 48)]
        w_split_hi, w_split_lo = count("w_split_hi", NTILE), count("w_split_lo", NTILE, 2)
        piece_done, piece_out = count("piece_done", 3 * NTILE, 6), count("piece_out", 3 * NTILE, 2)
        nat_turned, nat_out, dg_ready = count("nat_turned", 1), count("nat_out", 1), count("dg_ready", 1)
        ck_loaded = count("ck_loaded", 16)
        qk_done, scored, expd = count("qk_done", 16), count("scored", 16), count("expd", 16)
        p_turned, p_out_a, p_out_b = count("p_turned", 16), count("p_out_a", 16), count("p_out_b", 8)
        pv_done, pv_out = count("pv_done", 16), count("pv_out", 16)
        o_turned, mix_ready = count("o_turned", 1), count("mix_ready", 1)
        nat_stored = count("nat_stored", 16 * 4)
        k_loaded = [count("kpast_loaded0", 128 * 4), count("kpast_loaded1", 128 * 4)]
        v_loaded = count("vpast_loaded", 512 * 2)
        k_used = count("kpast_used", 8)
        qb_done, self_ready, self_done = count("qb_done", 2), count("self_ready", 1), count("self_done", 2)
        dmax_ready, dmax_all, dsub_ready, dexp = count("dmax_ready", 2), count("dmax_all", 2), count("dsub_ready", 2), count("dexp", 2)
        dpv_done, dec_out = count("dpv_done", 2), count("dec_out", 2)
        mix_stored = count("mix_stored", 32)
        rows_loaded, s_loaded = count("rows_loaded", 32), count("s_loaded", 16)
        g_ready, conv_done, conv_silu = count("g_ready", 1), count("conv_done", 3), count("conv_silu", 3)
        tail_ready, tail_turned, tail_out = count("tail_ready", 1), count("tail_turned", 1), count("tail_out", 1)
        tail_stored = count("tail_stored", 32)
        sq_ready, l2_done, l2_rstd, l2_out = count("sq_ready", 1), count("l2_done", 1), count("l2_rstd", 1), count("l2_out", 1)
        dif_ready, dec_exp, dec_masked, eg_row_ready = count("dif_ready", 1), count("dec_exp", 1), count("dec_masked", 1), count("eg_row_ready", 1)
        gs_exp = count("gs_exp", 1)
        gnat_turned, gnat_out, kk_done, a_ready = count("gnat_turned", 1), count("gnat_out", 1), count("kk_done", 1), count("a_ready", 1)
        gqk_done, q_ready = count("gqk_done", 1), count("q_ready", 1)
        level_ready, y0_ready, y0_turned, x0_ready = count("level_ready", 7), count("y0_ready", 1), count("y0_turned", 1), count("x0_ready", 1)
        z_done, z_out, xy_done, xy_out = count("z_done", 12), count("z_out", 12), count("xy_done", 12), count("xy_out", 12)
        w_done, w_out_ = count("wT_done", 1), count("wT_out", 1)
        state_zero = count("state_zero", 1)
        vn_done, vn_out = count("vn_done", NBLK), count("vn_out", NBLK)
        oc_done, oc_out, sc_done, sc_out = count("oc_done", NBLK), count("oc_out", NBLK), count("sc_done", NBLK), count("sc_out", NBLK)
        kq_ready, sdec_done, delta_ready, rows_turned = count("kq_ready", 1), count("sdec_done", 1), count("delta_ready", 1), count("rows_turned", 1)
        diag_ready, outer_done, sdec_ready = count("diag_ready", 1), count("outer_done", 1), count("sdec_ready", 1)
        osq_ready, osum_done, orstd_ready, o_ready = count("osq_ready", 1), count("osum_done", 1), count("orstd_ready", 1), count("o_ready", 1)
        state_stored = count("state_stored", 32)
        ctx_copied = v.mixer_sem("ctx_copied")
        credits = {"pe": (step_done["pe"], piece_done), "act": (step_done["act"], piece_out),
                   "dve": (step_done["dve"],), "pool": (step_done["pool"], w_split_lo)}

        def give_credits(eng, name):
            for c in credits[name]:
                eng.sem_inc(c.sem, c.credit)

        def wait(eng, c, j, n=None):
            eng.wait_ge(c.sem, c.at(j, c.per if n is None else n))

        passed = {e: v.mixer_sem("m_passed_" + e) for e in ("dve", "pool", "sp")}

        def settle(eng, name):
            eng.sem_inc(passed[name], 1)

        def start_step(eng, j, me):
            for name, c in step_done.items():
                if name != me:
                    wait(eng, c, j, 0)

        w_view = t["w_in"][0].rearrange("(k p) n -> p k n", p=P)
        NP_ = t["cache_k"].shape[1]
        before = [0] + [i - 1 for i in range(1, NTILE)]
        piece_before = [0] + [q - 1 for q in range(1, 3 * NTILE)]

        block = scope.enter_context(nc.Block())

        @block.sync
        def _(sp):
            sp.dma_start(t["new_gdn_conv_sample"][0, :, 0:2, :], t["state_gdn_conv"][0, :, 1:3, :]).then_inc(ctx_copied, 16)
            with sp.Fori(0, STEPS) as j:
                def load_weights(i):
                    wait(sp, w_split_lo, j, before[i])
                    sp.dma_start(w_raw[:, i % 2], w_view[:, :, ds(j * P + TILE_COL[i], P)]).then_inc(w_loaded[i % 2].sem, 16)

                def load_past(dst, cache, page, s):
                    sp.dma_start(dst, cache[0, ds(page, 1)].rearrange("a p h d -> p (a h d)")[:, ds(j * P, P)]).then_inc(s.sem, 16)

                def pages(b):
                    settle(sp, "sp")
                    return [sp.value_load(v.page_ids[0:1, b * PAGES + g:b * PAGES + g + 1], min_val=0, max_val=NP_ - 1)
                            for g in range(PAGES)]

                def load_b(half, b, with_v):
                    for g, page in enumerate(pages(half * 4 + b)):
                        load_past(k_past[:, b % 2, g], t["cache_k"], page, k_loaded[b % 2])
                        load_past(v_past[:, b, g], t["cache_v"], page, v_loaded)

                load_weights(0)
                load_weights(1)
                start_step(sp, j, "sp")
                sp.dma_start(ck_row, v.gate_dram[ds(R_F + 2 * j, 2), :].unsqueeze(0).broadcast_to([P, 2, SEQ])).then_inc(ck_loaded.sem, 16)
                for i in range(2, NTILE):
                    load_weights(i)
                load_b(0, 0, True)
                load_b(0, 1, True)
                wait(sp, nat_out, j)
                kp, vp = (t[n][0, 0].rearrange("(c p) h d -> p c (h d)", p=P) for n in ("new_k_prompt", "new_v_prompt"))
                ks, vs = (t[n][0].rearrange("b a h d -> b (a h d)") for n in ("new_k_sample", "new_v_sample"))
                sp.dma_start(kp[:, :, ds(j * P, P)], k_nat).then_inc(nat_stored.sem, 16)
                sp.dma_start(vp[:, :, ds(j * P, P)], v_nat).then_inc(nat_stored.sem, 16)
                sp.dma_start(ks[:, ds(j * P, P)], kv_dec[:, 0]).then_inc(nat_stored.sem, 16)
                sp.dma_start(vs[:, ds(j * P, P)], kv_dec[:, 1]).then_inc(nat_stored.sem, 16)
                for half in range(2):
                    for b in range(4):
                        if half == 0 and b < 2:
                            continue
                        wait(sp, k_used, j, half * 4 + b - 1)
                        settle(sp, "sp")
                        if half and b == 0:
                            wait(sp, dec_out, j, 1)
                        load_b(half, b, True)
                wait(sp, mix_ready, j)
                settle(sp, "sp")
                wait(sp, dec_out, j)
                sp.dma_start(gc_row, v.gate_dram[ds(R_A + j, 1), :].broadcast_to([P, SEQ])).then_inc(rows_loaded.sem, 16)
                sp.dma_start(beta_row, v.gate_dram[ds(R_B + j, 1), :].broadcast_to([P, SEQ])).then_inc(rows_loaded.sem, 16)
                sp.dma_start(blocks(s_dec), t["state_gdn"][0, :, ds(j, 1)].rearrange("b a k e -> k (b a) e")).then_inc(s_loaded.sem, 16)
                sp.dma_start(v.mix_dram[ds(j, 1)].rearrange("a p n -> p (a n)"), mix[:]).then_inc(mix_stored.sem, 16)
                wait(sp, tail_out, j)
                tp = t["new_gdn_conv_prompt"][0, 0].rearrange("i (y n) -> i y n", y=3)
                ts = t["new_gdn_conv_sample"][0, :, TAPS - 2, :].rearrange("b (y n) -> b y n", y=3)
                sp.dma_start(tp[:, :, ds(j * P, P)], tail_rows[0:3]).then_inc(tail_stored.sem, 16)
                sp.dma_start(ts[:, :, ds(j * P, P)], tail_rows[3:3 + DEC]).then_inc(tail_stored.sem, 16)
                wait(sp, sc_out, j)
                sp.dma_start(t["new_gdn_prompt"][0, 0, ds(j, 1)].rearrange("a k e -> k (a e)"), state[:]).then_inc(state_stored.sem, 16)
                wait(sp, sdec_ready, j)
                sp.dma_start(t["new_gdn_sample"][0, :, ds(j, 1)].rearrange("b a k e -> k (b a) e"), blocks(s_dec)).then_inc(state_stored.sem, 16)
                wait(sp, o_ready, j)
                sp.dma_start(v.mix_dram[ds(GH + j, 1)].rearrange("a p n -> p (a n)"), oT).then_inc(mix_stored.sem, 16)
            sp.wait_ge(ctx_copied, 16)

        @block.tensor
        def _(pe):
            give_credits(pe, "pe")
            with pe.Fori(0, STEPS) as j:
                start_step(pe, j, "pe")

                def project(i):
                    wait(pe, w_split_lo, j, i + 1)
                    for g in range(NG):
                        q = 3 * i + g
                        wait(pe, piece_out, j, piece_before[q])
                        out = ps[:, q % 2, 0:GRP]
                        for k in range(KC):
                            mm = split_piece(pe, out, w_hi[:, i % 2, k], w_lo[:, i % 2, k],
                                             v.hi[:, k, g * GRP:(g + 1) * GRP], v.lo[:, k, g * GRP:(g + 1) * GRP],
                                             k, k == 0, k == KC - 1)
                        mm.then_inc(piece_done.sem, 1)

                for i in range(NTILE):
                    project(i)
                wait(pe, piece_out, j, 9)
                for src, bank in ((kT, 3), (vT, 5)):
                    for c in range(NBLK):
                        pe.transpose(ps[:, bank + c // 4, (c % 4) * P:(c % 4 + 1) * P], src[:, c * P:(c + 1) * P], v.ident[:])
                pe.transpose(ps[0:DEC, 7, 0:P], kT[:, SEQ:TOK], v.ident[:])
                pe.transpose(ps[0:DEC, 7, P:2 * P], vT[:, SEQ:TOK], v.ident[:]).then_inc(nat_turned.sem, 1)
                wait(pe, nat_out, j)

                def scores(u):
                    h, i = u // NBLK, u % NBLK
                    if u:
                        wait(pe, scored, j, u)
                    rows = slice(h * FD, (h + 1) * FD)
                    n = (i + 1) * P
                    for a in range(0, n, 512):
                        b = min(n, a + 512)
                        mm = pe.matmul(ps[:, 3 + a // 512, 0:b - a], qT[rows, i * P:(i + 1) * P], kT[rows, a:b], start=True, stop=True)
                    mm.then_inc(qk_done.sem, 1)

                def turn_probs(u):
                    i = u % NBLK
                    wait(pe, expd, j, u + 1)
                    if u:
                        wait(pe, p_out_a, j, u)
                        if (u - 1) % NBLK >= 4:
                            wait(pe, p_out_b, j, 4 * ((u - 1) // NBLK) + (u - 1) % NBLK - 3)
                    for c in range(i + 1):
                        mm = pe.transpose(ps[:, 5 + c // 4, (c % 4) * P:(c % 4 + 1) * P], prob[:, u % 2, c * P:(c + 1) * P], v.ident[:])
                    mm.then_inc(p_turned.sem, 1)

                def weigh_values(u):
                    h, i = u // NBLK, u % NBLK
                    wait(pe, p_out_a, j, u + 1)
                    if i >= 4:
                        wait(pe, p_out_b, j, 4 * h + i - 3)
                    if u >= 2:
                        wait(pe, pv_out, j, u - 1)
                    for c in range(i + 1):
                        mm = pe.matmul(ps[:, (7, 2)[u % 2], 0:FD], probT[:, u % 2, c], v_nat[:, c, h * FD:(h + 1) * FD],
                                       start=(c == 0), stop=(c == i))
                    mm.then_inc(pv_done.sem, 1)

                for u in range(-1, 2 * NBLK + 1):
                    if u + 1 < 2 * NBLK:
                        scores(u + 1)
                    if 0 <= u < 2 * NBLK:
                        turn_probs(u)
                    if u >= 1:
                        weigh_values(u - 1)
                wait(pe, pv_out, j)
                for c in range(NBLK):
                    mm = pe.transpose(ps[:, 3 + c // 4, (c % 4) * P:(c % 4 + 1) * P], o_nat[:, c], v.ident[:])
                mm.then_inc(o_turned.sem, 1)
                for half in range(2):
                    if half:
                        wait(pe, dec_out, j, 1)
                    else:
                        wait(pe, mix_ready, j)
                    for b in range(4):
                        col = SEQ + 4 * half + b
                        mm = pe.matmul(ps[:, 3, b * P:(b + 1) * P], qT[:, col:col + 1].broadcast_to([P, P]), v.ident[:], start=True, stop=True)
                    mm.then_inc(qb_done.sem, 1)
                    wait(pe, self_ready, j)
                    for h in range(2):
                        mm = pe.matmul(ps[:, 4, 4 * h:4 * h + 4], v.head_ones[:, h], qk_self[:, 4 * half:4 * half + 4], start=True, stop=True)
                    mm.then_inc(self_done.sem, 1)
                    wait(pe, dexp, j, half + 1)
                    wait(pe, v_loaded, j, 512 * (half + 1))
                    pe.matmul(ps[:, 5, 0:64], v.ones[:], score.rearrange("p b g h -> p (b g h)"), start=True, stop=True)
                    for b in range(4):
                        for g in range(PAGES):
                            mm = pe.matmul(ps[:, 6, 2 * b:2 * b + 2], v_past[:, b, g], score[:, b, g], start=(g == 0), stop=(g == PAGES - 1))
                    mm.then_inc(dpv_done.sem, 1)
                wait(pe, dec_out, j)
                wait(pe, tail_ready, j)
                for y in range(3):
                    mm = pe.transpose(ps[0:TAPS - 1 + DEC, 7, y * P:(y + 1) * P], tail[:, y], v.ident[:])
                mm.then_inc(tail_turned.sem, 1)
                wait(pe, tail_out, j)
                wait(pe, sq_ready, j)
                for y in range(2):
                    for g, (a, w) in enumerate(groups(CONV, 3)):
                        mm = pe.matmul(ps[:, 2 + 3 * y + g, 0:w], v.ones[:], squares[:, y, a:a + w], start=True, stop=True)
                mm.then_inc(l2_done.sem, 1)
                wait(pe, l2_out, j)
                for y, bank in ((1, 2), (2, 4)):
                    for c in range(NBLK):
                        mm = pe.transpose(ps[:, bank + c // 4, (c % 4) * P:(c % 4 + 1) * P], conv[:, y, c * P:(c + 1) * P], v.ident[:])
                mm.then_inc(gnat_turned.sem, 1)
                qn, kn = blocks(conv[:, 0, 0:SEQ]), blocks(conv[:, 1, 0:SEQ])

                def per_chunk(bank, lhs, rhs):
                    for c in range(NBLK):
                        mm = pe.matmul(ps[:, bank + c // 4, (c % 4) * P:(c % 4 + 1) * P], lhs[:, c], rhs[:, c], start=True, stop=True)
                    return mm

                per_chunk(6, kn, blocks(k_scaled)).then_inc(kk_done.sem, 1)
                wait(pe, gnat_out, j)
                per_chunk(2, kn, qn).then_inc(gqk_done.sem, 1)
                wait(pe, y0_ready, j)
                for c in range(NBLK):
                    mm = pe.transpose(ps[:, 4 + c // 4, (c % 4) * P:(c % 4 + 1) * P], invT[:, c], v.ident[:])
                mm.then_inc(y0_turned.sem, 1)
                wait(pe, x0_ready, j)
                wait(pe, q_ready, j)
                for l in range(1, 7):
                    for hf in range(2):
                        n = 2 * (l - 1) + hf
                        wait(pe, level_ready, j, l + 1)
                        if l > 1:
                            wait(pe, xy_out, j, n - 1)
                        for c in range(4 * hf, 4 * hf + 4):
                            mm = pe.matmul(ps[:, 2 + hf, (c % 4) * P:(c % 4 + 1) * P], levelT[l % 2][:, c], inv[:, c], start=True, stop=True)
                        mm.then_inc(z_done.sem, 1)
                    for hf in range(2):
                        n = 2 * (l - 1) + hf
                        wait(pe, z_out, j, n + 1)
                        if l < 6:
                            for c in range(4 * hf, 4 * hf + 4):
                                pe.matmul(ps[:, 4 + hf, (c % 4) * P:(c % 4 + 1) * P], invT[:, c], z_mat[:, c], start=True, stop=True)
                        for c in range(4 * hf, 4 * hf + 4):
                            mm = pe.matmul(ps[:, 6 + hf, (c % 4) * P:(c % 4 + 1) * P], z_mat[:, c], invT[:, c], start=True, stop=True)
                        mm.then_inc(xy_done.sem, 1)
                wait(pe, xy_out, j)
                per_chunk(2, blocks(k_beta), invT).then_inc(w_done.sem, 1)
                wait(pe, w_out_, j)
                wait(pe, state_zero, j)
                qd = qn
                for c in range(NBLK):
                    if c:
                        wait(pe, vn_out, j, c)
                    pe.matmul(ps[:, 4, 0:GD], invT[:, c], blocks(v_beta)[:, c], start=True, stop=False)
                    if c:
                        wait(pe, sc_out, j, c)
                    pe.matmul(ps[:, 4, 0:GD], wT[:, c], state[:], start=False, stop=True).then_inc(vn_done.sem, 1)
                    if c >= 2:
                        wait(pe, oc_out, j, c - 1)
                    pe.matmul(ps[:, 6 + c % 2, 0:P], state[:], qd[:, c], start=True, stop=False)
                    wait(pe, vn_out, j, c + 1)
                    pe.matmul(ps[:, 2 + c % 2, 0:GD], blocks(k_dec)[:, c], v_new[:, c % 2], start=True, stop=True).then_inc(sc_done.sem, 1)
                    pe.matmul(ps[:, 6 + c % 2, 0:P], v_new[:, c % 2], blocks(qkT)[:, c], start=False, stop=True).then_inc(oc_done.sem, 1)
                wait(pe, kq_ready, j)
                wait(pe, vn_out, j)
                wait(pe, sc_out, j)
                for b in range(DEC):
                    pe.matmul(ps[:, 4, 2 * b:2 * b + 2], blocks(s_dec)[:, b], kq[:, b], start=True, stop=True)
                pe.matmul(ps[:, 5, 0:DEC], v.ones[:], kq_prod, start=True, stop=True).then_inc(sdec_done.sem, 1)
                wait(pe, delta_ready, j)
                pe.transpose(ps[0:DEC, 4, 0:P], kq[:, :, 0], v.ident[:])
                pe.transpose(ps[0:DEC, 4, P:2 * P], delta, v.ident[:]).then_inc(rows_turned.sem, 1)
                wait(pe, diag_ready, j)
                for hf in range(2):
                    mm = pe.matmul(ps[:, 2 + hf, 0:512], nat_dec[:, 0], delta_diag[:, 4 * hf:4 * hf + 4].rearrange("q b e -> q (b e)"), start=True, stop=True)
                mm.then_inc(outer_done.sem, 1)
                wait(pe, osq_ready, j)
                for g in range(NG):
                    mm = pe.matmul(ps[:, 5 + g, 0:GRP], v.ones[:], o_sq[:, g * GRP:(g + 1) * GRP], start=True, stop=True)
                mm.then_inc(osum_done.sem, 1)
                pe.drain().then_inc(step_done["pe"].sem, 1)

        @block.scalar
        def _(act):
            give_credits(act, "act")
            with act.Fori(0, STEPS) as j:
                def split(i):
                    wait(act, w_loaded[i % 2], j, 16 * (i // 2 + 1))
                    wait(act, piece_done, j, 3 * before[i])
                    act.activation(w_hi[:, i % 2], w_raw[:, i % 2], ACT.Copy).then_inc(w_split_hi.sem, 1)

                def evacuate(i):
                    for g in range(NG):
                        q = 3 * i + g
                        wait(act, piece_done, j, q + 1)
                        src, a = ps[:, q % 2, 0:GRP], g * GRP
                        if i < 3:
                            act.activation((qT, kT, vT)[i][:, a:a + GRP], src, ACT.Copy).then_inc(piece_out.sem, 1)
                        elif i < 6:
                            n = min(GRP, SEQ - a)
                            ins = act.activation(ext[:, i - 3, TAPS - 1 + a:TAPS - 1 + a + n], src[:, 0:n], ACT.Copy)
                            if n < GRP:
                                new = ext[:, i - 3, TAPS - 1 + SEQ:].rearrange("p (b i) -> p b i", b=DEC)[:, :, TAPS - 1]
                                ins = act.activation(new, src[:, n:GRP], ACT.Copy)
                            ins.then_inc(piece_out.sem, 1)
                        else:
                            act.activation(z_silu[:, a:a + GRP], src, ACT.Silu).then_inc(piece_out.sem, 1)

                split(0)
                split(1)
                start_step(act, j, "act")
                for i in range(NTILE):
                    evacuate(i)
                    if i + 2 < NTILE:
                        split(i + 2)

                def exp_scores(u):
                    wait(act, scored, j, u + 1)
                    p = prob[:, u % 2, 0:(u % NBLK + 1) * P]
                    act.activation(p, p, ACT.Exp, bias=neg_max[:, u:u + 1], scale=-1.0,
                                   accum_out=row_sum[:, u:u + 1]).then_inc(expd.sem, 1)

                def probs_out(u):
                    n = min(4, u % NBLK + 1)
                    wait(act, p_turned, j, u + 1)
                    if u >= 2:
                        wait(act, pv_done, j, u - 1)
                    act.activation(probT[:, u % 2, 0:n], ps[:, 5, 0:n * P].rearrange("p (c i) -> p c i", c=n), ACT.Copy).then_inc(p_out_a.sem, 1)

                for u in range(-1, 2 * NBLK):
                    if u + 1 < 2 * NBLK:
                        exp_scores(u + 1)
                    if u >= 0:
                        probs_out(u)
                for half in range(2):
                    wait(act, dsub_ready, j, half + 1)
                    act.activation(score, score, ACT.Exp)
                    act.activation(d_pself, d_self, ACT.Exp).then_inc(dexp.sem, 1)
                wait(act, rows_loaded, j)
                for y in range(3):
                    wait(act, conv_done, j, y + 1)
                    act.activation(conv[:, y], conv[:, y], ACT.Silu).then_inc(conv_silu.sem, 1)
                    act.drain()
                act.activation(squares[:, 0], conv[:, 0], ACT.Square)
                act.activation(squares[:, 1], conv[:, 1], ACT.Square).then_inc(sq_ready.sem, 1)
                wait(act, l2_done, j)
                for y in range(2):
                    for g, (a, w) in enumerate(groups(CONV, 3)):
                        act.activation(rs_qk[:, y, a:a + w], ps[:, 2 + 3 * y + g, 0:w], ACT.Ln, bias=EPS)
                act.drain()
                act.activation(rs_qk[:, 0], rs_qk[:, 0], ACT.Exp, scale=-0.5, bias=LN_GSCALE)
                act.activation(rs_qk[:, 1], rs_qk[:, 1], ACT.Exp, scale=-0.5).then_inc(l2_rstd.sem, 1)
                act.activation(eg_row, gc_row, ACT.Exp).then_inc(eg_row_ready.sem, 1)
                wait(act, g_ready, j)
                act.activation(gs[:, EG], gs[:, GCUM], ACT.Exp)
                act.activation(gs[:, KD], gs[:, KD], ACT.Exp)
                act.activation(gs[:, EGL], gs[:, GLAST], ACT.Exp).then_inc(gs_exp.sem, 1)
                wait(act, dif_ready, j)
                act.activation(decayT, decayT, ACT.Exp).then_inc(dec_exp.sem, 1)
                for n in range(12):
                    hf = n % 2
                    wait(act, z_done, j, n + 1)
                    if n >= 2:
                        wait(act, xy_done, j, n - 1)
                    act.activation(z_mat[:, 4 * hf:4 * hf + 4], ps[:, 2 + hf].rearrange("p (c i) -> p c i", c=4), ACT.Copy).then_inc(z_out.sem, 1)
                for c in range(NBLK):
                    wait(act, vn_done, j, c + 1)
                    if c >= 2:
                        wait(act, oc_done, j, c - 1)
                    act.activation(v_new[:, c % 2], ps[:, 4, 0:GD], ACT.Copy).then_inc(vn_out.sem, 1)
                    wait(act, oc_done, j, c + 1)
                    act.activation(oT[:, c * P:(c + 1) * P], ps[:, 6 + c % 2, 0:P], ACT.Copy).then_inc(oc_out.sem, 1)
                act.drain()
                wait(act, delta_ready, j)
                act.activation(o_sq, oT, ACT.Square).then_inc(osq_ready.sem, 1)
                wait(act, osum_done, j)
                for g in range(NG):
                    act.activation(o_rstd[:, g * GRP:(g + 1) * GRP], ps[:, 5 + g, 0:GRP], ACT.Ln, scale=1.0 / GD, bias=EPS)
                act.drain()
                act.activation(o_rstd, o_rstd, ACT.Exp, scale=-0.5).then_inc(orstd_ready.sem, 1)
                act.drain().then_inc(step_done["act"].sem, 1)

        @block.gpsimd
        def _(pool):
            give_credits(pool, "pool")
            pool.memset(ext[:, :, 0:TAPS - 1], 0.0)
            pool.drain()
            with pool.Fori(0, STEPS) as j:
                for i in range(NTILE):
                    wait(pool, w_split_hi, j, i + 1)
                    pool.tensor_tensor(w_lo[:, i % 2], w_raw[:, i % 2], w_hi[:, i % 2].bitcast(F32), ALU.subtract).then_inc(w_split_lo.sem, 1)
                for half in range(2):
                    wait(pool, dmax_ready, j, half + 1)
                    settle(pool, "pool")
                    pool.partition_all_reduce(d_all.rearrange("p b h -> p (b h)"), d_max.rearrange("p b h -> p (b h)"), P, RMAX).then_inc(dmax_all.sem, 1)
                wait(pool, dec_exp, j)
                settle(pool, "pool")
                pool.affine_select(out=blocks(decayT), in_=blocks(decayT), compare_op=ALU.is_ge, fill=0.0, base=0,
                                   pattern=[[0, NBLK], [1, P]], channel_multiplier=-1).then_inc(dec_masked.sem, 1)
                for l in range(7):
                    if l == 0:
                        wait(pool, a_ready, j)
                        wait(pool, q_ready, j)
                    if l == 2:
                        wait(pool, y0_ready, j)
                    if l >= 3:
                        wait(pool, z_done, j, 2 * (l - 2))
                    pool.tensor_tensor(levelT[l % 2], blocks(aT), v.level_mask[:, l].unsqueeze(1).broadcast_to([P, NBLK, P]),
                                       ALU.mult).then_inc(level_ready.sem, 1)
                pool.drain().then_inc(step_done["pool"].sem, 1)

        @block.vector
        def _(dve):
            give_credits(dve, "dve")
            with dve.Fori(0, STEPS) as j:
                start_step(dve, j, "dve")
                dve.tensor_copy(bias_j, v.dec_bias[:].rearrange("p (b g) h -> p b g h", b=DEC)[:, :, :, ds(2 * j, 2)])
                dve.tensor_copy(conv_j.unsqueeze(2), v.gconv[:].rearrange("p (y h) n -> p y h n", y=3)[:, :, ds(j, 1), :])
                dve.tensor_copy(dg.unsqueeze(2), v.dec_gates[:, :, ds(j, 1), :])
                dve.tensor_copy(gs[:, BETA].unsqueeze(2), v.beta_n[:, :, ds(j, 1)])
                dve.tensor_copy(gs[:, GCUM].unsqueeze(2), v.gcum_n[:, :, ds(j, 1)])
                wait(dve, ck_loaded, j)
                if True:
                    dve.tensor_tensor(ck_diag.rearrange("p h (c s) -> p (h c) s", c=NBLK),
                                      ck_row.rearrange("p h (c s) -> p (h c) s", c=NBLK),
                                      v.causal[:].unsqueeze(1).broadcast_to([P, 2 * NBLK, P]), ALU.add)
                wait(dve, nat_turned, j)
                for dst, bank in ((k_nat, 3), (v_nat, 5)):
                    for hf in range(2):
                        dve.tensor_copy(dst[:, 4 * hf:4 * hf + 4], ps[:, bank + hf].rearrange("p (c i) -> p c i", c=4))
                dve.tensor_copy(kv_dec[:].rearrange("p n d -> p (n d)"), ps[0:DEC, 7, 0:2 * P]).then_inc(nat_out.sem, 1)

                def score_unit(u):
                    h, i = u // NBLK, u % NBLK
                    wait(dve, qk_done, j, u + 1)
                    if u >= 2:
                        wait(dve, p_turned, j, u - 1)
                    settle(dve, "dve")
                    first = -NEG_BIG
                    if i:
                        dve.tensor_tensor_reduce(out=prob[:, u % 2, 0:i * P], in0=ps[:, 3:5].rearrange("p a n -> p (a n)")[:, 0:i * P],
                                                 in1=ck_row[:, h, 0:i * P], scale=-SCALE, scalar=-NEG_BIG, op0=ALU.add,
                                                 op1=ALU.min, accum_out=max_part[:, u:u + 1])
                        dve.drain()
                        first = max_part[:, u:u + 1]
                    dve.tensor_tensor_reduce(out=prob[:, u % 2, i * P:(i + 1) * P], in0=ps[:, 3 + i // 4, (i % 4) * P:(i % 4 + 1) * P],
                                             in1=ck_diag[:, h, i * P:(i + 1) * P], scale=-SCALE, scalar=first, op0=ALU.add,
                                             op1=ALU.min, accum_out=neg_max[:, u:u + 1]).then_inc(scored.sem, 1)

                def probs_out(u):
                    i = u % NBLK
                    if i < 4:
                        return
                    wait(dve, p_turned, j, u + 1)
                    if u >= 2:
                        wait(dve, pv_done, j, u - 1)
                    n = i - 3
                    dve.tensor_copy(probT[:, u % 2, 4:4 + n], ps[:, 6, 0:n * P].rearrange("p (c i) -> p c i", c=n)).then_inc(p_out_b.sem, 1)

                def unit_out(u):
                    h, i = u // NBLK, u % NBLK
                    wait(dve, expd, j, u + 1)
                    if u == 0:
                        wait(dve, nat_stored, j)
                    dve.reciprocal(row_inv[:, u:u + 1], row_sum[:, u:u + 1])
                    dve.drain()
                    wait(dve, pv_done, j, u + 1)
                    dve.tensor_scalar(o_nat[:, i, h * FD:(h + 1) * FD], ps[:, (7, 2)[u % 2], 0:FD], row_inv[:, u:u + 1], None,
                                      ALU.mult).then_inc(pv_out.sem, 1)

                for u in range(-1, 2 * NBLK + 1):
                    if u + 1 < 2 * NBLK:
                        score_unit(u + 1)
                    if 0 <= u < 2 * NBLK:
                        probs_out(u)
                    if u >= 1:
                        unit_out(u - 1)
                wait(dve, o_turned, j)
                dve.tensor_tensor(qk_self, qT[:, SEQ:TOK], kT[:, SEQ:TOK], ALU.mult).then_inc(self_ready.sem, 1)
                for hf in range(2):
                    ins = dve.tensor_copy(mix[:, 512 * hf:512 * (hf + 1)], ps[:, 3 + hf])
                ins.then_inc(mix_ready.sem, 1)
                for half in range(2):
                    wait(dve, qb_done, j, half + 1)
                    for b in range(4):
                        wait(dve, k_loaded[b % 2], j, 128 * (2 * half + b // 2 + 1))
                        prod = prob[:, b % 2].rearrange("p (g d) -> p g d", g=PAGES)
                        dve.tensor_tensor(prod, k_past[:, b % 2], ps[:, 3, b * P:(b + 1) * P].unsqueeze(1).broadcast_to([P, PAGES, P]), ALU.mult)
                        dve.drain()
                        dve.tensor_reduce(score[:, b].rearrange("p g h -> p (g h)"), prob[:, b % 2].rearrange("p (n d) -> p n d", d=FD), AX.X, ALU.add).then_inc(k_used.sem, 1)
                    dve.drain()
                    dve.scalar_tensor_tensor(out=score.rearrange("p b g h -> p (b g) h"), in0=score.rearrange("p b g h -> p (b g) h"), scalar=SCALE,
                                             in1=bias_j[:, 4 * half:4 * half + 4].rearrange("p b g h -> p (b g) h"), op0=ALU.mult, op1=ALU.add)
                    wait(dve, self_done, j, half + 1)
                    dve.tensor_scalar(d_self, ps[:, 4, 0:8].rearrange("p (h b) -> p b h", h=2), SCALE, None, ALU.mult)
                    dve.drain()
                    dve.tensor_reduce(d_max, score.rearrange("p b g h -> p b h g"), AX.X, ALU.max).then_inc(dmax_ready.sem, 1)
                    wait(dve, dmax_all, j, half + 1)
                    dve.tensor_tensor(d_max, d_all, d_self, ALU.max)
                    dve.drain()
                    dve.tensor_tensor(score, score, d_max.unsqueeze(2).broadcast_to([P, 4, PAGES, 2]), ALU.subtract)
                    dve.tensor_tensor(d_self, d_self, d_max, ALU.subtract).then_inc(dsub_ready.sem, 1)
                    wait(dve, dpv_done, j, half + 1)
                    dve.tensor_reduce(d_den, ps[:, 5, 0:64].rearrange("p (b g h) -> p b h g", b=4, g=PAGES), AX.X, ALU.add)
                    dve.drain()
                    dve.tensor_tensor(d_den, d_den, d_pself, ALU.add)
                    dve.drain()
                    dve.reciprocal(d_den, d_den)
                    for h in range(2):
                        r = slice(h * FD, (h + 1) * FD)
                        cols = slice(SEQ + 4 * half, SEQ + 4 * half + 4)
                        dve.drain()
                        dve.tensor_tensor(d_tmp[r, 0:4], vT[r, cols], d_pself[r, :, h], ALU.mult)
                        dve.drain()
                        dve.tensor_tensor(d_tmp[r, 0:4], d_tmp[r, 0:4], ps[r, 6, 0:8].rearrange("p (b h) -> p b h", h=2)[:, :, h], ALU.add)
                        dve.drain()
                        ins = dve.tensor_tensor(mix[r, cols], d_tmp[r, 0:4], d_den[r, :, h], ALU.mult)
                    ins.then_inc(dec_out.sem, 1)
                wait(dve, piece_out, j, 18)
                dve.tensor_copy(ext[:, :, TAPS - 1 + SEQ:].rearrange("p y (b i) -> p y b i", b=DEC)[:, 0, :, 0:3],
                                conv_j[:, 0, 4:28].rearrange("p (b i) -> p b i", b=DEC))
                for y in range(1, 3):
                    dve.tensor_copy(ext[:, y, TAPS - 1 + SEQ:].rearrange("p (b i) -> p b i", b=DEC)[:, :, 0:3],
                                    conv_j[:, y, 4:28].rearrange("p (b i) -> p b i", b=DEC))
                dve.tensor_copy(tail[:, :, 0:3], ext[:, :, SEQ:SEQ + 3])
                for y in range(3):
                    ins = dve.tensor_copy(tail[:, y, 3:3 + DEC], ext[:, y, TAPS - 1 + SEQ:].rearrange("p (b i) -> p b i", b=DEC)[:, :, TAPS - 1])
                ins.then_inc(tail_ready.sem, 1)
                dve.drain()
                for y in range(3):
                    dve.tensor_scalar(conv[:, y], ext[:, y, 0:CONV], conv_j[:, y, 0:1], None, ALU.mult)
                    for i in range(1, TAPS):
                        dve.drain()
                        ins = dve.scalar_tensor_tensor(out=conv[:, y], in0=ext[:, y, i:i + CONV], scalar=conv_j[:, y, i:i + 1], in1=conv[:, y],
                                                       op0=ALU.mult, op1=ALU.add)
                    ins.then_inc(conv_done.sem, 1)
                wait(dve, tail_turned, j)
                dve.tensor_copy(tail_rows[:].rearrange("p y n -> p (y n)"), ps[0:TAPS - 1 + DEC, 7, 0:3 * P]).then_inc(tail_out.sem, 1)
                wait(dve, rows_loaded, j)
                dve.tensor_copy(gs[:, GLAST], blocks(gc_row)[:, :, P - 1])
                dve.drain()
                dve.tensor_tensor(gs[:, KD], gs[:, GLAST], gs[:, GCUM], ALU.subtract).then_inc(g_ready.sem, 1)
                wait(dve, l2_rstd, j)
                dve.tensor_tensor(conv[:, 0:2], conv[:, 0:2], rs_qk, ALU.mult)
                dve.tensor_tensor(blocks(decayT), blocks(gc_row), gs[:, GCUM].unsqueeze(2).broadcast_to([P, NBLK, P]), ALU.subtract)
                dve.drain()
                dve.tensor_scalar(decayT, decayT, 0.0, None, ALU.min).then_inc(dif_ready.sem, 1)
                dve.tensor_tensor(k_scaled, conv[:, 1, 0:SEQ], beta_row, ALU.mult).then_inc(l2_out.sem, 1)
                wait(dve, gs_exp, j)
                dve.scalar_tensor_tensor(out=gs[:, KB], in0=gs[:, BETA], scalar=-1.0, in1=gs[:, EG], op0=ALU.mult, op1=ALU.mult)
                dve.drain()
                wait(dve, gnat_turned, j)
                for hf in range(2):
                    cs = slice(4 * hf, 4 * hf + 4)
                    kps, vps = (ps[:, bank + hf].rearrange("p (c i) -> p c i", c=4) for bank in (2, 4))
                    for out, src, which in ((k_dec, kps, KD), (k_beta, kps, KB), (v_beta, vps, BETA)):
                        ins = dve.tensor_tensor(blocks(out)[:, cs], src, gs[:, which, cs].unsqueeze(2).broadcast_to([P, 4, P]), ALU.mult)
                ins.then_inc(gnat_out.sem, 1)
                wait(dve, kk_done, j)
                wait(dve, dec_masked, j)
                for hf in range(2):
                    ins = dve.tensor_tensor(aT[:, 512 * hf:512 * (hf + 1)], ps[:, 6 + hf], decayT[:, 512 * hf:512 * (hf + 1)], ALU.mult)
                ins.then_inc(a_ready.sem, 1)
                wait(dve, gqk_done, j)
                for hf in range(2):
                    dve.tensor_tensor(qkT[:, 512 * hf:512 * (hf + 1)], ps[:, 2 + hf], decayT[:, 512 * hf:512 * (hf + 1)], ALU.mult)
                wait(dve, eg_row_ready, j)
                dve.tensor_tensor(conv[:, 0, 0:SEQ], conv[:, 0, 0:SEQ], eg_row, ALU.mult).then_inc(q_ready.sem, 1)
                wait(dve, level_ready, j, 1)
                dve.tensor_tensor(invT, v.ident[:].unsqueeze(1).broadcast_to([P, NBLK, P]), levelT[0], ALU.subtract).then_inc(y0_ready.sem, 1)
                wait(dve, y0_turned, j)
                for hf in range(2):
                    ins = dve.tensor_copy(inv[:, 4 * hf:4 * hf + 4], ps[:, 4 + hf].rearrange("p (c i) -> p c i", c=4))
                ins.then_inc(x0_ready.sem, 1)
                for n in range(12):
                    hf = n % 2
                    cs = slice(4 * hf, 4 * hf + 4)
                    wait(dve, xy_done, j, n + 1)
                    if n < 10:
                        dve.tensor_tensor(inv[:, cs], inv[:, cs], ps[:, 4 + hf].rearrange("p (c i) -> p c i", c=4), ALU.subtract)
                    dve.tensor_tensor(invT[:, cs], invT[:, cs], ps[:, 6 + hf].rearrange("p (c i) -> p c i", c=4), ALU.subtract).then_inc(xy_out.sem, 1)
                wait(dve, w_done, j)
                for hf in range(2):
                    ins = dve.tensor_copy(wT[:, 4 * hf:4 * hf + 4], ps[:, 2 + hf].rearrange("p (c i) -> p c i", c=4))
                ins.then_inc(w_out_.sem, 1)
                dve.memset(state[:], 0.0).then_inc(state_zero.sem, 1)
                for c in range(NBLK):
                    dve.drain()
                    wait(dve, sc_done, j, c + 1)
                    dve.scalar_tensor_tensor(out=state[:], in0=state[:], scalar=gs[:, EGL, c:c + 1], in1=ps[:, 2 + c % 2, 0:GD],
                                             op0=ALU.mult, op1=ALU.add).then_inc(sc_out.sem, 1)
                dec = conv[:, :, SEQ:CONV].rearrange("p y (b i) -> p y b i", i=TAPS)[:, :, :, TAPS - 1]
                dve.tensor_copy(kq[:, :, 0], dec[:, 1])
                dve.tensor_copy(kq[:, :, 1], dec[:, 0])
                dve.tensor_tensor(kq_prod, dec[:, 0], dec[:, 1], ALU.mult)
                wait(dve, s_loaded, j)
                dve.tensor_tensor(blocks(s_dec), blocks(s_dec), dg[:, 0].unsqueeze(2).broadcast_to([P, DEC, GD]), ALU.mult).then_inc(kq_ready.sem, 1)
                wait(dve, sdec_done, j)
                dve.tensor_copy(kq_dot, ps[:, 5, 0:DEC])
                sk = ps[:, 4, 0:2 * DEC].rearrange("p (b n) -> p b n", n=2)
                dve.tensor_tensor(delta, dec[:, 2], sk[:, :, 0], ALU.subtract)
                dve.drain()
                dve.tensor_tensor(delta, delta, dg[:, 1], ALU.mult)
                dve.drain()
                dve.tensor_tensor(d_tmp, delta, kq_dot, ALU.mult)
                dve.drain()
                dve.tensor_tensor(oT[:, SEQ:TOK], d_tmp, sk[:, :, 1], ALU.add).then_inc(delta_ready.sem, 1)
                wait(dve, rows_turned, j)
                dve.tensor_copy(nat_dec.rearrange("p n d -> p (n d)"), ps[0:DEC, 4, 0:2 * P])
                dve.drain()
                dve.tensor_tensor(delta_diag, nat_dec[:, 1].unsqueeze(1).broadcast_to([DEC, DEC, P]),
                                  v.ident[0:DEC, 0:DEC].unsqueeze(2).broadcast_to([DEC, DEC, P]), ALU.mult).then_inc(diag_ready.sem, 1)
                wait(dve, outer_done, j)
                for hf in range(2):
                    ins = dve.tensor_tensor(s_dec[:, 512 * hf:512 * (hf + 1)], s_dec[:, 512 * hf:512 * (hf + 1)], ps[:, 2 + hf], ALU.add)
                ins.then_inc(sdec_ready.sem, 1)
                wait(dve, orstd_ready, j)
                dve.scalar_tensor_tensor(out=oT, in0=oT, scalar=v.out_norm[:], in1=o_rstd, op0=ALU.mult, op1=ALU.mult)
                dve.drain()
                dve.tensor_tensor(oT, oT, z_silu[:], ALU.mult).then_inc(o_ready.sem, 1)
                dve.drain()
                for c in (nat_stored, mix_stored, tail_stored, state_stored):
                    wait(dve, c, j, {nat_stored: 64}.get(c, c.per))
                dve.sem_inc(step_done["dve"].sem, 1)


def out_projection(nc, t, v):
    with ExitStack() as scope:
        def sb(name, shape, dt=F32):
            return v.sb(name, shape, dt, scope)

        ps = v.ps
        xT = sb("xT1", [P, KC, TOK])
        mix = sb("mix_in", [P, 2, TOK])
        w_raw = sb("wo_raw", [P, 2, KC, P])
        w_hi = sb("wo_hi", [P, 2, KC, P], F32R)
        w_lo = sb("wo_lo", [P, 2, KC, P], F32R)
        sq = sb("sq1", [P, KC, GRP])
        rstd = sb("rstd1", [P, TOK])
        mix_loaded = [v.sem("mix_loaded0"), v.sem("mix_loaded1")]
        w_loaded = [v.sem("wo_loaded0"), v.sem("wo_loaded1")]
        x_loaded, mix_hi, mix_lo = v.sem("x1_loaded"), v.sem("mix_hi"), v.sem("mix_lo")
        w_split_hi, w_split_lo = v.sem("wo_split_hi"), v.sem("wo_split_lo")
        piece_done, piece_out, x_saved = v.sem("wo_piece_done"), v.sem("wo_piece_out"), v.sem("x1_saved")
        S = norm_signals(v, "n1")
        w_view = t["w_out"][0].rearrange("(k p) n -> p k n", p=P)

        block = scope.enter_context(nc.Block())

        @block.sync
        def _(sp):
            for i in range(2):
                sp.dma_start(w_raw[:, i], w_view[:, :, i * P:(i + 1) * P]).then_inc(w_loaded[i], 16)
            for k in range(KC):
                if k >= 2:
                    sp.wait_ge(mix_lo, k - 1)
                sp.dma_start(mix[:, k % 2], v.mix_dram[k]).then_inc(mix_loaded[k % 2], 16)
            sp.dma_start(xT[:], v.x_dram).then_inc(x_loaded, 16)
            with sp.Fori(1, KC // 2) as it:
                for i in range(2):
                    sp.wait_ge(w_split_lo, it * 2 + i - 1)
                    sp.dma_start(w_raw[:, i], w_view[:, :, ds((it * 2 + i) * P, P)]).then_inc(w_loaded[i], 16)
            sp.wait_ge(piece_out, NG * KC)
            sp.dma_start(v.x_dram, xT[:]).then_inc(x_saved, 16)
            sp.wait_ge(x_saved, 16)

        @block.scalar
        def _(act):
            for k in range(KC):
                act.wait_ge(mix_loaded[k % 2], 16 * (k // 2 + 1))
                act.activation(v.hi[:, k], mix[:, k % 2], ACT.Copy).then_inc(mix_hi, 1)
            for i in range(2):
                act.wait_ge(w_loaded[i], 16)
                act.activation(w_hi[:, i], w_raw[:, i], ACT.Copy).then_inc(w_split_hi, 1)
            with act.Fori(1, KC // 2) as it:
                for i in range(2):
                    act.wait_ge(w_loaded[i], it * 16 + 16)
                    act.wait_ge(piece_done, it * 6 + 3 * (i - 1))
                    act.activation(w_hi[:, i], w_raw[:, i], ACT.Copy).then_inc(w_split_hi, 1)
            act.wait_ge(piece_out, NG * KC)
            norm_act(act, v, S, xT, sq, rstd, mix)

        @block.gpsimd
        def _(pool):
            with pool.Fori(0, KC // 2) as it:
                for i in range(2):
                    pool.wait_ge(w_split_hi, it * 2 + i + 1)
                    pool.tensor_tensor(w_lo[:, i], w_raw[:, i], w_hi[:, i].bitcast(F32), ALU.subtract).then_inc(w_split_lo, 1)

        @block.tensor
        def _(pe):
            pe.wait_ge(mix_lo, KC)
            def tile(n, i, first):
                pe.wait_ge(w_split_lo, n + 1)
                for g in range(NG):
                    if not first:
                        pe.wait_ge(piece_out, n * NG + (g + 1 - 2 * NG))
                    for k in range(KC):
                        mm = split_piece(pe, ps[:, NG * i + g, 0:GRP], w_hi[:, i, k], w_lo[:, i, k],
                                         v.hi[:, k, g * GRP:(g + 1) * GRP], v.lo[:, k, g * GRP:(g + 1) * GRP],
                                         k, k == 0, k == KC - 1)
                    mm.then_inc(piece_done, 1)

            for i in range(2):
                tile(i, i, True)
            with pe.Fori(1, KC // 2) as it:
                for i in range(2):
                    tile(it * 2 + i, i, False)
            norm_pe(pe, v, S, sq)

        @block.vector
        def _(dve):
            for k in range(KC):
                dve.wait_ge(mix_hi, k + 1)
                dve.tensor_tensor(v.lo[:, k], mix[:, k % 2], v.hi[:, k].bitcast(F32), ALU.subtract).then_inc(mix_lo, 1)
            dve.wait_ge(x_loaded, 16)
            with dve.Fori(0, KC // 2) as it:
                for i in range(2):
                    for g in range(NG):
                        dve.wait_ge(piece_done, it * (2 * NG) + (NG * i + g + 1))
                        x = xT[:, ds(it * 2 + i, 1), g * GRP:(g + 1) * GRP].rearrange("p a n -> p (a n)")
                        dve.tensor_tensor(x, x, ps[:, NG * i + g, 0:GRP], ALU.add).then_inc(piece_out, 1)
            dve.drain()
            norm_dve(dve, v, S, xT, rstd, mix, 1, v.lo)


def ffn_up_down(nc, t, v):
    with ExitStack() as outer:
        act_t = v.sb("ffn_act", [P, FT, TOK], F32, outer)
        ffn_up(nc, t, v, act_t)
        ffn_down(nc, t, v, act_t)


def ffn_up(nc, t, v, act_t):
    with ExitStack() as scope:
        def sb(name, shape, dt=F32):
            return v.sb(name, shape, dt, scope)

        ps = v.ps
        w_raw = sb("wu_raw", [P, 2, KC, P])
        w_hi = sb("wu_hi", [P, 2, KC, P], F32R)
        w_lo = sb("wu_lo", [P, 2, KC, P], F32R)
        gate = sb("gate_ext", [P, FEXT])
        y = sb("gate_conv", [P, FCONV])
        par = sb("fconv_f", [P, 20])
        tail = sb("gate_tail", [P, FTAPS - 1 + DEC])
        tail_rows = sb("gate_tail_rows", [FTAPS - 1 + DEC, P])
        w_loaded = [v.sem("wu_loaded0"), v.sem("wu_loaded1")]
        w_split_hi, w_split_lo = v.sem("wu_split_hi"), v.sem("wu_split_lo")
        piece_done, gate_out, up_out = v.sem("wu_piece_done"), v.sem("gate_out"), v.sem("up_out")
        context_in, conv_done, silu_done = v.sem("gate_context_in"), v.sem("gate_conv_done"), v.sem("gate_silu_done")
        tail_ready, tail_turned, tail_out, tail_stored = v.sem("gt_ready"), v.sem("gt_turned"), v.sem("gt_out"), v.sem("gt_stored")
        ctx_copied, gate_zeroed = v.sem("gate_ctx_copied"), v.sem("gate_zeroed")
        w_view = t["w_up"][0].rearrange("(k p) n -> p k n", p=P)
        CREDIT = 2

        block = scope.enter_context(nc.Block())

        @block.sync
        def _(sp):
            sp.dma_start(t["new_ffn_conv_sample"][0, :, 0:1, :], t["state_ffn_conv"][0, :, 1:2, :]).then_inc(ctx_copied, 16)
            with sp.Fori(0, FT) as f:
                for i in range(2):
                    sp.wait_ge(w_split_lo, f * 2 + (i + 1 - 2 + CREDIT))
                    sp.dma_start(w_raw[:, i], w_view[:, :, ds(f * P + FFN * i, P)]).then_inc(w_loaded[i], 16)
            sp.wait_ge(ctx_copied, 16)

        @block.gpsimd
        def _(pool):
            pool.sem_inc(w_split_lo, CREDIT)
            pool.memset(gate[:, 0:FTAPS - 1], 0.0).then_inc(gate_zeroed, 1)
            with pool.Fori(0, FT) as f:
                for i in range(2):
                    pool.wait_ge(w_split_hi, f * 2 + (i + 1))
                    pool.tensor_tensor(w_lo[:, i], w_raw[:, i], w_hi[:, i].bitcast(F32), ALU.subtract).then_inc(w_split_lo, 1)

        @block.tensor
        def _(pe):
            pe.sem_inc(piece_done, 2 * NG)
            pe.sem_inc(tail_turned, 1)
            with pe.Fori(0, FT) as f:
                for i in range(2):
                    pe.wait_ge(w_split_lo, f * 2 + (i + 1 + CREDIT))
                    for g in range(NG):
                        pe.wait_ge((gate_out, up_out)[i], f * NG + (g + 1))
                        for k in range(KC):
                            mm = split_piece(pe, ps[:, NG * i + g, 0:GRP], w_hi[:, i, k], w_lo[:, i, k],
                                             v.hi[:, k, g * GRP:(g + 1) * GRP], v.lo[:, k, g * GRP:(g + 1) * GRP],
                                             k, k == 0, k == KC - 1)
                        mm.then_inc(piece_done, 1)
                    pe.wait_ge(tail_ready, f + 1)
                pe.transpose(ps[0:FTAPS - 1 + DEC, 6, 0:P], tail[:], v.ident[:]).then_inc(tail_turned, 1)

        @block.scalar
        def _(act):
            act.sem_inc(gate_out, NG)
            act.sem_inc(tail_stored, 32)
            act.wait_ge(gate_zeroed, 1)
            def split(f, i):
                act.wait_ge(w_loaded[i], f * 16 + 16)
                act.wait_ge(piece_done, f * (2 * NG) + NG * (i + 1))
                act.activation(w_hi[:, i], w_raw[:, i], ACT.Copy).then_inc(w_split_hi, 1)

            with act.Fori(0, FT) as f:
                split(f, 0)
                split(f, 1)
                act.wait_ge(conv_done, f + 1)
                for g in range(NG):
                    act.wait_ge(piece_done, f * (2 * NG) + (2 * NG + g + 1))
                    a = g * GRP
                    n = min(GRP, SEQ - a)
                    ins = act.activation(gate[:, FTAPS - 1 + a:FTAPS - 1 + a + n], ps[:, g, 0:n], ACT.Copy)
                    if n < GRP:
                        ins = act.activation(gate[:, FTAPS - 1 + SEQ:].rearrange("p (b i) -> p b i", b=DEC)[:, :, FTAPS - 1], ps[:, g, n:GRP], ACT.Copy)
                    ins.then_inc(gate_out, 1)
                act.wait_ge(conv_done, f + 2)
                act.activation(y[:], y[:], ACT.Silu).then_inc(silu_done, 1)
                act.wait_ge(tail_out, f + 2)
                act.dma_start(t["new_ffn_conv_prompt"][0, 0, :, ds(f * P, P)], tail_rows[0:FTAPS - 1]).then_inc(tail_stored, 16)
                act.dma_start(t["new_ffn_conv_sample"][0, :, FTAPS - 2, ds(f * P, P)], tail_rows[FTAPS - 1:]).then_inc(tail_stored, 16)
            act.wait_ge(tail_stored, 32 * (FT + 1))

        @block.vector
        def _(dve):
            dve.sem_inc(up_out, NG)
            dve.sem_inc(conv_done, 1)
            dve.sem_inc(tail_out, 1)
            with dve.Fori(0, FT) as f:
                dve.tensor_copy(par[:].unsqueeze(1), v.fconv[:, ds(f, 1), :])
                dve.drain()
                decode = gate[:, FTAPS - 1 + SEQ:].rearrange("p (b i) -> p b i", b=DEC)
                dve.tensor_copy(decode[:, :, 0:FTAPS - 1], par[:, 4:20].rearrange("p (b i) -> p b i", b=DEC))
                dve.wait_ge(gate_out, f * NG + 2 * NG)
                dve.wait_ge(tail_turned, f + 1)
                dve.tensor_copy(tail[:, 0:FTAPS - 1], gate[:, SEQ:SEQ + FTAPS - 1])
                dve.tensor_copy(tail[:, FTAPS - 1:], decode[:, :, FTAPS - 1]).then_inc(tail_ready, 1)
                dve.drain()
                dve.tensor_scalar(y[:], gate[:, 0:FCONV], par[:, 0:1], par[:, 3:4], ALU.mult, ALU.add)
                for i in range(1, FTAPS):
                    dve.drain()
                    ins = dve.scalar_tensor_tensor(out=y[:], in0=gate[:, i:i + FCONV], scalar=par[:, i:i + 1], in1=y[:], op0=ALU.mult, op1=ALU.add)
                ins.then_inc(conv_done, 1)
                dve.wait_ge(tail_turned, f + 2)
                dve.wait_ge(tail_stored, f * 32 + 32)
                dve.tensor_copy(tail_rows[:], ps[0:FTAPS - 1 + DEC, 6, 0:P]).then_inc(tail_out, 1)
                dve.wait_ge(silu_done, f + 1)
                for g in range(NG):
                    dve.wait_ge(piece_done, f * (2 * NG) + (3 * NG + g + 1))
                    a = g * GRP
                    n = min(GRP, SEQ - a)
                    ins = dve.tensor_tensor(act_t[:, ds(f, 1), a:a + n].rearrange("p a n -> p (a n)"), y[:, a:a + n], ps[:, NG + g, 0:n], ALU.mult)
                    if n < GRP:
                        yd = y[:, SEQ:FCONV].rearrange("p (b i) -> p b i", b=DEC)[:, :, FTAPS - 1]
                        ins = dve.tensor_tensor(act_t[:, ds(f, 1), SEQ:TOK].rearrange("p a n -> p (a n)"), yd, ps[:, NG + g, n:GRP], ALU.mult)
                    ins.then_inc(up_out, 1)


def ffn_down(nc, t, v, act_t):
    with ExitStack() as scope:
        def sb(name, shape, dt=F32):
            return v.sb(name, shape, dt, scope)

        ps = v.ps
        COLS = 2
        PASSES = KC // COLS
        w_raw = sb("wd_raw", [P, 2, COLS * P])
        w_hi = sb("wd_hi", [P, 2, COLS * P], F32R)
        w_lo = sb("wd_lo", [P, 2, COLS * P], F32R)
        x_cols = sb("x_cols", [P, COLS, TOK])
        w_loaded = [v.sem("wd_loaded0"), v.sem("wd_loaded1")]
        w_split_hi, w_split_lo, used = v.sem("wd_split_hi"), v.sem("wd_split_lo"), v.sem("wd_used")
        a_hi, a_lo = v.sem("ffn_act_hi"), v.sem("ffn_act_lo")
        pass_out = v.sem("down_pass_out")
        x_loaded, x_saved = v.sem("x_cols_loaded"), v.sem("x_cols_saved")
        CREDIT = 2

        block = scope.enter_context(nc.Block())

        def over_chunks(eng, c, step):
            def pair(k, first, last):
                for i in range(2):
                    step(c * FT + (k + i), k + i, i, first and i == 0, last and i == 1)
            pair(0, True, False)
            with eng.Fori(1, FT // 2 - 1) as it:
                pair(it * 2, False, False)
            pair(FT - 2, False, True)

        @block.sync
        def _(sp):
            with sp.Fori(0, PASSES) as c:
                sp.wait_ge(x_saved, c * 16 + 16)
                xs = v.x_dram[:, ds(c * COLS, COLS), :]
                sp.dma_start(x_cols[:], xs).then_inc(x_loaded, 16)

                def load(n, k, i, first, last):
                    sp.wait_ge(w_split_lo, n + (1 - 2 + CREDIT))
                    sp.dma_start(w_raw[:, i], t["w_down"][0, ds(k * P, P), ds(c * (COLS * P), COLS * P)]).then_inc(w_loaded[i], 16)

                over_chunks(sp, c, load)
                sp.wait_ge(pass_out, c * (COLS * NG) + 2 * COLS * NG)
                sp.dma_start(xs, x_cols[:]).then_inc(x_saved, 16)
            sp.wait_ge(x_saved, 16 * (PASSES + 1))

        @block.gpsimd
        def _(pool):
            pool.sem_inc(w_split_lo, CREDIT)
            pool.sem_inc(x_saved, 16)
            with pool.Fori(0, PASSES) as c:
                def split(n, k, i, first, last):
                    pool.wait_ge(w_split_hi, n + 1)
                    pool.tensor_tensor(w_lo[:, i], w_raw[:, i], w_hi[:, i].bitcast(F32), ALU.subtract).then_inc(w_split_lo, 1)

                over_chunks(pool, c, split)

        @block.scalar
        def _(act):
            with act.Fori(0, PASSES) as c:
                def split(n, k, i, first, last):
                    act.wait_ge(used, n + (1 - 2 + CREDIT))
                    act.activation(v.hi[:, i], act_t[:, k] if isinstance(k, int) else act_t[:, ds(k, 1)].rearrange("p a n -> p (a n)"), ACT.Copy).then_inc(a_hi, 1)
                    act.wait_ge(w_loaded[i], c * (8 * FT) + (k - i) * 8 + 16)
                    act.activation(w_hi[:, i], w_raw[:, i], ACT.Copy).then_inc(w_split_hi, 1)

                over_chunks(act, c, split)

        @block.tensor
        def _(pe):
            pe.sem_inc(used, CREDIT)
            with pe.Fori(0, PASSES) as c:
                def multiply(n, k, i, first, last):
                    pe.wait_ge(a_lo, n + 1)
                    pe.wait_ge(w_split_lo, n + (1 + CREDIT))
                    for m in range(COLS):
                        for g in range(NG):
                            if first:
                                pe.wait_ge(pass_out, c * (COLS * NG) + (m * NG + g + 1))
                            cols = slice(m * P, (m + 1) * P)
                            mm = split_piece(pe, ps[:, m * NG + g, 0:GRP], w_hi[:, i, cols], w_lo[:, i, cols],
                                             v.hi[:, i, g * GRP:(g + 1) * GRP], v.lo[:, i, g * GRP:(g + 1) * GRP],
                                             0, first, last)
                    mm.then_inc(used, 1)

                over_chunks(pe, c, multiply)

        @block.vector
        def _(dve):
            dve.sem_inc(pass_out, COLS * NG)
            with dve.Fori(0, PASSES) as c:
                def split(n, k, i, first, last):
                    dve.wait_ge(a_hi, n + 1)
                    src = act_t[:, k] if isinstance(k, int) else act_t[:, ds(k, 1)].rearrange("p a n -> p (a n)")
                    dve.tensor_tensor(v.lo[:, i], src, v.hi[:, i].bitcast(F32), ALU.subtract).then_inc(a_lo, 1)

                over_chunks(dve, c, split)
                dve.wait_ge(x_loaded, c * 16 + 16)
                dve.wait_ge(used, c * FT + (FT + CREDIT))
                for m in range(COLS):
                    for g in range(NG):
                        x = x_cols[:, m, g * GRP:(g + 1) * GRP]
                        dve.tensor_tensor(x, x, ps[:, m * NG + g, 0:GRP], ALU.add).then_inc(pass_out, 1)


def finish(nc, t, v):
    with ExitStack() as scope:
        def sb(name, shape, dt=F32):
            return v.sb(name, shape, dt, scope)

        ps = v.ps
        xT = sb("xT2", [P, KC, TOK])
        sq = sb("sq2", [P, KC, GRP])
        rstd = sb("rstd2", [P, TOK])
        yT = sb("yT", [P, 2, KC, P])
        rows = sb("y_rows", [P, 2, D])
        x_loaded, y_ready, y_turned = v.sem("x2_loaded"), v.sem("y_ready"), v.sem("y_turned")
        y_copied = v.sem("y_copied")
        y_stored = [v.sem("y_stored0"), v.sem("y_stored1")]
        S = norm_signals(v, "n2")
        CREDIT = 2

        block = scope.enter_context(nc.Block())

        @block.sync
        def _(sp):
            sp.dma_start(xT[:], v.x_dram).then_inc(x_loaded, 16)
            with sp.Fori(0, NBLK // 2) as it:
                for i in range(2):
                    sp.wait_ge(y_copied, it * 2 + (i + 1 + CREDIT))
                    sp.dma_start(t["y_prompt"][0, ds((it * 2 + i) * P, P)], rows[:, i]).then_inc(y_stored[i], 16)
            sp.wait_ge(y_copied, NBLK + 1 + CREDIT)
            sp.dma_start(t["y_sample"].rearrange("b a d -> (b a) d"), rows[0:DEC, 0]).then_inc(y_stored[0], 16)
            sp.wait_ge(y_stored[0], 16 * (NBLK // 2 + 2))
            sp.wait_ge(y_stored[1], 16 * (NBLK // 2 + 1))

        @block.gpsimd
        def _(pool):
            pool.sem_inc(y_stored[0], 16)
            pool.sem_inc(y_stored[1], 16)

        def normed(dve, cols, i, n, turned):
            dve.wait_ge(y_turned, turned)
            dve.tensor_tensor(yT[:, i, :, 0:n], xT[:, :, cols], rstd[:, cols].unsqueeze(1).broadcast_to([P, KC, n]), ALU.mult)
            dve.drain()
            dve.tensor_tensor(yT[:, i, :, 0:n], yT[:, i, :, 0:n], v.norms[:, :, 2:3].broadcast_to([P, KC, n]), ALU.mult).then_inc(y_ready, 1)

        @block.vector
        def _(dve):
            dve.sem_inc(y_copied, CREDIT)
            dve.wait_ge(S["rstd"], 1)
            with dve.Fori(0, NBLK // 2) as it:
                for i in range(2):
                    normed(dve, ds((it * 2 + i) * P, P), i, P, it * 2 + (i - 1 + CREDIT))
                for i in range(2):
                    dve.wait_ge(y_turned, it * 2 + (i + 1 + CREDIT))
                    dve.wait_ge(y_stored[i], it * 16 + 16)
                    ins = [dve.tensor_copy(rows[:, i, 512 * hf:512 * (hf + 1)], ps[:, 2 * i + hf]) for hf in range(2)][1]
                    ins.then_inc(y_copied, 1)
            normed(dve, slice(SEQ, TOK), 0, DEC, NBLK - 1 + CREDIT)
            dve.wait_ge(y_turned, NBLK + 1 + CREDIT)
            dve.wait_ge(y_stored[0], 16 * (NBLK // 2 + 1))
            ins = [dve.tensor_copy(rows[0:DEC, 0, 512 * hf:512 * (hf + 1)], ps[0:DEC, hf]) for hf in range(2)][1]
            ins.then_inc(y_copied, 1)

        @block.scalar
        def _(act):
            act.wait_ge(x_loaded, 16)
            norm_act(act, v, S, xT, sq, rstd, None)

        @block.tensor
        def _(pe):
            pe.sem_inc(y_turned, CREDIT)
            norm_pe(pe, v, S, sq)
            pe.wait_ge(S["rstd"], 1)

            def turn(n, i, width):
                pe.wait_ge(y_ready, n + 1)
                pe.wait_ge(y_copied, n + (1 - 2 + CREDIT))
                for k in range(KC):
                    mm = pe.transpose(ps[0:width, 2 * i + k // 4, (k % 4) * P:(k % 4 + 1) * P], yT[:, i, k, 0:width], v.ident[:])
                mm.then_inc(y_turned, 1)

            with pe.Fori(0, NBLK // 2) as it:
                for i in range(2):
                    turn(it * 2 + i, i, P)
            turn(NBLK, 0, DEC)


INPUTS = ["x_prompt", "x_sample", "cache_k", "cache_v", "cache_logf", "state_gdn", "state_gdn_conv",
          "state_ffn_conv", "page_table", "norm_mix", "w_in", "b_forget", "gdn_a_log", "gdn_dt_bias",
          "w_gdn_conv", "gdn_out_norm", "w_out", "norm_ffn", "w_up", "w_ffn_conv", "b_ffn_conv", "w_down",
          "norm_final"]
OUTPUTS = [("y_prompt", (1, SEQ, D)), ("y_sample", (DEC, 1, D)),
           ("new_k_prompt", (1, 1, SEQ, FH, FD)), ("new_v_prompt", (1, 1, SEQ, FH, FD)),
           ("new_logf_prompt", (1, 1, SEQ, FH)), ("new_gdn_prompt", (1, 1, GH, GD, GD)),
           ("new_gdn_conv_prompt", (1, 1, TAPS - 1, 3 * GW)), ("new_ffn_conv_prompt", (1, 1, FTAPS - 1, FFN)),
           ("new_k_sample", (1, DEC, 1, FH, FD)), ("new_v_sample", (1, DEC, 1, FH, FD)),
           ("new_logf_sample", (1, DEC, 1, FH)), ("new_gdn_sample", (1, DEC, GH, GD, GD)),
           ("new_gdn_conv_sample", (1, DEC, TAPS - 1, 3 * GW)), ("new_ffn_conv_sample", (1, DEC, FTAPS - 1, FFN))]


def kernel(**inputs):
    import numpy as np
    import concourse.bacc as bacc
    from concourse import mybir as mb
    from concourse.bass_utils import run_bass_kernel_spmd

    nc = bacc.Bacc("TRN2", target_bir_lowering=False, num_devices=1)
    arrays, t = {}, {}
    for name in INPUTS:
        a = np.ascontiguousarray(inputs[name])
        arrays[f"in_{name}"] = a
        t[name] = nc.dram_tensor(f"in_{name}", a.shape, mb.dt.from_np(a.dtype), kind="ExternalInput").ap()
    for name, shape in OUTPUTS:
        t[name] = nc.dram_tensor(f"out_{name}", shape, mb.dt.float32, kind="ExternalOutput").ap()
    program(nc, t)
    r = run_bass_kernel_spmd(nc, [arrays], core_ids=[0])
    return tuple(r.results[0][f"out_{name}"] for name, _ in OUTPUTS)
```

```python
from contextlib import ExitStack

import concourse.bass as bass
from concourse import mybir

ALU = mybir.AluOpType
ACT = mybir.ActivationFunctionType
AX = mybir.AxisListType
F32 = mybir.dt.float32
F32R = mybir.dt.float32r
I32 = mybir.dt.int32
RMAX = bass.bass_isa.ReduceOp.max
ds = bass.ds

P = 128
D = 1024
KC = D // P
SEQ = 1024
NBLK = SEQ // P
DEC = 8
TOK = SEQ + DEC
GRP = TOK // 3
NG = TOK // GRP
FH, FD = 8, 64
FW = FH * FD
GH, GD = 4, 128
GW = GH * GD
PAGES = 8
TAPS = 4
EXT = (TAPS - 1) + SEQ + TAPS * DEC
CONV = EXT - (TAPS - 1)
FFN = 2816
FT = FFN // P
FTAPS = 3
FEXT = (FTAPS - 1) + SEQ + FTAPS * DEC
FCONV = FEXT - (FTAPS - 1)
EPS = 1e-6
NEG_BIG = -1e30
SCALE = FD ** -0.5
LN_GSCALE = -0.5 * 4.852030263919617
EARLY_PAGES = 32
STEPS = 4
R_F, R_A, R_B, GROWS = 0, 32, 64, 96
C_FQ, C_FK, C_FV, C_FF = 0, FW, 2 * FW, 3 * FW
C_GQ = C_FF + FH
C_GK, C_GV = C_GQ + GW, C_GQ + 2 * GW
C_GA = C_GQ + 3 * GW
C_GZ = C_GA + 2 * GH
TILE_COL = (C_FQ, C_FK, C_FV, C_GQ, C_GK, C_GV, C_GZ)
NTILE = len(TILE_COL)


class OnChip:

    def __init__(self, sem, mixer_sem, sb, ps, x_dram, mix_dram, gate_dram, ident, ones, head_ones, later,
                 causal, level_mask, norms, gconv, fconv, out_norm, hi, lo, logf_n,
                 beta_n, gcum_n, page_ids, dec_bias, dec_gates):
        self.sem = sem
        self.mixer_sem = mixer_sem
        self.sb = sb
        self.ps = ps
        self.x_dram = x_dram
        self.mix_dram = mix_dram
        self.gate_dram = gate_dram
        self.ident = ident
        self.ones = ones
        self.head_ones = head_ones
        self.later = later
        self.causal = causal
        self.level_mask = level_mask
        self.norms = norms
        self.gconv = gconv
        self.fconv = fconv
        self.out_norm = out_norm
        self.hi = hi
        self.lo = lo
        self.logf_n = logf_n
        self.beta_n = beta_n
        self.gcum_n = gcum_n
        self.page_ids = page_ids
        self.dec_bias = dec_bias
        self.dec_gates = dec_gates


def groups(width, n):
    step = width // n
    return [(g * step, step) for g in range(n)]


def program(nc, t):
    stack = ExitStack()
    mixer_sems = []

    def sem(name):
        return stack.enter_context(nc.semaphore(name))

    def mixer_sem(name):
        mixer_sems.append(nc.alloc_semaphore(name))
        return mixer_sems[-1]

    def sb(name, shape, dt=F32, scope=None):
        return (scope or stack).enter_context(nc.sbuf_tensor(name, shape, dt))

    with stack:
        ps = stack.enter_context(nc.psum_tensor("ps", [P, 8, 512], F32))
        x_dram = nc.dram_tensor("x_scratch", [P, KC, TOK], F32, kind="Internal").ap()
        mix_dram = nc.dram_tensor("mix_scratch", [KC, P, TOK], F32, kind="Internal").ap()
        gate_dram = nc.dram_tensor("gate_scratch", [GROWS, SEQ], F32, kind="Internal").ap()

        ident = sb("ident", [P, P])
        ones = sb("ones", [P, P])
        head_ones = sb("head_ones", [P, 2, P])
        later = sb("later", [P, P])
        causal = sb("causal", [P, P])
        level_mask = sb("level_mask", [P, 7, P])
        norms = sb("norms", [P, KC, 3])
        gconv = sb("gconv", [P, 3 * GH, 28])
        fconv = sb("fconv", [P, FT, 20])
        out_norm = sb("out_norm", [P, 1])
        hi = sb("act_hi", [P, KC, TOK], F32R)
        lo = sb("act_lo", [P, KC, TOK], F32R)
        logf_n = sb("logf_n", [P, NBLK + 1, FH])
        beta_n = sb("beta_n", [P, NBLK, GH])
        gcum_n = sb("gcum_n", [P, NBLK, GH])
        page_ids = sb("page_ids", [1, DEC * PAGES], I32)
        dec_bias = sb("dec_bias", [P, DEC * PAGES, FH])
        dec_gates = sb("dec_gates", [P, 2, GH, DEC])

        v = OnChip(sem, mixer_sem, sb, ps, x_dram, mix_dram, gate_dram, ident, ones, head_ones, later,
                   causal, level_mask, norms, gconv, fconv, out_norm, hi, lo,
                   logf_n, beta_n, gcum_n, page_ids, dec_bias, dec_gates)

        with ExitStack() as early:
            past = sb("past_logf", [P, DEC * PAGES, FH], scope=early)
            past_loaded = sem("past_loaded")
            setup(nc, t, v, past, past_loaded)
            gates(nc, t, v, past, past_loaded)
        mixer(nc, t, v)
        nc.clear_and_free_semaphores(mixer_sems)
        nc.all_engine_barrier()
        dense(nc, t, v)


def split_piece(pe, out, w_hi, w_lo, a_hi, a_lo, k, first, last):
    pe.matmul(out, w_hi, a_hi, start=first, stop=False)
    pe.matmul(out, w_hi, a_lo, start=False, stop=False)
    return pe.matmul(out, w_lo, a_hi, start=False, stop=last)


def load_pages(eng, v, t, past, past_loaded, first, end):
    with eng.Fori(first, end) as n:
        page = eng.value_load(v.page_ids[0:1, ds(n, 1)], min_val=0, max_val=t["cache_logf"].shape[1] - 1)
        eng.dma_start(past[:, ds(n, 1), :].rearrange("p a h -> p (a h)"),
                      t["cache_logf"][0, ds(page, 1)].rearrange("a p h -> p (a h)")).then_inc(past_loaded, 16)


def setup(nc, t, v, past, past_loaded):
    with ExitStack() as scope:
        def sb(name, shape, dt=F32):
            return v.sb(name, shape, dt, scope)

        xT = sb("xT0", [P, KC, TOK])
        xn = sb("x_rows", [P, 2, D])
        vec_rows = sb("vec_rows", [3, D])
        gconv_rows = sb("gconv_rows", [28, 3 * GW])
        fconv_rows = sb("fconv_rows", [20, FFN])
        sq = sb("sq0", [P, 2, KC, P])
        sq_sum = sb("sq_sum0", [P, TOK])
        rstd = sb("rstd0", [P, TOK])
        tmp = sb("h_tmp0", [P, KC, TOK])
        ps = v.ps
        x_loaded = [v.sem("x_loaded0"), v.sem("x_loaded1")]
        params_loaded, consts_ready = v.sem("params_loaded"), v.sem("consts_ready")
        x_turned, x_copied = v.sem("x_turned"), v.sem("x_copied")
        par_turned, par_copied = v.sem("par_turned"), v.sem("par_copied")
        blk_squared, blk_summed = v.sem("blk_squared"), v.sem("blk_summed")
        x_saved, ids_loaded = v.sem("x_saved"), v.sem("ids_loaded")
        S = norm_signals(v, "n0")

        block = scope.enter_context(nc.Block())

        @block.sync
        def _(sp):
            sp.dma_start(v.page_ids[:], t["page_table"].rearrange("b p -> (b p)").rearrange("(a n) -> a n", a=1)).then_inc(ids_loaded, 16)
            sp.dma_start(vec_rows[0:1, :], t["norm_mix"]).then_inc(params_loaded, 16)
            sp.dma_start(vec_rows[1:2, :], t["norm_ffn"]).then_inc(params_loaded, 16)
            sp.dma_start(vec_rows[2:3, :], t["norm_final"].rearrange("(a d) -> a d", a=1)).then_inc(params_loaded, 16)
            sp.dma_start(gconv_rows[0:4, :], t["w_gdn_conv"][0]).then_inc(params_loaded, 16)
            sp.dma_start(gconv_rows[4:28, :], t["state_gdn_conv"][0].rearrange("b i c -> (b i) c")).then_inc(params_loaded, 16)
            sp.dma_start(fconv_rows[0:3, :], t["w_ffn_conv"][0]).then_inc(params_loaded, 16)
            sp.dma_start(fconv_rows[3:4, :], t["b_ffn_conv"]).then_inc(params_loaded, 16)
            sp.dma_start(fconv_rows[4:20, :], t["state_ffn_conv"][0].rearrange("b i c -> (b i) c")).then_inc(params_loaded, 16)
            sp.dma_start(v.out_norm[:], t["gdn_out_norm"].rearrange("a d -> d a")).then_inc(params_loaded, 16)
            sp.wait_ge(ids_loaded, 16)
            load_pages(sp, v, t, past, past_loaded, 0, EARLY_PAGES)

        @block.gpsimd
        def _(pool):
            pool.memset(v.ident[:], 0.0)
            pool.memset(v.ones[:], 1.0)
            pool.memset(v.later[:], 1.0)
            pool.memset(v.causal[:], 0.0)
            pool.memset(v.head_ones[:], 0.0)
            pool.memset(v.level_mask[:], 0.0)
            pool.drain()
            pool.memset(v.head_ones[0:FD, 0], 1.0)
            pool.drain()
            pool.memset(v.head_ones[FD:P, 1], 1.0)
            pool.drain()
            for l in range(7):
                b = 1 << l
                m = v.level_mask[:, l].rearrange("p (n w) -> p n w", w=2 * b)
                pool.memset(m[:, :, b:2 * b], 1.0)
            pool.affine_select(out=v.ident[:], in_=v.ident[:], compare_op=ALU.not_equal, fill=1.0, base=0,
                               pattern=[[-1, P]], channel_multiplier=1)
            pool.affine_select(out=v.later[:], in_=v.later[:], compare_op=ALU.is_ge, fill=0.0, base=-1,
                               pattern=[[-1, P]], channel_multiplier=1)
            pool.affine_select(out=v.causal[:], in_=v.causal[:], compare_op=ALU.is_ge, fill=NEG_BIG / SCALE, base=0,
                               pattern=[[-1, P]], channel_multiplier=1)
            pool.drain()
            for l in range(7):
                b = 1 << l
                m = v.level_mask[:, l].rearrange("p (n w) -> p n w", w=2 * b)
                n = P // (2 * b)
                pool.affine_select(out=m, in_=m, compare_op=ALU.is_ge, fill=0.0, base=0,
                                   pattern=[[-2 * b, n], [0, 2 * b]], channel_multiplier=1)
                pool.drain()
                pool.affine_select(out=m, in_=m, compare_op=ALU.is_ge, fill=0.0, base=b - 1,
                                   pattern=[[2 * b, n], [0, 2 * b]], channel_multiplier=-1)
            pool.drain()
            pool.drain().then_inc(consts_ready, 1)
            pool.wait_ge(x_copied, NBLK + 1)
            pool.dma_start(v.x_dram, xT[:]).then_inc(x_saved, 16)
            norm_pool(pool, v, S, tmp, v.lo)
            pool.wait_ge(x_saved, 16)

        def turn(pe, i, slot, n, last_of):
            for k in range(KC):
                mm = pe.transpose(ps[:, 2 * slot + k // 4, (k % 4) * P:(k % 4) * P + n],
                                  xn[0:n, slot, k * P:(k + 1) * P], v.ident[0:n, 0:n])
            mm.then_inc(x_turned, 1)

        @block.tensor
        def _(pe):
            pe.wait_ge(consts_ready, 1)
            for i in range(2):
                pe.wait_ge(x_loaded[i], 16)
                turn(pe, i, i, P, None)
            with pe.Fori(1, NBLK // 2) as it:
                for i in range(2):
                    pe.wait_ge(x_loaded[i], it * 16 + 16)
                    pe.wait_ge(x_copied, it * 2 + i - 1)
                    turn(pe, i, i, P, None)
            pe.wait_ge(x_loaded[0], 16 * (NBLK // 2 + 1))
            pe.wait_ge(x_copied, NBLK - 1)
            turn(pe, NBLK, 0, DEC, None)
            pe.wait_ge(params_loaded, 144)
            for k in range(KC):
                pe.transpose(ps[:, 4, k * 3:k * 3 + 3], vec_rows[0:3, k * P:(k + 1) * P], v.ident[0:3, 0:3])
            for k in range(3 * GH):
                pe.transpose(ps[:, 5, k * 28:k * 28 + 28], gconv_rows[:, k * P:(k + 1) * P], v.ident[0:28, 0:28])
            for k in range(FT):
                mm = pe.transpose(ps[:, 6, k * 20:k * 20 + 20], fconv_rows[:, k * P:(k + 1) * P], v.ident[0:20, 0:20])
            mm.then_inc(par_turned, 1)
            norm_pe(pe, v, S, sq_sum)

        def copy_out(dve, slot, n, cols):
            for half in range(2):
                src = ps[:, 2 * slot + half].rearrange("p (k t) -> p k t", k=4)[:, :, 0:n]
                ins = dve.tensor_copy(xT[:, 4 * half:4 * half + 4, cols], src)
            ins.then_inc(x_copied, 1)

        @block.vector
        def _(dve):
            def sum_squares(n, i, cols, width):
                dve.wait_ge(blk_squared, n + 1)
                dve.tensor_reduce(sq_sum[:, cols], sq[:, i, :, 0:width].rearrange("p k t -> p t k"), AX.X, ALU.add).then_inc(blk_summed, 1)

            with dve.Fori(0, NBLK // 2) as it:
                for i in range(2):
                    dve.wait_ge(x_turned, it * 2 + i + 1)
                    copy_out(dve, i, P, ds((it * 2 + i) * P, P))
                for i in range(2):
                    sum_squares(it * 2 + i, i, ds((it * 2 + i) * P, P), P)
            dve.wait_ge(x_turned, NBLK + 1)
            copy_out(dve, 0, DEC, slice(SEQ, TOK))
            sum_squares(NBLK, 0, slice(SEQ, TOK), DEC)
            dve.drain().then_inc(S["squared"], 1)
            dve.wait_ge(par_turned, 1)
            dve.tensor_copy(v.norms[:].rearrange("p k n -> p (k n)"), ps[:, 4, 0:3 * KC])
            dve.tensor_copy(v.gconv[:].rearrange("p k n -> p (k n)"), ps[:, 5, 0:28 * 3 * GH])
            dve.tensor_copy(v.fconv[:].rearrange("p k n -> p (k n)"), ps[:, 6, 0:20 * FT])
            dve.drain()
            norm_dve(dve, v, S, xT, rstd, tmp, 0, v.lo)

        @block.scalar
        def _(act):
            def square(n, i, cols, width):
                act.wait_ge(x_copied, n + 1)
                act.activation(sq[:, i, :, 0:width], xT[:, :, cols], ACT.Square).then_inc(blk_squared, 1)

            def load_x(i, rows):
                act.dma_start(xn[:, i], t["x_prompt"][0, rows]).then_inc(x_loaded[i], 16)

            for i in range(2):
                load_x(i, slice(i * P, (i + 1) * P))
            for i in range(2):
                square(i, i, slice(i * P, (i + 1) * P), P)
                load_x(i, slice((i + 2) * P, (i + 3) * P))
            with act.Fori(1, NBLK // 2 - 1) as it:
                for i in range(2):
                    act.wait_ge(blk_summed, it * 2 + i - 1)
                    square(it * 2 + i, i, ds((it * 2 + i) * P, P), P)
                    load_x(i, ds((it * 2 + i + 2) * P, P))
            for i in range(2):
                n = NBLK - 2 + i
                act.wait_ge(blk_summed, n - 1)
                square(n, i, slice(n * P, (n + 1) * P), P)
                if i == 0:
                    act.dma_start(xn[0:DEC, 0], t["x_sample"].rearrange("b a d -> (b a) d")).then_inc(x_loaded[0], 16)
            act.wait_ge(blk_summed, NBLK - 1)
            square(NBLK, 0, slice(SEQ, TOK), DEC)
            norm_act(act, v, S, rstd, tmp)


def norm_signals(v, name):
    return {k: v.sem(f"{name}_{k}") for k in ("squared", "summed", "rstd", "normed", "hi")}


def add_squares(dve, x, sq):
    dve.tensor_tensor(sq[:, 0], x, x, ALU.mult)
    dve.drain()
    dve.tensor_tensor(sq[:, 1], sq[:, 1], sq[:, 0], ALU.add)


def norm_act(act, v, S, rstd, tmp):
    for g in range(NG):
        act.wait_ge(S["summed"], g + 1)
        act.activation(rstd[:, g * GRP:(g + 1) * GRP], v.ps[:, g, 0:GRP], ACT.Ln, scale=1.0 / D, bias=EPS)
    act.drain()
    act.activation(rstd[:], rstd[:], ACT.Exp, scale=-0.5).then_inc(S["rstd"], 1)
    if tmp is not None:
        for k in range(KC):
            act.wait_ge(S["normed"], k + 1)
            act.activation(v.hi[:, k], tmp[:, k], ACT.Copy).then_inc(S["hi"], 1)


def norm_pe(pe, v, S, sq_sum):
    pe.wait_ge(S["squared"], 1)
    for g in range(NG):
        pe.matmul(v.ps[:, g, 0:GRP], v.ones[:], sq_sum[:, g * GRP:(g + 1) * GRP], start=True, stop=True).then_inc(S["summed"], 1)


def norm_dve(dve, v, S, xT, rstd, tmp, which, lo):
    dve.wait_ge(S["rstd"], 1)
    for k in range(KC + 1):
        if k < KC:
            dve.scalar_tensor_tensor(out=tmp[:, k], in0=xT[:, k], scalar=v.norms[:, k, which:which + 1],
                                     in1=rstd[:], op0=ALU.mult, op1=ALU.mult).then_inc(S["normed"], 1)
        if k % 2:
            dve.wait_ge(S["hi"], k)
            dve.tensor_tensor(lo[:, k - 1], tmp[:, k - 1], v.hi[:, k - 1].bitcast(F32), ALU.subtract)


def norm_pool(pool, v, S, tmp, lo):
    for k in range(1, KC, 2):
        pool.wait_ge(S["hi"], k + 1)
        pool.tensor_tensor(lo[:, k], tmp[:, k], v.hi[:, k].bitcast(F32), ALU.subtract)




def gates(nc, t, v, past, past_loaded):
    with ExitStack() as scope:
        def sb(name, shape, dt=F32):
            return v.sb(name, shape, dt, scope)

        w_raw = sb("wg_raw", [P, KC, FH + 2 * GH])
        w_hi = sb("wg_hi", [P, KC, GROWS], F32R)
        w_lo = sb("wg_lo", [P, KC, GROWS], F32R)
        sign, bias, coef = sb("g_sign", [GROWS, 1]), sb("g_bias", [GROWS, 1]), sb("g_coef", [GROWS, 1])
        y, mag, gate = sb("g_y", [GROWS, TOK]), sb("g_mag", [GROWS, TOK]), sb("g_gate", [GROWS, TOK])
        run, keep = sb("g_run", [GROWS, SEQ]), sb("g_keep", [GROWS, SEQ])
        dsel = sb("dec_sel", [GROWS, P])
        total = sb("dec_total", [P, DEC, FH])
        ps = v.ps
        w_loaded, b_loaded = v.sem("wg_loaded"), v.sem("gbias_loaded")
        prepared, bias_set = v.sem("g_prepared"), v.sem("g_bias_zeroed")
        split_hi, split_lo = v.sem("wg_split_hi"), v.sem("wg_split_lo")
        summed, y_ready, mag_ready = v.sem("g_summed"), v.sem("g_y_ready"), v.sem("g_mag_ready")
        coef_ready, gate_ready, beta_ready = v.sem("g_coef_ready"), v.sem("g_gate_ready"), v.sem("g_beta_ready")
        run_ready, turned, sel_ready = v.sem("g_run_ready"), v.sem("g_turned"), v.sem("g_sel_ready")
        dec_done, gates_out, stored, eg_done, dec_copied = v.sem("g_dec_done"), v.sem("g_gates_out"), v.sem("g_stored"), v.sem("g_eg_done"), v.sem("g_dec_copied")
        w_view = t["w_in"][0].rearrange("(k p) n -> p k n", p=P)
        NPG = DEC * PAGES

        block = scope.enter_context(nc.Block())

        @block.sync
        def _(sp):
            sp.dma_start(w_raw[:, :, 0:FH], w_view[:, :, C_FF:C_FF + FH]).then_inc(w_loaded, 16)
            sp.dma_start(w_raw[:, :, FH:], w_view[:, :, C_GA:C_GA + 2 * GH]).then_inc(w_loaded, 16)
            sp.wait_ge(bias_set, 1)
            sp.dma_start(bias[R_F:R_F + FH, :], t["b_forget"].rearrange("a h -> h a")).then_inc(b_loaded, 16)
            sp.dma_start(bias[R_A:R_A + GH, :], t["gdn_dt_bias"].rearrange("a h -> h a")).then_inc(b_loaded, 16)
            sp.dma_start(coef[R_A:R_A + GH, :], t["gdn_a_log"].rearrange("a h -> h a")).then_inc(b_loaded, 16)
            load_pages(sp, v, t, past, past_loaded, EARLY_PAGES, NPG)
            sp.wait_ge(run_ready, 1)
            sp.dma_start(v.gate_dram, run[:]).then_inc(stored, 16)
            sp.wait_ge(gates_out, 1)
            sp.dma_start(t["new_logf_prompt"][0, 0].rearrange("(c p) h -> p c h", p=P),
                         v.logf_n[:, 0:NBLK]).then_inc(stored, 16)
            sp.dma_start(t["new_logf_sample"][0].rearrange("b a h -> b (a h)"),
                         v.logf_n[0:DEC, NBLK]).then_inc(stored, 16)
            sp.wait_ge(stored, 48)

        @block.gpsimd
        def _(pool):
            pool.memset(bias[:], 0.0)
            pool.memset(coef[:], 0.0)
            pool.drain()
            pool.drain().then_inc(bias_set, 1)
            pool.memset(sign[:], -1.0)
            pool.memset(keep[:], 1.0)
            pool.memset(dsel[:], 0.0)
            pool.drain()
            pool.memset(sign[R_A:R_A + 32, :], 1.0)
            pool.drain()
            pool.memset(keep[R_A:R_A + 32, :].rearrange("p (c i) -> p c i", c=NBLK)[:, :, 0:1], 0.0)
            pool.drain()
            pool.memset(w_hi[:].bitcast(F32), 0.0)
            pool.memset(w_lo[:].bitcast(F32), 0.0)
            pool.drain()
            pool.drain().then_inc(prepared, 1)

        cols = [(0, FH, R_F), (FH, GH, R_A), (FH + GH, GH, R_B)]

        @block.scalar
        def _(act):
            act.wait_ge(w_loaded, 32)
            act.wait_ge(prepared, 1)
            for a, n, r in cols:
                ins = act.activation(w_hi[:, :, r:r + n], w_raw[:, :, a:a + n], ACT.Copy)
            ins.then_inc(split_hi, 1)
            act.wait_ge(y_ready, 1)
            act.activation(mag[:], y[:], ACT.Abs)
            act.drain()
            act.activation(mag[:], mag[:], ACT.Exp, scale=-1.0)
            act.wait_ge(b_loaded, 48)
            act.activation(coef[R_A:R_A + 32, :], coef[R_A:R_A + 32, :], ACT.Exp).then_inc(coef_ready, 1)
            act.drain()
            act.activation(mag[:], mag[:], ACT.Ln, bias=1.0).then_inc(mag_ready, 1)
            act.wait_ge(gate_ready, 1)
            act.activation(gate[R_B:R_B + 32, :], gate[R_B:R_B + 32, :], ACT.Exp).then_inc(beta_ready, 1)
            act.wait_ge(dec_copied, 1)
            act.activation(v.dec_gates[:, 0], v.dec_gates[:, 0], ACT.Exp).then_inc(eg_done, 1)
            act.wait_ge(eg_done, 1)

        @block.tensor
        def _(pe):
            pe.wait_ge(split_lo, 1)
            for g in range(NG):
                for k in range(KC):
                    mm = split_piece(pe, ps[0:GROWS, 3 + g, 0:GRP], w_hi[:, k], w_lo[:, k],
                                     v.hi[:, k, g * GRP:(g + 1) * GRP], v.lo[:, k, g * GRP:(g + 1) * GRP],
                                     k, k == 0, k == KC - 1)
            mm.then_inc(summed, 1)
            pe.wait_ge(past_loaded, 16 * NPG)
            past_flat = past[:].rearrange("p n h -> p (n h)")
            pe.matmul(ps[:, 0, 0:512], v.later[:], past_flat, start=True, stop=True)
            pe.matmul(ps[:, 1, 0:512], v.ones[:], past_flat, start=True, stop=True)
            pe.wait_ge(sel_ready, 1)
            pe.matmul(ps[:, 2, 0:P], v.ones[0:GROWS, :], dsel[:], start=True, stop=True).then_inc(dec_done, 1)
            for c in range(NBLK):
                pe.transpose(ps[:, 6 + c // 4, (c % 4) * GROWS:(c % 4 + 1) * GROWS], gate[:, c * P:(c + 1) * P],
                             v.ident[0:GROWS, 0:GROWS])
            pe.transpose(ps[0:DEC, 3, 0:GROWS], gate[:, SEQ:TOK], v.ident[0:GROWS, 0:GROWS])
            for c in range(NBLK):
                mm = pe.transpose(ps[:, 4 + c // 4, (c % 4) * GROWS:(c % 4 + 1) * GROWS], run[:, c * P:(c + 1) * P],
                                  v.ident[0:GROWS, 0:GROWS])
            mm.then_inc(turned, 1)

        @block.vector
        def _(dve):
            dve.wait_ge(split_hi, 1)
            for a, n, r in cols:
                ins = dve.tensor_tensor(w_lo[:, :, r:r + n], w_raw[:, :, a:a + n], w_hi[:, :, r:r + n].bitcast(F32), ALU.subtract)
            ins.then_inc(split_lo, 1)
            dve.wait_ge(summed, 1)
            dve.wait_ge(b_loaded, 48)
            for g in range(NG):
                ins = dve.tensor_scalar(y[:, g * GRP:(g + 1) * GRP], ps[0:GROWS, 3 + g, 0:GRP], bias[:], sign[:], ALU.add, ALU.mult)
            ins.then_inc(y_ready, 1)
            dve.wait_ge(coef_ready, 1)
            dve.tensor_scalar(coef[R_A:R_A + 32, :], coef[R_A:R_A + 32, :], -1.0, None, ALU.mult)
            dve.memset(coef[R_F:R_F + 32, :], -1.0)
            dve.memset(coef[R_B:R_B + 32, :], -1.0)
            dve.wait_ge(mag_ready, 1)
            dve.scalar_tensor_tensor(out=gate[:], in0=y[:], scalar=0.0, in1=mag[:], op0=ALU.max, op1=ALU.add)
            dve.drain()
            dve.tensor_scalar(gate[:], gate[:], coef[:], None, ALU.mult).then_inc(gate_ready, 1)
            dve.drain()
            dve.tensor_tensor_scan(run[0:64, :], keep[0:64, :], gate[0:64, 0:SEQ], 0.0, ALU.mult, ALU.add)
            dve.wait_ge(beta_ready, 1)
            dve.tensor_copy(run[R_B:R_B + 32, :], gate[R_B:R_B + 32, 0:SEQ])
            dve.drain()
            dve.tensor_scalar(run[R_F:R_F + 32, :], run[R_F:R_F + 32, :], -1.0 / SCALE, None, ALU.mult).then_inc(run_ready, 1)
            for r, n in ((R_F, FH), (R_A, GH), (R_B, GH)):
                g_row = gate[r:r + n, SEQ:TOK]
                if r == R_F:
                    out = dsel[r:r + n, 0:64].rearrange("p (b h) -> p b h", b=DEC)
                    a = g_row.unsqueeze(2).broadcast_to([n, DEC, n])
                    b = v.ident[r:r + n, r:r + n].unsqueeze(1).broadcast_to([n, DEC, n])
                else:
                    at = 64 if r == R_A else 96
                    out = dsel[r:r + n, at:at + 32].rearrange("p (h b) -> p h b", h=GH)
                    a = g_row.unsqueeze(1).broadcast_to([n, GH, DEC])
                    b = v.ident[r:r + n, r:r + n].unsqueeze(2).broadcast_to([n, GH, DEC])
                ins = dve.tensor_tensor(out, a, b, ALU.mult)
            ins.then_inc(sel_ready, 1)
            dve.wait_ge(dec_done, 1)
            dve.tensor_copy(v.dec_gates[:].rearrange("p n h b -> p (n h b)"), ps[:, 2, 64:128]).then_inc(dec_copied, 1)
            dve.tensor_copy(total[:].rearrange("p b h -> p (b h)"), ps[:, 2, 0:64])
            within = ps[:, 0].rearrange("p (b g h) -> p b g h", b=DEC, g=PAGES)
            whole = ps[:, 1].rearrange("p (b g h) -> p b g h", b=DEC, g=PAGES)
            bias_v = v.dec_bias[:].rearrange("p (b g) h -> p b g h", b=DEC)
            for pg in reversed(range(PAGES)):
                dve.drain()
                dve.tensor_tensor(bias_v[:, :, pg, :], total[:], within[:, :, pg, :], ALU.add)
                if pg:
                    dve.drain()
                    dve.tensor_tensor(total[:], total[:], whole[:, :, pg, :], ALU.add)
            dve.wait_ge(turned, 1)
            for half in range(2):
                rows_n = ps[:, 6 + half, 0:4 * GROWS].rearrange("p (c r) -> p c r", c=4)
                dve.tensor_copy(v.logf_n[:, 4 * half:4 * half + 4, :], rows_n[:, :, R_F:R_F + FH])
                dve.tensor_copy(v.beta_n[:, 4 * half:4 * half + 4, :], rows_n[:, :, R_B:R_B + GH])
                dve.tensor_copy(v.gcum_n[:, 4 * half:4 * half + 4, :],
                                ps[:, 4 + half, 0:4 * GROWS].rearrange("p (c r) -> p c r", c=4)[:, :, R_A:R_A + GH])
            dve.tensor_copy(v.logf_n[0:DEC, NBLK, :], ps[0:DEC, 3, R_F:R_F + FH]).then_inc(gates_out, 1)


class Count:

    def __init__(self, sem, per, credit=0):
        self.sem, self.per, self.credit = sem, per, credit

    def at(self, j, n):
        return j * self.per + (n + self.credit)


def mixer(nc, t, v):
    with ExitStack() as scope:
        def sb(name, shape, dt=F32):
            return v.sb(name, shape, dt, scope)

        ps = v.ps
        w_raw = sb("wm_raw", [P, 2, KC, P])
        w_hi = sb("wm_hi", [P, 2, KC, P], F32R)
        w_lo = sb("wm_lo", [P, 2, KC, P], F32R)
        qT, kT, vT = sb("qT", [P, TOK]), sb("kT", [P, TOK]), sb("vT", [P, TOK])
        ext = sb("gdn_ext", [P, 3, EXT])
        z_silu = sb("z_silu", [P, TOK])
        mix = sb("mix", [P, TOK])
        small = sb("mix_small", [P, 640])
        region = sb("region", [P, 16544])
        at = [0]

        def view(width):
            at[0] += width
            assert at[0] <= 16544
            return region[:, at[0] - width:at[0]]

        def blocks(ap):
            return ap.rearrange("p (c i) -> p c i", i=P)

        def halves(ap, level):
            return ap.rearrange("p (n h w) -> p n h w", h=2, w=1 << level)

        k_nat, v_nat = blocks(view(SEQ)), blocks(view(SEQ))
        q_wide = blocks(z_silu[:, 0:SEQ])
        ck_row = view(2 * SEQ).rearrange("p (h s) -> p h s", h=2)
        ck_diag = view(2 * SEQ).rearrange("p (h s) -> p h s", h=2)
        prob = view(2 * SEQ).rearrange("p (u s) -> p u s", u=2)
        probT = view(2 * SEQ).rearrange("p (u c i) -> p u c i", u=2, i=P)
        o_nat = k_nat
        v_past = view(4 * SEQ).rearrange("p (b g d) -> p b g d", b=4, d=P)
        k_past = view(2 * SEQ).rearrange("p (b g d) -> p b g d", b=2, d=P)
        at[0] = 0
        conv = view(3 * CONV).rearrange("p (y e) -> p y e", y=3)
        rs_qk = view(2 * CONV).rearrange("p (y e) -> p y e", y=2)
        slots = [view(SEQ) for _ in range(11)]
        decayT, k_dec, k_beta, v_beta, aT, qkT, gc_row, beta_row, eg_row, k_scaled, s_dec = slots
        squares = region[:, 5 * CONV:7 * CONV].rearrange("p (y e) -> p y e", y=2)
        levelT = [blocks(decayT), blocks(gc_row)]
        inv, invT, z_mat = blocks(k_scaled), blocks(beta_row), blocks(eg_row)
        wT = blocks(conv[:, 1, 0:SEQ])
        oT = rs_qk[:, 1, 0:TOK]
        o_sq, o_rstd = region[:, 5 * CONV:5 * CONV + TOK], region[:, 5 * CONV + 2 * SEQ:5 * CONV + 2 * SEQ + TOK]
        state = sb("state", [P, GD])
        v_new = sb("v_new", [P, 2, GD])

        off = [0]

        def sm(n):
            off[0] += n
            assert off[0] <= 640
            return small[:, off[0] - n:off[0]]

        kv_dec = sb("kv_dec", [DEC, 2, P])
        neg_max, row_sum, row_inv, max_part = sm(16), sm(16), sm(16), sm(16)
        bias_j = sm(2 * DEC * PAGES).rearrange("p (b g h) -> p b g h", b=DEC, g=PAGES)
        score = sm(2 * 64).rearrange("p (b g h) -> p b g h", b=DEC, g=PAGES)
        d_max, d_all, d_self, d_pself, d_den = (sm(2 * DEC).rearrange("p (b h) -> p b h", b=DEC) for _ in range(5))
        qk_self = sm(DEC)
        conv_j = sm(3 * 28).rearrange("p (y n) -> p y n", y=3)
        gs = sm(7 * NBLK).rearrange("p (n c) -> p n c", n=7)
        BETA, GCUM, GLAST, EG, KB, KD, EGL = range(7)
        dg = sm(2 * DEC).rearrange("p (n b) -> p n b", n=2)
        kq = sm(2 * DEC).rearrange("p (b n) -> p b n", n=2)
        kq_dot, kq_prod, delta, d_tmp = sm(DEC), sm(DEC), sm(DEC), sm(DEC)
        tail = sb("conv_tail", [P, 3, TAPS - 1 + DEC])
        tail_rows = sb("conv_tail_rows", [TAPS - 1 + DEC, 3, P])
        nat_dec = v_beta[0:DEC, 0:2 * P].rearrange("p (n d) -> p n d", n=2)
        delta_diag = blocks(k_beta[0:DEC, :])

        C = {}

        def count(name, per, credit=0):
            C[name] = Count(v.mixer_sem("m_" + name), per, credit)
            return C[name]

        w_loaded = [count("w_loaded0", 64), count("w_loaded1", 48)]
        w_split_hi, w_split_lo = count("w_split_hi", NTILE), count("w_split_lo", NTILE, 2)
        piece_done, piece_out = count("piece_done", 3 * NTILE, 6), count("piece_out", 3 * NTILE, 2)
        nat_turned, nat_out, dg_ready = count("nat_turned", 1), count("nat_out", 1), count("dg_ready", 1)
        ck_loaded = count("ck_loaded", 16)
        qk_done, scored, expd = count("qk_done", 16), count("scored", 16), count("expd", 16)
        p_turned, p_out_a, p_out_b = count("p_turned", 16), count("p_out_a", 16), count("p_out_b", 8)
        pv_done, pv_out = count("pv_done", 16), count("pv_out", 16)
        o_turned, mix_ready = count("o_turned", 1), count("mix_ready", 1)
        nat_stored = count("nat_stored", 16 * 4)
        k_loaded = [count("kpast_loaded0", 128 * 4), count("kpast_loaded1", 128 * 4)]
        v_loaded = count("vpast_loaded", 512 * 2)
        k_used = count("kpast_used", 8)
        self_ready, self_done, q_wide_done, q_wide_out = count("self_ready", 1), count("self_done", 1), count("q_wide_done", 1), count("q_wide_out", 1)
        dmax_ready, dmax_all, dsub_ready, dexp = count("dmax_ready", 2), count("dmax_all", 2), count("dsub_ready", 2), count("dexp", 2)
        dself_out, dpv_done, dec_out = count("dself_out", 1), count("dpv_done", 2), count("dec_out", 2)
        mix_stored = count("mix_stored", 32, 16)
        rows_loaded, s_loaded = count("rows_loaded", 32), count("s_loaded", 16)
        g_ready, conv_done, conv_silu = count("g_ready", 1), count("conv_done", 3), count("conv_silu", 3)
        tail_ready, tail_turned, tail_out = count("tail_ready", 1), count("tail_turned", 1), count("tail_out", 1)
        tail_stored = count("tail_stored", 32, 16)
        sq_ready, l2_done, l2_rstd, l2_out = count("sq_ready", 1), count("l2_done", 1), count("l2_rstd", 1), count("l2_out", 1)
        dif_ready, dec_exp, dec_masked, eg_row_ready = count("dif_ready", 1), count("dec_exp", 1), count("dec_masked", 1), count("eg_row_ready", 1)
        gs_exp = count("gs_exp", 1)
        gnat_turned, gnat_out, kk_done, a_ready = count("gnat_turned", 1), count("gnat_out", 1), count("kk_done", 1), count("a_ready", 1)
        gqk_done, q_ready = count("gqk_done", 1), count("q_ready", 1)
        level_ready, y0_ready, y0_turned, x0_ready = count("level_ready", 7), count("y0_ready", 1), count("y0_turned", 1), count("x0_ready", 1)
        z_done, z_out, xy_done, xy_out = count("z_done", 12), count("z_out", 12), count("xy_done", 12), count("xy_out", 12)
        w_done, w_out_ = count("wT_done", 1), count("wT_out", 1)
        state_zero = count("state_zero", 1)
        vn_done, vn_out = count("vn_done", NBLK), count("vn_out", NBLK)
        oc_done, oc_out, sc_done, sc_out = count("oc_done", NBLK), count("oc_out", NBLK), count("sc_done", NBLK), count("sc_out", NBLK)
        kq_ready, sdec_done, delta_ready, rows_turned = count("kq_ready", 1), count("sdec_done", 1), count("delta_ready", 1), count("rows_turned", 1)
        diag_ready, outer_done, sdec_ready = count("diag_ready", 1), count("outer_done", 1), count("sdec_ready", 1, 1)
        osq_ready, osum_done, orstd_ready, o_ready = count("osq_ready", 1), count("osum_done", 1), count("orstd_ready", 1, 1), count("o_ready", 1)
        state_stored = count("state_stored", 32, 16)
        ctx_copied = v.mixer_sem("ctx_copied")
        credits = {"pe": (piece_done,), "act": (piece_out, orstd_ready), "pool": (w_split_lo,),
                   "dve": (mix_stored, tail_stored, state_stored, sdec_ready)}

        def give_credits(eng, name):
            for c in credits[name]:
                eng.sem_inc(c.sem, c.credit)

        def wait(eng, c, j, n=None, ahead=0):
            eng.wait_ge(c.sem, c.at(j, (c.per if n is None else n) + ahead * c.per))

        def each_step(eng, step):
            with eng.Fori(0, STEPS - 1) as j:
                step(j, False)
            step(STEPS - 1, True)

        passed = {e: v.mixer_sem("m_passed_" + e) for e in ("dve", "pool", "sp")}

        def settle(eng, name):
            eng.sem_inc(passed[name], 1)

        FOX_PIECES = 3 * NG
        PIECE_AT = (-1, 0, 1, 3, 5, 7, 9, 11, 13)
        DEC_SCORE_AT = (2, 3, 5, 7, 11, 12, 14)
        DEC_PV_AT = 10
        w_view = t["w_in"][0].rearrange("(k p) n -> p k n", p=P)
        NP_ = t["cache_k"].shape[1]
        before = [0] + [i - 1 for i in range(1, NTILE)]
        piece_before = [0] + [q - 1 for q in range(1, 3 * NTILE)]

        block = scope.enter_context(nc.Block())

        @block.sync
        def _(sp):
            sp.dma_start(t["new_gdn_conv_sample"][0, :, 0:2, :], t["state_gdn_conv"][0, :, 1:3, :]).then_inc(ctx_copied, 16)

            def load_past(j, dst, cache, b, loaded, pages):
                for g, page in enumerate(pages):
                    sp.dma_start(dst[:, b, g], cache[0, ds(page, 1)].rearrange("a p h d -> p (a h d)")[:, ds(j * P, P)]).then_inc(loaded.sem, 16)

            def pages(b):
                settle(sp, "sp")
                return [sp.value_load(v.page_ids[0:1, b * PAGES + g:b * PAGES + g + 1], min_val=0, max_val=NP_ - 1)
                        for g in range(PAGES)]

            def load_k(j, b, ids):
                load_past(j, k_past, t["cache_k"], b % 2, k_loaded[b % 2], ids)

            def load_v(j, b, ids):
                load_past(j, v_past, t["cache_v"], b % 4, v_loaded, ids)

            def load_first(j, b):
                if b == 0:
                    sp.dma_start(ck_row, v.gate_dram[ds(R_F + 2 * j, 2), :].unsqueeze(0).broadcast_to([P, 2, SEQ])).then_inc(ck_loaded.sem, 16)
                ids = pages(b)
                load_k(j, b, ids)
                load_v(j, b, ids)

            for b in range(2):
                load_first(0, b)

            def step(j, last):
                def k_free(b):
                    wait(sp, k_used, j, b - 1)

                wait(sp, nat_out, j)
                settle(sp, "sp")
                kp, vp = (t[n][0, 0].rearrange("(c p) h d -> p c (h d)", p=P) for n in ("new_k_prompt", "new_v_prompt"))
                ks, vs = (t[n][0].rearrange("b a h d -> b (a h d)") for n in ("new_k_sample", "new_v_sample"))
                sp.dma_start(kp[:, :, ds(j * P, P)], k_nat).then_inc(nat_stored.sem, 16)
                sp.dma_start(vp[:, :, ds(j * P, P)], v_nat).then_inc(nat_stored.sem, 16)
                sp.dma_start(ks[:, ds(j * P, P)], kv_dec[:, 0]).then_inc(nat_stored.sem, 16)
                sp.dma_start(vs[:, ds(j * P, P)], kv_dec[:, 1]).then_inc(nat_stored.sem, 16)
                for b in range(2, DEC):
                    k_free(b)
                    ids = pages(b)
                    load_k(j, b, ids)
                    if b == 4:
                        wait(sp, dpv_done, j, 1)
                        settle(sp, "sp")
                    load_v(j, b, ids)
                wait(sp, mix_ready, j)
                settle(sp, "sp")
                wait(sp, dec_out, j)
                sp.dma_start(gc_row, v.gate_dram[ds(R_A + j, 1), :].broadcast_to([P, SEQ])).then_inc(rows_loaded.sem, 16)
                sp.dma_start(beta_row, v.gate_dram[ds(R_B + j, 1), :].broadcast_to([P, SEQ])).then_inc(rows_loaded.sem, 16)
                sp.dma_start(blocks(s_dec), t["state_gdn"][0, :, ds(j, 1)].rearrange("b a k e -> k (b a) e")).then_inc(s_loaded.sem, 16)
                sp.dma_start(v.mix_dram[ds(j, 1)].rearrange("a p n -> p (a n)"), mix[:]).then_inc(mix_stored.sem, 16)
                wait(sp, tail_out, j)
                tp = t["new_gdn_conv_prompt"][0, 0].rearrange("i (y n) -> i y n", y=3)
                ts = t["new_gdn_conv_sample"][0, :, TAPS - 2, :].rearrange("b (y n) -> b y n", y=3)
                sp.dma_start(tp[:, :, ds(j * P, P)], tail_rows[0:3]).then_inc(tail_stored.sem, 16)
                sp.dma_start(ts[:, :, ds(j * P, P)], tail_rows[3:3 + DEC]).then_inc(tail_stored.sem, 16)
                wait(sp, sc_out, j)
                sp.dma_start(t["new_gdn_prompt"][0, 0, ds(j, 1)].rearrange("a k e -> k (a e)"), state[:]).then_inc(state_stored.sem, 16)
                wait(sp, sdec_ready, j)
                sp.dma_start(t["new_gdn_sample"][0, :, ds(j, 1)].rearrange("b a k e -> k (b a) e"), blocks(s_dec)).then_inc(state_stored.sem, 16)
                if not last:
                    settle(sp, "sp")
                    load_first(j + 1, 0)
                if not last:
                    wait(sp, state_stored, j)
                    load_first(j + 1, 1)

            each_step(sp, step)
            sp.wait_ge(ctx_copied, 16)

        @block.tensor
        def _(pe):
            give_credits(pe, "pe")

            def project(j, q, ahead=0):
                i, g = q // NG, q % NG
                if g == 0:
                    wait(pe, w_split_lo, j, i + 1, ahead)
                wait(pe, piece_out, j, piece_before[q], ahead)
                out = ps[:, q % 2, 0:GRP]
                for k in range(KC):
                    mm = split_piece(pe, out, w_hi[:, i % 2, k], w_lo[:, i % 2, k],
                                     v.hi[:, k, g * GRP:(g + 1) * GRP], v.lo[:, k, g * GRP:(g + 1) * GRP],
                                     k, k == 0, k == KC - 1)
                mm.then_inc(piece_done.sem, 1)

            for q in range(FOX_PIECES):
                project(0, q)

            def step(j, last):
                def project_next(q):
                    if not last:
                        project(j, q, 1)

                wait(pe, piece_out, j, 9)
                wait(pe, sdec_ready, j, 0)
                for b in range(DEC):
                    mm = pe.matmul(ps[:, b // 4, (b % 4) * P:(b % 4 + 1) * P], qT[:, SEQ + b:SEQ + b + 1].broadcast_to([P, P]), v.ident[:], start=True, stop=True)
                mm.then_inc(q_wide_done.sem, 1)
                wait(pe, self_ready, j)
                for h in range(2):
                    mm = pe.matmul(ps[:, 2, DEC * h:DEC * (h + 1)], v.head_ones[:, h], qk_self, start=True, stop=True)
                mm.then_inc(self_done.sem, 1)
                wait(pe, orstd_ready, j, 0)
                for src, bank in ((kT, 3), (vT, 5)):
                    for c in range(NBLK):
                        pe.transpose(ps[:, bank + c // 4, (c % 4) * P:(c % 4 + 1) * P], src[:, c * P:(c + 1) * P], v.ident[:])
                pe.transpose(ps[0:DEC, 7, 0:P], kT[:, SEQ:TOK], v.ident[:])
                pe.transpose(ps[0:DEC, 7, P:2 * P], vT[:, SEQ:TOK], v.ident[:]).then_inc(nat_turned.sem, 1)
                wait(pe, nat_out, j)

                def scores(u):
                    h, i = u // NBLK, u % NBLK
                    if u:
                        wait(pe, scored, j, u)
                    rows = slice(h * FD, (h + 1) * FD)
                    n = (i + 1) * P
                    for a in range(0, n, 512):
                        b = min(n, a + 512)
                        mm = pe.matmul(ps[:, 3 + a // 512, 0:b - a], qT[rows, i * P:(i + 1) * P], kT[rows, a:b], start=True, stop=True)
                    mm.then_inc(qk_done.sem, 1)

                def turn_probs(u):
                    i = u % NBLK
                    wait(pe, expd, j, u + 1)
                    if u:
                        wait(pe, p_out_a, j, u)
                        if (u - 1) % NBLK >= 4:
                            wait(pe, p_out_b, j, 4 * ((u - 1) // NBLK) + (u - 1) % NBLK - 3)
                    for c in range(i + 1):
                        mm = pe.transpose(ps[:, 5 + c // 4, (c % 4) * P:(c % 4 + 1) * P], prob[:, u % 2, c * P:(c + 1) * P], v.ident[:])
                    mm.then_inc(p_turned.sem, 1)

                def weigh_values(u):
                    h, i = u // NBLK, u % NBLK
                    wait(pe, p_out_a, j, u + 1)
                    if i >= 4:
                        wait(pe, p_out_b, j, 4 * h + i - 3)
                    if u:
                        wait(pe, pv_out, j, u)
                    for c in range(i + 1):
                        mm = pe.matmul(ps[:, 7, 0:FD], probT[:, u % 2, c], v_nat[:, c, h * FD:(h + 1) * FD],
                                       start=(c == 0), stop=(c == i))
                    mm.then_inc(pv_done.sem, 1)

                def dec_values(half):
                    wait(pe, dexp, j, half + 1)
                    wait(pe, v_loaded, j, 512 * (half + 1))
                    if half:
                        wait(pe, dec_out, j, half)
                    else:
                        wait(pe, dself_out, j)
                    r = slice(4 * half, 4 * half + 4)
                    pe.matmul(ps[:, 2, 0:64], v.ones[:], score[:, r].rearrange("p b g h -> p (b g h)"), start=True, stop=True)
                    for b in range(4):
                        for g in range(PAGES):
                            mm = pe.matmul(ps[:, 2, 64 + 2 * b:66 + 2 * b], v_past[:, b, g], score[:, 4 * half + b, g], start=(g == 0), stop=(g == PAGES - 1))
                    mm.then_inc(dpv_done.sem, 1)

                for u in range(-1, 2 * NBLK + 1):
                    if u + 1 < 2 * NBLK:
                        scores(u + 1)
                    if u in PIECE_AT:
                        if u == PIECE_AT[0]:
                            wait(pe, q_wide_out, j)
                        project(j, FOX_PIECES + PIECE_AT.index(u))
                    if 0 <= u < 2 * NBLK:
                        turn_probs(u)
                    if u >= 1:
                        weigh_values(u - 1)
                    if u == DEC_PV_AT:
                        dec_values(0)
                wait(pe, pv_out, j)
                for c in range(NBLK):
                    mm = pe.transpose(ps[:, 3 + c // 4, (c % 4) * P:(c % 4 + 1) * P], o_nat[:, c], v.ident[:])
                mm.then_inc(o_turned.sem, 1)
                project(j, 18)
                dec_values(1)
                wait(pe, tail_ready, j)
                for y in range(3):
                    mm = pe.transpose(ps[0:TAPS - 1 + DEC, 7, y * P:(y + 1) * P], tail[:, y], v.ident[:])
                mm.then_inc(tail_turned.sem, 1)
                project(j, 19)
                project(j, 20)
                wait(pe, tail_out, j)
                wait(pe, dec_out, j)
                wait(pe, sq_ready, j)
                for y in range(2):
                    for g, (a, w) in enumerate(groups(CONV, 3)):
                        mm = pe.matmul(ps[:, 2 + 3 * y + g, 0:w], v.ones[:], squares[:, y, a:a + w], start=True, stop=True)
                mm.then_inc(l2_done.sem, 1)
                project_next(0)
                project_next(1)
                wait(pe, l2_out, j)
                for y, bank in ((1, 2), (2, 4)):
                    for c in range(NBLK):
                        mm = pe.transpose(ps[:, bank + c // 4, (c % 4) * P:(c % 4 + 1) * P], conv[:, y, c * P:(c + 1) * P], v.ident[:])
                mm.then_inc(gnat_turned.sem, 1)
                qn, kn = blocks(conv[:, 0, 0:SEQ]), blocks(conv[:, 1, 0:SEQ])

                def per_chunk(bank, lhs, rhs):
                    for c in range(NBLK):
                        mm = pe.matmul(ps[:, bank + c // 4, (c % 4) * P:(c % 4 + 1) * P], lhs[:, c], rhs[:, c], start=True, stop=True)
                    return mm

                per_chunk(6, kn, blocks(k_scaled)).then_inc(kk_done.sem, 1)
                project_next(2)
                wait(pe, gnat_out, j)
                per_chunk(2, kn, qn).then_inc(gqk_done.sem, 1)
                project_next(3)
                wait(pe, y0_ready, j)
                for c in range(NBLK):
                    mm = pe.transpose(ps[:, 4 + c // 4, (c % 4) * P:(c % 4 + 1) * P], invT[:, c], v.ident[:])
                mm.then_inc(y0_turned.sem, 1)
                wait(pe, x0_ready, j)
                wait(pe, q_ready, j)
                for l in range(1, 7):
                    for hf in range(2):
                        n = 2 * (l - 1) + hf
                        wait(pe, level_ready, j, l + 1)
                        if l > 1:
                            wait(pe, xy_out, j, n - 1)
                        for c in range(4 * hf, 4 * hf + 4):
                            mm = pe.matmul(ps[:, 2 + hf, (c % 4) * P:(c % 4 + 1) * P], levelT[l % 2][:, c], inv[:, c], start=True, stop=True)
                        mm.then_inc(z_done.sem, 1)
                    if l in (2, 4):
                        project_next(3 + l // 2)
                    for hf in range(2):
                        n = 2 * (l - 1) + hf
                        wait(pe, z_out, j, n + 1)
                        if l < 6:
                            for c in range(4 * hf, 4 * hf + 4):
                                pe.matmul(ps[:, 4 + hf, (c % 4) * P // 2:(c % 4 + 1) * P // 2], invT[:, c], halves(z_mat[:, c], l)[:, :, 0], start=True, stop=True)
                        for c in range(4 * hf, 4 * hf + 4):
                            mm = pe.matmul(ps[:, 6 + hf, (c % 4) * P // 2:(c % 4 + 1) * P // 2], z_mat[:, c], halves(invT[:, c], l)[:, :, 1], start=True, stop=True)
                        mm.then_inc(xy_done.sem, 1)
                wait(pe, xy_out, j)
                per_chunk(2, blocks(k_beta), invT).then_inc(w_done.sem, 1)
                wait(pe, w_out_, j)
                wait(pe, state_zero, j)
                qd = qn
                for c in range(NBLK):
                    if c:
                        wait(pe, vn_out, j, c)
                    pe.matmul(ps[:, 4, 0:GD], invT[:, c], blocks(v_beta)[:, c], start=True, stop=False)
                    if c:
                        wait(pe, sc_out, j, c)
                    pe.matmul(ps[:, 4, 0:GD], wT[:, c], state[:], start=False, stop=True).then_inc(vn_done.sem, 1)
                    if c >= 2:
                        wait(pe, oc_out, j, c - 1)
                    pe.matmul(ps[:, 6 + c % 2, 0:P], state[:], qd[:, c], start=True, stop=False)
                    wait(pe, vn_out, j, c + 1)
                    pe.matmul(ps[:, 2 + c % 2, 0:GD], blocks(k_dec)[:, c], v_new[:, c % 2], start=True, stop=True).then_inc(sc_done.sem, 1)
                    pe.matmul(ps[:, 6 + c % 2, 0:P], v_new[:, c % 2], blocks(qkT)[:, c], start=False, stop=True).then_inc(oc_done.sem, 1)
                    if c == 3:
                        project_next(6)
                wait(pe, kq_ready, j)
                wait(pe, vn_out, j)
                wait(pe, sc_out, j)
                for b in range(DEC):
                    pe.matmul(ps[:, 4, 2 * b:2 * b + 2], blocks(s_dec)[:, b], kq[:, b], start=True, stop=True)
                pe.matmul(ps[:, 5, 0:DEC], v.ones[:], kq_prod, start=True, stop=True).then_inc(sdec_done.sem, 1)
                project_next(7)
                wait(pe, delta_ready, j)
                pe.transpose(ps[0:DEC, 4, 0:P], kq[:, :, 0], v.ident[:])
                pe.transpose(ps[0:DEC, 4, P:2 * P], delta, v.ident[:]).then_inc(rows_turned.sem, 1)
                wait(pe, diag_ready, j)
                for hf in range(2):
                    mm = pe.matmul(ps[:, 2 + hf, 0:512], nat_dec[:, 0], delta_diag[:, 4 * hf:4 * hf + 4].rearrange("q b e -> q (b e)"), start=True, stop=True)
                mm.then_inc(outer_done.sem, 1)
                wait(pe, osq_ready, j)
                for g in range(NG):
                    mm = pe.matmul(ps[:, 5 + g, 0:GRP], v.ones[:], o_sq[:, g * GRP:(g + 1) * GRP], start=True, stop=True)
                mm.then_inc(osum_done.sem, 1)
                project_next(8)

            each_step(pe, step)

        @block.scalar
        def _(act):
            give_credits(act, "act")

            def load(j, i, ahead=0):
                act.dma_start(w_raw[:, i % 2], w_view[:, :, ds((j + ahead) * P + TILE_COL[i], P)]).then_inc(w_loaded[i % 2].sem, 16)

            def split(j, i, ahead=0):
                wait(act, w_loaded[i % 2], j, 16 * (i // 2 + 1), ahead)
                wait(act, piece_done, j, 3 * before[i], ahead)
                act.activation(w_hi[:, i % 2], w_raw[:, i % 2], ACT.Copy).then_inc(w_split_hi.sem, 1)

            def evacuate(j, q, ahead=0, last=False):
                i, g = q // NG, q % NG
                wait(act, piece_done, j, q + 1, ahead)
                src, a = ps[:, q % 2, 0:GRP], g * GRP
                if 3 <= i < 6:
                    n = min(GRP, SEQ - a)
                    ins = act.activation(ext[:, i - 3, TAPS - 1 + a:TAPS - 1 + a + n], src[:, 0:n], ACT.Copy)
                    if n < GRP:
                        new = ext[:, i - 3, TAPS - 1 + SEQ:].rearrange("p (b i) -> p b i", b=DEC)[:, :, TAPS - 1]
                        ins = act.activation(new, src[:, n:GRP], ACT.Copy)
                    ins.then_inc(piece_out.sem, 1)
                else:
                    act.activation({0: qT, 1: kT, 2: vT, 6: z_silu}[i][:, a:a + GRP], src, ACT.Copy).then_inc(piece_out.sem, 1)
                if g == 0 and (i + 2 < NTILE or not last):
                    wait(act, w_split_lo, j, i + 1, ahead)
                    if i + 2 < NTILE:
                        load(j, i + 2, ahead)
                    else:
                        load(j, {5: 1, 6: 0}[i], ahead + 1)
                if g == NG - 1 and i + 2 < NTILE:
                    split(j, i + 2, ahead)
                if q == 3 * NTILE - 1 and not last:
                    split(j, 0, ahead + 1)
                    split(j, 1, ahead + 1)

            load(0, 0)
            load(0, 1)
            split(0, 0)
            split(0, 1)
            for q in range(FOX_PIECES):
                evacuate(0, q)

            def step(j, last):
                def evacuate_next(q):
                    if not last:
                        evacuate(j, q, 1)

                wait(act, q_wide_done, j)
                for hf in range(2):
                    ins = act.activation(q_wide[:, 4 * hf:4 * hf + 4], ps[:, hf].rearrange("p (c i) -> p c i", c=4), ACT.Copy)
                ins.then_inc(q_wide_out.sem, 1)

                def exp_scores(u):
                    wait(act, scored, j, u + 1)
                    p = prob[:, u % 2, 0:(u % NBLK + 1) * P]
                    act.activation(p, p, ACT.Exp, bias=neg_max[:, u:u + 1], scale=-1.0,
                                   accum_out=row_sum[:, u:u + 1]).then_inc(expd.sem, 1)

                def probs_out(u):
                    n = min(4, u % NBLK + 1)
                    wait(act, p_turned, j, u + 1)
                    if u >= 2:
                        wait(act, pv_done, j, u - 1)
                    act.activation(probT[:, u % 2, 0:n], ps[:, 5, 0:n * P].rearrange("p (c i) -> p c i", c=n), ACT.Copy).then_inc(p_out_a.sem, 1)

                def exp_decode(half):
                    r = slice(4 * half, 4 * half + 4)
                    wait(act, dsub_ready, j, half + 1)
                    act.activation(score[:, r], score[:, r], ACT.Exp)
                    act.activation(d_pself[:, r], d_self[:, r], ACT.Exp).then_inc(dexp.sem, 1)

                for u in range(-1, 2 * NBLK):
                    if u + 1 < 2 * NBLK:
                        exp_scores(u + 1)
                    if u in PIECE_AT:
                        evacuate(j, FOX_PIECES + PIECE_AT.index(u), 0, last)
                    if u >= 0:
                        probs_out(u)
                    if u == DEC_PV_AT - 1:
                        exp_decode(0)
                wait(act, k_used, j)
                evacuate(j, 18, 0, last)
                exp_decode(1)
                for y in range(3):
                    wait(act, conv_done, j, y + 1)
                    act.activation(conv[:, y], conv[:, y], ACT.Silu).then_inc(conv_silu.sem, 1)
                    if y < 2:
                        evacuate(j, 19 + y, 0, last)
                    act.drain()
                act.activation(z_silu[:], z_silu[:], ACT.Silu)
                act.activation(squares[:, 0], conv[:, 0], ACT.Square)
                act.activation(squares[:, 1], conv[:, 1], ACT.Square).then_inc(sq_ready.sem, 1)
                wait(act, l2_done, j)
                for y in range(2):
                    for g, (a, w) in enumerate(groups(CONV, 3)):
                        act.activation(rs_qk[:, y, a:a + w], ps[:, 2 + 3 * y + g, 0:w], ACT.Ln, bias=EPS)
                act.drain()
                act.activation(rs_qk[:, 0], rs_qk[:, 0], ACT.Exp, scale=-0.5, bias=LN_GSCALE)
                act.activation(rs_qk[:, 1], rs_qk[:, 1], ACT.Exp, scale=-0.5).then_inc(l2_rstd.sem, 1)
                wait(act, rows_loaded, j)
                act.activation(eg_row, gc_row, ACT.Exp).then_inc(eg_row_ready.sem, 1)
                evacuate_next(0)
                wait(act, g_ready, j)
                act.activation(gs[:, EG], gs[:, GCUM], ACT.Exp)
                act.activation(gs[:, KD], gs[:, KD], ACT.Exp)
                act.activation(gs[:, EGL], gs[:, GLAST], ACT.Exp).then_inc(gs_exp.sem, 1)
                evacuate_next(1)
                wait(act, dif_ready, j)
                act.activation(decayT, decayT, ACT.Exp).then_inc(dec_exp.sem, 1)
                evacuate_next(2)
                evacuate_next(3)
                for n in range(12):
                    hf = n % 2
                    wait(act, z_done, j, n + 1)
                    if n >= 2:
                        wait(act, xy_done, j, n - 1)
                    act.activation(z_mat[:, 4 * hf:4 * hf + 4], ps[:, 2 + hf].rearrange("p (c i) -> p c i", c=4), ACT.Copy).then_inc(z_out.sem, 1)
                    if n in (3, 7):
                        evacuate_next(4 + n // 4)
                for c in range(NBLK):
                    wait(act, vn_done, j, c + 1)
                    if c >= 2:
                        wait(act, oc_done, j, c - 1)
                    act.activation(v_new[:, c % 2], ps[:, 4, 0:GD], ACT.Copy).then_inc(vn_out.sem, 1)
                    wait(act, oc_done, j, c + 1)
                    act.activation(oT[:, c * P:(c + 1) * P], ps[:, 6 + c % 2, 0:P], ACT.Copy).then_inc(oc_out.sem, 1)
                    if c == 3:
                        evacuate_next(6)
                evacuate_next(7)
                act.drain()
                wait(act, delta_ready, j)
                act.activation(o_sq, oT, ACT.Square).then_inc(osq_ready.sem, 1)
                wait(act, osum_done, j)
                for g in range(NG):
                    act.activation(o_rstd[:, g * GRP:(g + 1) * GRP], ps[:, 5 + g, 0:GRP], ACT.Ln, scale=1.0 / GD, bias=EPS)
                act.drain()
                act.activation(o_rstd, o_rstd, ACT.Exp, scale=-0.5).then_inc(orstd_ready.sem, 1)
                evacuate_next(8)
                wait(act, o_ready, j)
                act.dma_start(v.mix_dram[ds(GH + j, 1)].rearrange("a p n -> p (a n)"), oT).then_inc(mix_stored.sem, 16)

            each_step(act, step)

        @block.gpsimd
        def _(pool):
            give_credits(pool, "pool")
            pool.memset(ext[:, :, 0:TAPS - 1], 0.0)
            pool.drain()

            def split(j, i, ahead=0):
                wait(pool, w_split_hi, j, i + 1, ahead)
                pool.tensor_tensor(w_lo[:, i % 2], w_raw[:, i % 2], w_hi[:, i % 2].bitcast(F32), ALU.subtract).then_inc(w_split_lo.sem, 1)

            for i in range(5):
                split(0, i)

            def step(j, last):
                def split_next(i):
                    if not last:
                        split(j, i, 1)

                split(j, 5)
                for half in range(2):
                    r = slice(4 * half, 4 * half + 4)
                    wait(pool, dmax_ready, j, half + 1)
                    settle(pool, "pool")
                    pool.partition_all_reduce(d_all[:, r].rearrange("p b h -> p (b h)"), d_max[:, r].rearrange("p b h -> p (b h)"), P, RMAX).then_inc(dmax_all.sem, 1)
                    if half == 0:
                        split(j, 6)
                split_next(0)
                split_next(1)
                wait(pool, dec_exp, j)
                settle(pool, "pool")
                pool.affine_select(out=blocks(decayT), in_=blocks(decayT), compare_op=ALU.is_ge, fill=0.0, base=0,
                                   pattern=[[0, NBLK], [1, P]], channel_multiplier=-1).then_inc(dec_masked.sem, 1)
                for l in range(7):
                    if l == 0:
                        wait(pool, a_ready, j)
                        wait(pool, q_ready, j)
                    if l == 2:
                        wait(pool, y0_ready, j)
                    if l >= 3:
                        wait(pool, z_done, j, 2 * (l - 2))
                    pool.tensor_tensor(levelT[l % 2], blocks(aT), v.level_mask[:, l].unsqueeze(1).broadcast_to([P, NBLK, P]),
                                       ALU.mult).then_inc(level_ready.sem, 1)
                    if l == 1:
                        split_next(2)
                split_next(3)
                split_next(4)

            each_step(pool, step)

        @block.vector
        def _(dve):
            give_credits(dve, "dve")

            def step(j, last):
                wait(dve, piece_out, j, 9)
                dve.tensor_tensor(qk_self, qT[:, SEQ:TOK], kT[:, SEQ:TOK], ALU.mult).then_inc(self_ready.sem, 1)
                dve.tensor_copy(bias_j, v.dec_bias[:].rearrange("p (b g) h -> p b g h", b=DEC)[:, :, :, ds(2 * j, 2)])
                dve.tensor_copy(conv_j.unsqueeze(2), v.gconv[:].rearrange("p (y h) n -> p y h n", y=3)[:, :, ds(j, 1), :])
                dve.tensor_copy(dg.unsqueeze(2), v.dec_gates[:, :, ds(j, 1), :])
                dve.tensor_copy(gs[:, BETA].unsqueeze(2), v.beta_n[:, :, ds(j, 1)])
                dve.tensor_copy(gs[:, GCUM].unsqueeze(2), v.gcum_n[:, :, ds(j, 1)])
                wait(dve, ck_loaded, j)
                wait(dve, mix_stored, j, 0)
                dve.tensor_tensor(ck_diag.rearrange("p h (c s) -> p (h c) s", c=NBLK),
                                  ck_row.rearrange("p h (c s) -> p (h c) s", c=NBLK),
                                  v.causal[:].unsqueeze(1).broadcast_to([P, 2 * NBLK, P]), ALU.add)
                wait(dve, nat_turned, j)
                for dst, bank in ((k_nat, 3), (v_nat, 5)):
                    for hf in range(2):
                        dve.tensor_copy(dst[:, 4 * hf:4 * hf + 4], ps[:, bank + hf].rearrange("p (c i) -> p c i", c=4))
                dve.tensor_copy(kv_dec[:].rearrange("p n d -> p (n d)"), ps[0:DEC, 7, 0:2 * P]).then_inc(nat_out.sem, 1)
                wait(dve, self_done, j)
                dve.tensor_scalar(d_self, ps[:, 2, 0:2 * DEC].rearrange("p (h b) -> p b h", h=2), SCALE, None, ALU.mult).then_inc(dself_out.sem, 1)

                def score_unit(u):
                    h, i = u // NBLK, u % NBLK
                    wait(dve, qk_done, j, u + 1)
                    if u >= 2:
                        wait(dve, p_turned, j, u - 1)
                    settle(dve, "dve")
                    first = -NEG_BIG
                    if i:
                        dve.tensor_tensor_reduce(out=prob[:, u % 2, 0:i * P], in0=ps[:, 3:5].rearrange("p a n -> p (a n)")[:, 0:i * P],
                                                 in1=ck_row[:, h, 0:i * P], scale=-SCALE, scalar=-NEG_BIG, op0=ALU.add,
                                                 op1=ALU.min, accum_out=max_part[:, u:u + 1])
                        dve.drain()
                        first = max_part[:, u:u + 1]
                    dve.tensor_tensor_reduce(out=prob[:, u % 2, i * P:(i + 1) * P], in0=ps[:, 3 + i // 4, (i % 4) * P:(i % 4 + 1) * P],
                                             in1=ck_diag[:, h, i * P:(i + 1) * P], scale=-SCALE, scalar=first, op0=ALU.add,
                                             op1=ALU.min, accum_out=neg_max[:, u:u + 1]).then_inc(scored.sem, 1)

                def probs_out(u):
                    i = u % NBLK
                    if i < 4:
                        return
                    wait(dve, p_turned, j, u + 1)
                    if u >= 2:
                        wait(dve, pv_done, j, u - 1)
                    n = i - 3
                    dve.tensor_copy(probT[:, u % 2, 4:4 + n], ps[:, 6, 0:n * P].rearrange("p (c i) -> p c i", c=n)).then_inc(p_out_b.sem, 1)

                def unit_out(u):
                    h, i = u // NBLK, u % NBLK
                    wait(dve, expd, j, u + 1)
                    if u == 0:
                        wait(dve, nat_stored, j)
                    dve.reciprocal(row_inv[:, u:u + 1], row_sum[:, u:u + 1])
                    dve.drain()
                    wait(dve, pv_done, j, u + 1)
                    dve.tensor_scalar(o_nat[:, i, h * FD:(h + 1) * FD], ps[:, 7, 0:FD], row_inv[:, u:u + 1], None,
                                      ALU.mult).then_inc(pv_out.sem, 1)

                def dec_score(b):
                    if b == 0:
                        wait(dve, q_wide_out, j)
                    wait(dve, k_loaded[b % 2], j, 128 * (b // 2 + 1))
                    k = k_past[:, b % 2]
                    dve.tensor_tensor(k, k, q_wide[:, b:b + 1].broadcast_to([P, PAGES, P]), ALU.mult)
                    dve.drain()
                    dve.tensor_reduce(score[:, b].rearrange("p g h -> p (g h)"), k.rearrange("p g (h d) -> p (g h) d", h=2), AX.X, ALU.add).then_inc(k_used.sem, 1)

                def dec_max(half):
                    r = slice(4 * half, 4 * half + 4)
                    dve.drain()
                    s = score[:, r].rearrange("p b g h -> p (b g) h")
                    dve.scalar_tensor_tensor(out=s, in0=s, scalar=SCALE, in1=bias_j[:, r].rearrange("p b g h -> p (b g) h"), op0=ALU.mult, op1=ALU.add)
                    dve.drain()
                    dve.tensor_reduce(d_max[:, r], score[:, r].rearrange("p b g h -> p b h g"), AX.X, ALU.max).then_inc(dmax_ready.sem, 1)

                def dec_less_max(half):
                    r = slice(4 * half, 4 * half + 4)
                    wait(dve, dmax_all, j, half + 1)
                    dve.tensor_tensor(d_max[:, r], d_all[:, r], d_self[:, r], ALU.max)
                    dve.drain()
                    dve.tensor_tensor(score[:, r], score[:, r], d_max[:, r].unsqueeze(2).broadcast_to([P, 4, PAGES, 2]), ALU.subtract)
                    dve.tensor_tensor(d_self[:, r], d_self[:, r], d_max[:, r], ALU.subtract).then_inc(dsub_ready.sem, 1)

                def dec_result(half):
                    r4 = slice(4 * half, 4 * half + 4)
                    wait(dve, dpv_done, j, half + 1)
                    dve.tensor_reduce(d_den[:, r4], ps[:, 2, 0:64].rearrange("p (b g h) -> p b h g", b=4, g=PAGES), AX.X, ALU.add)
                    dve.drain()
                    dve.tensor_tensor(d_den[:, r4], d_den[:, r4], d_pself[:, r4], ALU.add)
                    dve.drain()
                    dve.reciprocal(d_den[:, r4], d_den[:, r4])
                    for h in range(2):
                        r = slice(h * FD, (h + 1) * FD)
                        cols = slice(SEQ + 4 * half, SEQ + 4 * half + 4)
                        dve.drain()
                        dve.tensor_tensor(d_tmp[r, 0:4], vT[r, cols], d_pself[r, r4, h], ALU.mult)
                        dve.drain()
                        dve.tensor_tensor(d_tmp[r, 0:4], d_tmp[r, 0:4], ps[r, 2, 64:72].rearrange("p (b h) -> p b h", h=2)[:, :, h], ALU.add)
                        dve.drain()
                        ins = dve.tensor_tensor(mix[r, cols], d_tmp[r, 0:4], d_den[r, r4, h], ALU.mult)
                    ins.then_inc(dec_out.sem, 1)

                for u in range(-1, 2 * NBLK + 1):
                    if u + 1 < 2 * NBLK:
                        score_unit(u + 1)
                    if 0 <= u < 2 * NBLK:
                        probs_out(u)
                    if u >= 1:
                        unit_out(u - 1)
                    if u in DEC_SCORE_AT:
                        dec_score(DEC_SCORE_AT.index(u))
                    if u == DEC_SCORE_AT[3]:
                        dec_max(0)
                    if u == DEC_PV_AT - 2:
                        dec_less_max(0)
                    if u == DEC_PV_AT:
                        dec_result(0)
                wait(dve, o_turned, j)
                for hf in range(2):
                    ins = dve.tensor_copy(mix[:, 512 * hf:512 * (hf + 1)], ps[:, 3 + hf])
                ins.then_inc(mix_ready.sem, 1)
                for b in range(len(DEC_SCORE_AT), DEC):
                    dec_score(b)
                dec_max(1)
                wait(dve, piece_out, j, 18)
                dve.tensor_copy(ext[:, :, TAPS - 1 + SEQ:].rearrange("p y (b i) -> p y b i", b=DEC)[:, 0, :, 0:3],
                                conv_j[:, 0, 4:28].rearrange("p (b i) -> p b i", b=DEC))
                for y in range(1, 3):
                    dve.tensor_copy(ext[:, y, TAPS - 1 + SEQ:].rearrange("p (b i) -> p b i", b=DEC)[:, :, 0:3],
                                    conv_j[:, y, 4:28].rearrange("p (b i) -> p b i", b=DEC))
                dve.tensor_copy(tail[:, :, 0:3], ext[:, :, SEQ:SEQ + 3])
                for y in range(3):
                    ins = dve.tensor_copy(tail[:, y, 3:3 + DEC], ext[:, y, TAPS - 1 + SEQ:].rearrange("p (b i) -> p b i", b=DEC)[:, :, TAPS - 1])
                ins.then_inc(tail_ready.sem, 1)
                dve.drain()
                for y in range(3):
                    if y == 1:
                        dec_less_max(1)
                    dve.tensor_scalar(conv[:, y], ext[:, y, 0:CONV], conv_j[:, y, 0:1], None, ALU.mult)
                    for i in range(1, TAPS):
                        dve.drain()
                        ins = dve.scalar_tensor_tensor(out=conv[:, y], in0=ext[:, y, i:i + CONV], scalar=conv_j[:, y, i:i + 1], in1=conv[:, y],
                                                       op0=ALU.mult, op1=ALU.add)
                    ins.then_inc(conv_done.sem, 1)
                wait(dve, tail_turned, j)
                wait(dve, tail_stored, j, 0)
                dve.tensor_copy(tail_rows[:].rearrange("p y n -> p (y n)"), ps[0:TAPS - 1 + DEC, 7, 0:3 * P]).then_inc(tail_out.sem, 1)
                dec_result(1)
                wait(dve, rows_loaded, j)
                dve.tensor_copy(gs[:, GLAST], blocks(gc_row)[:, :, P - 1])
                dve.drain()
                dve.tensor_tensor(gs[:, KD], gs[:, GLAST], gs[:, GCUM], ALU.subtract).then_inc(g_ready.sem, 1)
                wait(dve, l2_rstd, j)
                dve.tensor_tensor(conv[:, 0:2], conv[:, 0:2], rs_qk, ALU.mult)
                dve.tensor_tensor(blocks(decayT), blocks(gc_row), gs[:, GCUM].unsqueeze(2).broadcast_to([P, NBLK, P]), ALU.subtract)
                dve.drain()
                dve.tensor_scalar(decayT, decayT, 0.0, None, ALU.min).then_inc(dif_ready.sem, 1)
                dve.tensor_tensor(k_scaled, conv[:, 1, 0:SEQ], beta_row, ALU.mult).then_inc(l2_out.sem, 1)
                wait(dve, gs_exp, j)
                dve.scalar_tensor_tensor(out=gs[:, KB], in0=gs[:, BETA], scalar=-1.0, in1=gs[:, EG], op0=ALU.mult, op1=ALU.mult)
                dve.drain()
                wait(dve, gnat_turned, j)
                for hf in range(2):
                    cs = slice(4 * hf, 4 * hf + 4)
                    kps, vps = (ps[:, bank + hf].rearrange("p (c i) -> p c i", c=4) for bank in (2, 4))
                    for out, src, which in ((k_dec, kps, KD), (k_beta, kps, KB), (v_beta, vps, BETA)):
                        ins = dve.tensor_tensor(blocks(out)[:, cs], src, gs[:, which, cs].unsqueeze(2).broadcast_to([P, 4, P]), ALU.mult)
                ins.then_inc(gnat_out.sem, 1)
                wait(dve, kk_done, j)
                wait(dve, dec_masked, j)
                for hf in range(2):
                    ins = dve.tensor_tensor(aT[:, 512 * hf:512 * (hf + 1)], ps[:, 6 + hf], decayT[:, 512 * hf:512 * (hf + 1)], ALU.mult)
                ins.then_inc(a_ready.sem, 1)
                wait(dve, gqk_done, j)
                for hf in range(2):
                    dve.tensor_tensor(qkT[:, 512 * hf:512 * (hf + 1)], ps[:, 2 + hf], decayT[:, 512 * hf:512 * (hf + 1)], ALU.mult)
                wait(dve, eg_row_ready, j)
                dve.tensor_tensor(conv[:, 0, 0:SEQ], conv[:, 0, 0:SEQ], eg_row, ALU.mult).then_inc(q_ready.sem, 1)
                wait(dve, level_ready, j, 1)
                dve.tensor_tensor(invT, v.ident[:].unsqueeze(1).broadcast_to([P, NBLK, P]), levelT[0], ALU.subtract).then_inc(y0_ready.sem, 1)
                wait(dve, y0_turned, j)
                for hf in range(2):
                    ins = dve.tensor_copy(inv[:, 4 * hf:4 * hf + 4], ps[:, 4 + hf].rearrange("p (c i) -> p c i", c=4))
                ins.then_inc(x0_ready.sem, 1)
                for n in range(12):
                    hf = n % 2
                    cs = slice(4 * hf, 4 * hf + 4)
                    l = 1 + n // 2
                    wait(dve, xy_done, j, n + 1)
                    if n < 10:
                        x = halves(inv[:, cs].rearrange("p c i -> p (c i)"), l)[:, :, 0]
                        dve.tensor_tensor(x, x, ps[:, 4 + hf, 0:256].rearrange("p (n w) -> p n w", w=1 << l), ALU.subtract)
                    y = halves(invT[:, cs].rearrange("p c i -> p (c i)"), l)[:, :, 1]
                    dve.tensor_tensor(y, y, ps[:, 6 + hf, 0:256].rearrange("p (n w) -> p n w", w=1 << l), ALU.subtract).then_inc(xy_out.sem, 1)
                wait(dve, w_done, j)
                for hf in range(2):
                    ins = dve.tensor_copy(wT[:, 4 * hf:4 * hf + 4], ps[:, 2 + hf].rearrange("p (c i) -> p c i", c=4))
                ins.then_inc(w_out_.sem, 1)
                wait(dve, state_stored, j, 0)
                dve.memset(state[:], 0.0).then_inc(state_zero.sem, 1)
                for c in range(NBLK):
                    dve.drain()
                    wait(dve, sc_done, j, c + 1)
                    dve.scalar_tensor_tensor(out=state[:], in0=state[:], scalar=gs[:, EGL, c:c + 1], in1=ps[:, 2 + c % 2, 0:GD],
                                             op0=ALU.mult, op1=ALU.add).then_inc(sc_out.sem, 1)
                dec = conv[:, :, SEQ:CONV].rearrange("p y (b i) -> p y b i", i=TAPS)[:, :, :, TAPS - 1]
                dve.tensor_copy(kq[:, :, 0], dec[:, 1])
                dve.tensor_copy(kq[:, :, 1], dec[:, 0])
                dve.tensor_tensor(kq_prod, dec[:, 0], dec[:, 1], ALU.mult)
                wait(dve, s_loaded, j)
                dve.tensor_tensor(blocks(s_dec), blocks(s_dec), dg[:, 0].unsqueeze(2).broadcast_to([P, DEC, GD]), ALU.mult).then_inc(kq_ready.sem, 1)
                wait(dve, sdec_done, j)
                dve.tensor_copy(kq_dot, ps[:, 5, 0:DEC])
                sk = ps[:, 4, 0:2 * DEC].rearrange("p (b n) -> p b n", n=2)
                dve.tensor_tensor(delta, dec[:, 2], sk[:, :, 0], ALU.subtract)
                dve.drain()
                dve.tensor_tensor(delta, delta, dg[:, 1], ALU.mult)
                dve.drain()
                dve.tensor_tensor(d_tmp, delta, kq_dot, ALU.mult)
                dve.drain()
                dve.tensor_tensor(oT[:, SEQ:TOK], d_tmp, sk[:, :, 1], ALU.add).then_inc(delta_ready.sem, 1)
                wait(dve, rows_turned, j)
                dve.tensor_copy(nat_dec.rearrange("p n d -> p (n d)"), ps[0:DEC, 4, 0:2 * P])
                dve.drain()
                dve.tensor_tensor(delta_diag, nat_dec[:, 1].unsqueeze(1).broadcast_to([DEC, DEC, P]),
                                  v.ident[0:DEC, 0:DEC].unsqueeze(2).broadcast_to([DEC, DEC, P]), ALU.mult).then_inc(diag_ready.sem, 1)
                wait(dve, outer_done, j)
                for hf in range(2):
                    ins = dve.tensor_tensor(s_dec[:, 512 * hf:512 * (hf + 1)], s_dec[:, 512 * hf:512 * (hf + 1)], ps[:, 2 + hf], ALU.add)
                ins.then_inc(sdec_ready.sem, 1)
                wait(dve, orstd_ready, j)
                dve.scalar_tensor_tensor(out=oT, in0=oT, scalar=v.out_norm[:], in1=o_rstd, op0=ALU.mult, op1=ALU.mult)
                dve.drain()
                dve.tensor_tensor(oT, oT, z_silu[:], ALU.mult).then_inc(o_ready.sem, 1)

            each_step(dve, step)
            for c in (nat_stored, mix_stored, tail_stored, state_stored):
                wait(dve, c, STEPS - 1)


def out_projection(nc, t, v, act_t, w, up):
    with ExitStack() as scope:
        ps = v.ps
        xT = act_t[:, 0:KC]
        mix = act_t[:, KC:2 * KC]
        sq = act_t[:, 2 * KC:2 * KC + 2]
        rstd = act_t[:, 2 * KC + 2]
        w_raw, w_hi, w_lo = w
        mix_loaded = [v.sem(f"mix_loaded{k}") for k in range(KC)]
        w_loaded = [v.sem("wo_loaded0"), v.sem("wo_loaded1")]
        x_loaded, mix_hi, mix_lo = v.sem("x1_loaded"), v.sem("mix_hi"), v.sem("mix_lo")
        w_split_hi, w_split_lo = v.sem("wo_split_hi"), v.sem("wo_split_lo")
        piece_done, piece_out, x_saved = v.sem("wo_piece_done"), v.sem("wo_piece_out"), v.sem("x1_saved")
        S = norm_signals(v, "n1")
        w_view = t["w_out"][0].rearrange("(k p) n -> p k n", p=P)

        block = scope.enter_context(nc.Block())

        @block.sync
        def _(sp):
            for i in range(2):
                sp.dma_start(w_raw[:, i], w_view[:, :, i * P:(i + 1) * P]).then_inc(w_loaded[i], 16)
            for k in range(KC):
                sp.dma_start(mix[:, k], v.mix_dram[k]).then_inc(mix_loaded[k], 16)
            sp.dma_start(xT, v.x_dram).then_inc(x_loaded, 16)
            with sp.Fori(1, KC // 2) as it:
                for i in range(2):
                    sp.wait_ge(w_split_lo, it * 2 + i - 1)
                    sp.dma_start(w_raw[:, i], w_view[:, :, ds((it * 2 + i) * P, P)]).then_inc(w_loaded[i], 16)
            w_up = t["w_up"][0].rearrange("(k p) n -> p k n", p=P)
            for i in range(2):
                sp.wait_ge(w_split_lo, KC - 1 + i)
                sp.dma_start(w_raw[:, i], w_up[:, :, FFN * i:FFN * i + P]).then_inc(up["loaded"][i], 16)
            sp.wait_ge(piece_out, NG * KC)
            sp.dma_start(v.x_dram, xT).then_inc(x_saved, 16)
            sp.wait_ge(x_saved, 16)

        @block.scalar
        def _(act):
            for i in range(2):
                act.wait_ge(w_loaded[i], 16)
                act.activation(w_hi[:, i], w_raw[:, i], ACT.Copy).then_inc(w_split_hi, 1)
            for k in range(KC):
                act.wait_ge(mix_loaded[k], 16)
                act.activation(v.hi[:, k], mix[:, k], ACT.Copy).then_inc(mix_hi, 1)
            with act.Fori(1, KC // 2) as it:
                for i in range(2):
                    act.wait_ge(w_loaded[i], it * 16 + 16)
                    act.wait_ge(piece_done, it * 6 + 3 * (i - 1))
                    act.activation(w_hi[:, i], w_raw[:, i], ACT.Copy).then_inc(w_split_hi, 1)
            for i in range(2):
                act.wait_ge(up["loaded"][i], 16)
                act.wait_ge(piece_done, NG * (KC - 1 + i))
                act.activation(w_hi[:, i], w_raw[:, i], ACT.Copy).then_inc(up["hi"], 1)
            norm_act(act, v, S, rstd, mix)

        @block.gpsimd
        def _(pool):
            with pool.Fori(0, KC // 2) as it:
                for i in range(2):
                    pool.wait_ge(w_split_hi, it * 2 + i + 1)
                    pool.tensor_tensor(w_lo[:, i], w_raw[:, i], w_hi[:, i].bitcast(F32), ALU.subtract).then_inc(w_split_lo, 1)
            for i in range(2):
                pool.wait_ge(up["hi"], i + 1)
                pool.tensor_tensor(w_lo[:, i], w_raw[:, i], w_hi[:, i].bitcast(F32), ALU.subtract).then_inc(up["lo"], 1)
            norm_pool(pool, v, S, mix, v.lo)

        @block.tensor
        def _(pe):
            pe.wait_ge(mix_lo, KC)
            def tile(n, i, first):
                pe.wait_ge(w_split_lo, n + 1)
                for g in range(NG):
                    if not first:
                        pe.wait_ge(piece_out, n * NG + (g + 1 - 2 * NG))
                    for k in range(KC):
                        mm = split_piece(pe, ps[:, NG * i + g, 0:GRP], w_hi[:, i, k], w_lo[:, i, k],
                                         v.hi[:, k, g * GRP:(g + 1) * GRP], v.lo[:, k, g * GRP:(g + 1) * GRP],
                                         k, k == 0, k == KC - 1)
                    mm.then_inc(piece_done, 1)

            for i in range(2):
                tile(i, i, True)
            with pe.Fori(1, KC // 2) as it:
                for i in range(2):
                    tile(it * 2 + i, i, False)
            norm_pe(pe, v, S, sq[:, 1])

        @block.vector
        def _(dve):
            for k in range(KC):
                dve.wait_ge(mix_hi, k + 1)
                dve.tensor_tensor(v.lo[:, k], mix[:, k], v.hi[:, k].bitcast(F32), ALU.subtract).then_inc(mix_lo, 1)
            dve.memset(sq[:, 1], 0.0)
            dve.wait_ge(x_loaded, 16)
            with dve.Fori(0, KC // 2) as it:
                for i in range(2):
                    for g in range(NG):
                        dve.wait_ge(piece_done, it * (2 * NG) + (NG * i + g + 1))
                        x = xT[:, ds(it * 2 + i, 1), g * GRP:(g + 1) * GRP].rearrange("p a n -> p (a n)")
                        dve.tensor_tensor(x, x, ps[:, NG * i + g, 0:GRP], ALU.add).then_inc(piece_out, 1)
                    dve.drain()
                    add_squares(dve, xT[:, ds(it * 2 + i, 1)].rearrange("p a n -> p (a n)"), sq)
            dve.drain().then_inc(S["squared"], 1)
            norm_dve(dve, v, S, xT, rstd, mix, 1, v.lo)


def dense(nc, t, v):
    with ExitStack() as outer:
        act_t = v.sb("ffn_act", [P, FT, TOK], F32, outer)
        with ExitStack() as scope:
            w = [v.sb(name, [P, 2, KC, P], dt, scope) for name, dt in (("w2_raw", F32), ("w2_hi", F32R), ("w2_lo", F32R))]
            up = {"loaded": [v.sem("wu_loaded0"), v.sem("wu_loaded1")], "hi": v.sem("wu_split_hi"), "lo": v.sem("wu_split_lo")}
            out_projection(nc, t, v, act_t, w, up)
            ffn_up(nc, t, v, act_t, w, up)
        xT = v.sb("xT2", [P, KC, TOK], F32, outer)
        sq = act_t[:, 0:2]
        S = norm_signals(v, "n2")
        ffn_down(nc, t, v, act_t, xT, sq, S)
        finish(nc, t, v, act_t, xT, sq, S)


def ffn_up(nc, t, v, act_t, w, up):
    with ExitStack() as scope:
        def sb(name, shape, dt=F32):
            return v.sb(name, shape, dt, scope)

        ps = v.ps
        w_raw, w_hi, w_lo = w
        gate = sb("gate_ext", [P, FEXT])
        y = sb("gate_conv", [P, FCONV])
        par = sb("fconv_f", [P, 20])
        tail = sb("gate_tail", [P, FTAPS - 1 + DEC])
        tail_rows = sb("gate_tail_rows", [FTAPS - 1 + DEC, P])
        w_loaded, w_split_hi, w_split_lo = up["loaded"], up["hi"], up["lo"]
        piece_done, gate_out, up_out = v.sem("wu_piece_done"), v.sem("gate_out"), v.sem("up_out")
        context_in, conv_done, silu_done = v.sem("gate_context_in"), v.sem("gate_conv_done"), v.sem("gate_silu_done")
        tail_ready, tail_turned, tail_out, tail_stored = v.sem("gt_ready"), v.sem("gt_turned"), v.sem("gt_out"), v.sem("gt_stored")
        ctx_copied, gate_zeroed = v.sem("gate_ctx_copied"), v.sem("gate_zeroed")
        w_view = t["w_up"][0].rearrange("(k p) n -> p k n", p=P)

        block = scope.enter_context(nc.Block())

        @block.sync
        def _(sp):
            sp.dma_start(t["new_ffn_conv_sample"][0, :, 0:1, :], t["state_ffn_conv"][0, :, 1:2, :]).then_inc(ctx_copied, 16)
            with sp.Fori(1, FT) as f:
                for i in range(2):
                    sp.wait_ge(w_split_lo, f * 2 + (i + 1 - 2))
                    sp.dma_start(w_raw[:, i], w_view[:, :, ds(f * P + FFN * i, P)]).then_inc(w_loaded[i], 16)
            sp.wait_ge(ctx_copied, 16)

        @block.gpsimd
        def _(pool):
            pool.memset(gate[:, 0:FTAPS - 1], 0.0).then_inc(gate_zeroed, 1)
            with pool.Fori(1, FT) as f:
                for i in range(2):
                    pool.wait_ge(w_split_hi, f * 2 + (i + 1))
                    pool.tensor_tensor(w_lo[:, i], w_raw[:, i], w_hi[:, i].bitcast(F32), ALU.subtract).then_inc(w_split_lo, 1)

        @block.tensor
        def _(pe):
            pe.sem_inc(piece_done, 2 * NG)
            pe.sem_inc(tail_turned, 1)
            with pe.Fori(0, FT) as f:
                for i in range(2):
                    pe.wait_ge(w_split_lo, f * 2 + (i + 1))
                    for g in range(NG):
                        pe.wait_ge((gate_out, up_out)[i], f * NG + (g + 1))
                        for k in range(KC):
                            mm = split_piece(pe, ps[:, NG * i + g, 0:GRP], w_hi[:, i, k], w_lo[:, i, k],
                                             v.hi[:, k, g * GRP:(g + 1) * GRP], v.lo[:, k, g * GRP:(g + 1) * GRP],
                                             k, k == 0, k == KC - 1)
                        mm.then_inc(piece_done, 1)
                        if i == 1 and g == 0:
                            pe.wait_ge(tail_ready, f + 1)
                            pe.transpose(ps[0:FTAPS - 1 + DEC, 6, 0:P], tail[:], v.ident[:]).then_inc(tail_turned, 1)

        @block.scalar
        def _(act):
            act.sem_inc(gate_out, NG)
            act.sem_inc(tail_stored, 32)
            act.wait_ge(gate_zeroed, 1)
            def split(f, i):
                act.wait_ge(w_loaded[i], f * 16 + 32)
                act.wait_ge(piece_done, f * (2 * NG) + NG * (i + 3))
                act.activation(w_hi[:, i], w_raw[:, i], ACT.Copy).then_inc(w_split_hi, 1)

            def channel_tile(f):
                act.wait_ge(conv_done, f + 1)
                for g in range(NG):
                    act.wait_ge(piece_done, f * (2 * NG) + (2 * NG + g + 1))
                    a = g * GRP
                    n = min(GRP, SEQ - a)
                    ins = act.activation(gate[:, FTAPS - 1 + a:FTAPS - 1 + a + n], ps[:, g, 0:n], ACT.Copy)
                    if n < GRP:
                        ins = act.activation(gate[:, FTAPS - 1 + SEQ:].rearrange("p (b i) -> p b i", b=DEC)[:, :, FTAPS - 1], ps[:, g, n:GRP], ACT.Copy)
                    ins.then_inc(gate_out, 1)
                act.wait_ge(conv_done, f + 2)
                act.activation(y[:], y[:], ACT.Silu).then_inc(silu_done, 1)
                act.wait_ge(tail_out, f + 2)
                act.dma_start(t["new_ffn_conv_prompt"][0, 0, :, ds(f * P, P)], tail_rows[0:FTAPS - 1]).then_inc(tail_stored, 16)
                act.dma_start(t["new_ffn_conv_sample"][0, :, FTAPS - 2, ds(f * P, P)], tail_rows[FTAPS - 1:]).then_inc(tail_stored, 16)

            with act.Fori(0, FT - 1) as f:
                channel_tile(f)
                split(f, 0)
                split(f, 1)
            channel_tile(FT - 1)
            act.wait_ge(tail_stored, 32 * (FT + 1))

        @block.vector
        def _(dve):
            dve.sem_inc(up_out, NG)
            dve.sem_inc(conv_done, 1)
            dve.sem_inc(tail_out, 1)
            with dve.Fori(0, FT) as f:
                dve.tensor_copy(par[:].unsqueeze(1), v.fconv[:, ds(f, 1), :])
                dve.drain()
                decode = gate[:, FTAPS - 1 + SEQ:].rearrange("p (b i) -> p b i", b=DEC)
                dve.tensor_copy(decode[:, :, 0:FTAPS - 1], par[:, 4:20].rearrange("p (b i) -> p b i", b=DEC))
                dve.wait_ge(gate_out, f * NG + 2 * NG)
                dve.wait_ge(tail_turned, f + 1)
                dve.tensor_copy(tail[:, 0:FTAPS - 1], gate[:, SEQ:SEQ + FTAPS - 1])
                dve.tensor_copy(tail[:, FTAPS - 1:], decode[:, :, FTAPS - 1]).then_inc(tail_ready, 1)
                dve.drain()
                dve.tensor_scalar(y[:], gate[:, 0:FCONV], par[:, 0:1], par[:, 3:4], ALU.mult, ALU.add)
                for i in range(1, FTAPS):
                    dve.drain()
                    ins = dve.scalar_tensor_tensor(out=y[:], in0=gate[:, i:i + FCONV], scalar=par[:, i:i + 1], in1=y[:], op0=ALU.mult, op1=ALU.add)
                ins.then_inc(conv_done, 1)
                dve.wait_ge(tail_turned, f + 2)
                dve.wait_ge(tail_stored, f * 32 + 32)
                dve.tensor_copy(tail_rows[:], ps[0:FTAPS - 1 + DEC, 6, 0:P]).then_inc(tail_out, 1)
                dve.wait_ge(silu_done, f + 1)
                for g in range(NG):
                    dve.wait_ge(piece_done, f * (2 * NG) + (3 * NG + g + 1))
                    a = g * GRP
                    n = min(GRP, SEQ - a)
                    ins = dve.tensor_tensor(act_t[:, ds(f, 1), a:a + n].rearrange("p a n -> p (a n)"), y[:, a:a + n], ps[:, NG + g, 0:n], ALU.mult)
                    if n < GRP:
                        yd = y[:, SEQ:FCONV].rearrange("p (b i) -> p b i", b=DEC)[:, :, FTAPS - 1]
                        ins = dve.tensor_tensor(act_t[:, ds(f, 1), SEQ:TOK].rearrange("p a n -> p (a n)"), yd, ps[:, NG + g, n:GRP], ALU.mult)
                    ins.then_inc(up_out, 1)


def ffn_down(nc, t, v, act_t, xT, sq, S):
    with ExitStack() as scope:
        def sb(name, shape, dt=F32):
            return v.sb(name, shape, dt, scope)

        ps = v.ps
        COLS = 2
        PASSES = KC // COLS
        w_raw = sb("wd_raw", [P, 2, COLS * P])
        w_hi = sb("wd_hi", [P, 2, COLS * P], F32R)
        w_lo = sb("wd_lo", [P, 2, COLS * P], F32R)
        w_loaded = [v.sem("wd_loaded0"), v.sem("wd_loaded1")]
        w_split_hi, w_split_lo, used = v.sem("wd_split_hi"), v.sem("wd_split_lo"), v.sem("wd_used")
        a_hi, a_lo = v.sem("ffn_act_hi"), v.sem("ffn_act_lo")
        pass_out = v.sem("down_pass_out")
        x_loaded = v.sem("x2_loaded")
        CREDIT = 2
        KEPT = 6

        block = scope.enter_context(nc.Block())

        def over_chunks(eng, c, step):
            def pair(k, kept, first, last):
                for i in range(2):
                    step(c * FT + (k + i), k + i, i, 2 + k + i if kept else i, first and i == 0, last and i == 1)
            for k in range(0, KEPT, 2):
                pair(k, True, k == 0, False)
            with eng.Fori(KEPT // 2, FT // 2 - 1) as it:
                pair(it * 2, False, False, False)
            pair(FT - 2, False, False, True)

        @block.sync
        def _(sp):
            with sp.Fori(0, PASSES) as c:
                def load(n, k, i, slot, first, last):
                    sp.wait_ge(w_split_lo, n + (1 - 2 + CREDIT))
                    sp.dma_start(w_raw[:, i], t["w_down"][0, ds(k * P, P), ds(c * (COLS * P), COLS * P)]).then_inc(w_loaded[i], 16)

                over_chunks(sp, c, load)

        @block.gpsimd
        def _(pool):
            pool.sem_inc(w_split_lo, CREDIT)
            pool.dma_start(xT[:], v.x_dram).then_inc(x_loaded, 16)
            with pool.Fori(0, PASSES) as c:
                def split(n, k, i, slot, first, last):
                    pool.wait_ge(w_split_hi, n + 1)
                    pool.tensor_tensor(w_lo[:, i], w_raw[:, i], w_hi[:, i].bitcast(F32), ALU.subtract).then_inc(w_split_lo, 1)

                over_chunks(pool, c, split)

        @block.scalar
        def _(act):
            for k in range(KEPT):
                act.activation(v.hi[:, 2 + k], act_t[:, k], ACT.Copy).then_inc(a_hi, 1)
            with act.Fori(0, PASSES) as c:
                def split(n, k, i, slot, first, last):
                    act.wait_ge(used, n + (1 - 2 + CREDIT))
                    if slot < 2:
                        act.activation(v.hi[:, slot], act_t[:, ds(k, 1)].rearrange("p a n -> p (a n)"), ACT.Copy).then_inc(a_hi, 1)
                    act.wait_ge(w_loaded[i], c * (8 * FT) + (k - i) * 8 + 16)
                    act.activation(w_hi[:, i], w_raw[:, i], ACT.Copy).then_inc(w_split_hi, 1)

                over_chunks(act, c, split)

        @block.tensor
        def _(pe):
            pe.sem_inc(used, CREDIT)
            with pe.Fori(0, PASSES) as c:
                def multiply(n, k, i, slot, first, last):
                    if slot < 2:
                        pe.wait_ge(a_lo, c * (FT - KEPT) + (k + 1))
                    else:
                        pe.wait_ge(a_lo, k + 1)
                    pe.wait_ge(w_split_lo, n + (1 + CREDIT))
                    for m in range(COLS):
                        for g in range(NG):
                            if first:
                                pe.wait_ge(pass_out, c * (COLS * NG) + (m * NG + g + 1))
                            cols = slice(m * P, (m + 1) * P)
                            mm = split_piece(pe, ps[:, m * NG + g, 0:GRP], w_hi[:, i, cols], w_lo[:, i, cols],
                                             v.hi[:, slot, g * GRP:(g + 1) * GRP], v.lo[:, slot, g * GRP:(g + 1) * GRP],
                                             0, first, last)
                    mm.then_inc(used, 1)

                over_chunks(pe, c, multiply)

        @block.vector
        def _(dve):
            dve.sem_inc(pass_out, COLS * NG)
            for k in range(KEPT):
                dve.wait_ge(a_hi, k + 1)
                dve.tensor_tensor(v.lo[:, 2 + k], act_t[:, k], v.hi[:, 2 + k].bitcast(F32), ALU.subtract).then_inc(a_lo, 1)
            dve.drain()
            dve.memset(sq[:, 1], 0.0)
            with dve.Fori(0, PASSES) as c:
                def split(n, k, i, slot, first, last):
                    if slot < 2:
                        dve.wait_ge(a_hi, c * (FT - KEPT) + (k + 1))
                        dve.tensor_tensor(v.lo[:, slot], act_t[:, ds(k, 1)].rearrange("p a n -> p (a n)"), v.hi[:, slot].bitcast(F32),
                                          ALU.subtract).then_inc(a_lo, 1)

                over_chunks(dve, c, split)
                dve.wait_ge(x_loaded, 16)
                dve.wait_ge(used, c * FT + (FT + CREDIT))
                for m in range(COLS):
                    for g in range(NG):
                        x = xT[:, ds(c * COLS + m, 1), g * GRP:(g + 1) * GRP].rearrange("p a n -> p (a n)")
                        dve.tensor_tensor(x, x, ps[:, m * NG + g, 0:GRP], ALU.add).then_inc(pass_out, 1)
                for m in range(COLS):
                    dve.drain()
                    add_squares(dve, xT[:, ds(c * COLS + m, 1)].rearrange("p a n -> p (a n)"), sq)
            dve.drain().then_inc(S["squared"], 1)


def finish(nc, t, v, act_t, xT, sq, S):
    with ExitStack() as scope:
        ps = v.ps
        rstd = act_t[:, 2]
        SLOTS = 4
        rows = act_t[:, 3:3 + SLOTS, 0:D]
        y_ready, y_turned, y_copied = v.sem("y_ready"), v.sem("y_turned"), v.sem("y_copied")
        y_stored = [v.sem(f"y_stored{i}") for i in range(SLOTS)]

        block = scope.enter_context(nc.Block())

        @block.vector
        def _(dve):
            dve.wait_ge(S["rstd"], 1)
            for cols in (slice(0, SEQ // 2), slice(SEQ // 2, TOK)):
                for k in range(KC):
                    ins = dve.scalar_tensor_tensor(out=xT[:, k, cols], in0=xT[:, k, cols], scalar=v.norms[:, k, 2:3],
                                                   in1=rstd[:, cols], op0=ALU.mult, op1=ALU.mult)
                ins.then_inc(y_ready, 1)

        @block.tensor
        def _(pe):
            norm_pe(pe, v, S, sq[:, 1])
            pe.wait_ge(S["rstd"], 1)

            def turn(first, i, width):
                for k in range(KC):
                    mm = pe.transpose(ps[0:width, 2 * i + k // 4, (k % 4) * P:(k % 4 + 1) * P],
                                      xT[:, k, ds(first, width)], v.ident[:])
                mm.then_inc(y_turned, 1)

            pe.wait_ge(y_ready, 1)
            for i in range(SLOTS):
                turn(i * P, i, P)
            pe.wait_ge(y_ready, 2)
            for n in range(SLOTS, NBLK + 1):
                pe.wait_ge(y_copied, n - SLOTS + 1)
                turn(n * P, n % SLOTS, P if n < NBLK else DEC)

        @block.scalar
        def _(act):
            norm_act(act, v, S, rstd, None)
            for n in range(NBLK + 1):
                i, width = n % SLOTS, P if n < NBLK else DEC
                act.wait_ge(y_turned, n + 1)
                if n >= SLOTS:
                    act.wait_ge(y_stored[i], 16 * (n // SLOTS))
                act.activation(rows[0:width, i], ps[0:width, 2 * i:2 * i + 2].rearrange("p a n -> p (a n)"), ACT.Copy).then_inc(y_copied, 1)

        @block.sync
        def _(sp):
            for n in range(NBLK + 1):
                i = n % SLOTS
                sp.wait_ge(y_copied, n + 1)
                if n < NBLK:
                    sp.dma_start(t["y_prompt"][0, n * P:(n + 1) * P], rows[:, i]).then_inc(y_stored[i], 16)
                else:
                    sp.dma_start(t["y_sample"].rearrange("b a d -> (b a) d"), rows[0:DEC, i]).then_inc(y_stored[i], 16)
            for i in range(SLOTS):
                sp.wait_ge(y_stored[i], 16 * (2 + (i == 0)))


INPUTS = ["x_prompt", "x_sample", "cache_k", "cache_v", "cache_logf", "state_gdn", "state_gdn_conv",
          "state_ffn_conv", "page_table", "norm_mix", "w_in", "b_forget", "gdn_a_log", "gdn_dt_bias",
          "w_gdn_conv", "gdn_out_norm", "w_out", "norm_ffn", "w_up", "w_ffn_conv", "b_ffn_conv", "w_down",
          "norm_final"]
OUTPUTS = [("y_prompt", (1, SEQ, D)), ("y_sample", (DEC, 1, D)),
           ("new_k_prompt", (1, 1, SEQ, FH, FD)), ("new_v_prompt", (1, 1, SEQ, FH, FD)),
           ("new_logf_prompt", (1, 1, SEQ, FH)), ("new_gdn_prompt", (1, 1, GH, GD, GD)),
           ("new_gdn_conv_prompt", (1, 1, TAPS - 1, 3 * GW)), ("new_ffn_conv_prompt", (1, 1, FTAPS - 1, FFN)),
           ("new_k_sample", (1, DEC, 1, FH, FD)), ("new_v_sample", (1, DEC, 1, FH, FD)),
           ("new_logf_sample", (1, DEC, 1, FH)), ("new_gdn_sample", (1, DEC, GH, GD, GD)),
           ("new_gdn_conv_sample", (1, DEC, TAPS - 1, 3 * GW)), ("new_ffn_conv_sample", (1, DEC, FTAPS - 1, FFN))]


def kernel(**inputs):
    import numpy as np
    import concourse.bacc as bacc
    from concourse import mybir as mb
    from concourse.bass_utils import run_bass_kernel_spmd

    nc = bacc.Bacc("TRN2", target_bir_lowering=False, num_devices=1)
    arrays, t = {}, {}
    for name in INPUTS:
        a = np.ascontiguousarray(inputs[name])
        arrays[f"in_{name}"] = a
        t[name] = nc.dram_tensor(f"in_{name}", a.shape, mb.dt.from_np(a.dtype), kind="ExternalInput").ap()
    for name, shape in OUTPUTS:
        t[name] = nc.dram_tensor(f"out_{name}", shape, mb.dt.float32, kind="ExternalOutput").ap()
    program(nc, t)
    r = run_bass_kernel_spmd(nc, [arrays], core_ids=[0])
    return tuple(r.results[0][f"out_{name}"] for name, _ in OUTPUTS)
```

```python
from contextlib import ExitStack

import concourse.bass as bass
from concourse import mybir

ALU = mybir.AluOpType
ACT = mybir.ActivationFunctionType
AX = mybir.AxisListType
F32 = mybir.dt.float32
F32R = mybir.dt.float32r
I32 = mybir.dt.int32
RMAX = bass.bass_isa.ReduceOp.max
ds = bass.ds

P = 128
D = 1024
KC = D // P
SEQ = 1024
NBLK = SEQ // P
DEC = 8
TOK = SEQ + DEC
GRP = TOK // 3
NG = TOK // GRP
FH, FD = 8, 64
FW = FH * FD
GH, GD = 4, 128
GW = GH * GD
PAGES = 8
TAPS = 4
EXT = (TAPS - 1) + SEQ + TAPS * DEC
CONV = EXT - (TAPS - 1)
FFN = 2816
FT = FFN // P
FTAPS = 3
FEXT = (FTAPS - 1) + SEQ + FTAPS * DEC
FCONV = FEXT - (FTAPS - 1)
EPS = 1e-6
NEG_BIG = -1e30
SCALE = FD ** -0.5
LN_GSCALE = -0.5 * 4.852030263919617
EARLY_PAGES, POOL_PAGES = 28, 20
STEPS = 4
R_F, R_A, R_B, GROWS = 0, 32, 64, 96
C_FQ, C_FK, C_FV, C_FF = 0, FW, 2 * FW, 3 * FW
C_GQ = C_FF + FH
C_GK, C_GV = C_GQ + GW, C_GQ + 2 * GW
C_GA = C_GQ + 3 * GW
C_GZ = C_GA + 2 * GH
TILE_COL = (C_FQ, C_FK, C_FV, C_GQ, C_GK, C_GV, C_GZ)
NTILE = len(TILE_COL)


class OnChip:

    def __init__(self, sem, mixer_sem, sb, ps, x_dram, mix_dram, gate_dram, ident, ones, head_ones, later,
                 causal, level_mask, norms, gconv, fconv, out_norm, hi, lo, logf_n,
                 beta_n, gcum_n, page_ids, dec_bias, dec_gates):
        self.sem = sem
        self.mixer_sem = mixer_sem
        self.sb = sb
        self.ps = ps
        self.x_dram = x_dram
        self.mix_dram = mix_dram
        self.gate_dram = gate_dram
        self.ident = ident
        self.ones = ones
        self.head_ones = head_ones
        self.later = later
        self.causal = causal
        self.level_mask = level_mask
        self.norms = norms
        self.gconv = gconv
        self.fconv = fconv
        self.out_norm = out_norm
        self.hi = hi
        self.lo = lo
        self.logf_n = logf_n
        self.beta_n = beta_n
        self.gcum_n = gcum_n
        self.page_ids = page_ids
        self.dec_bias = dec_bias
        self.dec_gates = dec_gates


def groups(width, n):
    step = width // n
    return [(g * step, step) for g in range(n)]


def program(nc, t):
    stack = ExitStack()
    mixer_sems = []

    def sem(name):
        return stack.enter_context(nc.semaphore(name))

    def mixer_sem(name):
        mixer_sems.append(nc.alloc_semaphore(name))
        return mixer_sems[-1]

    def sb(name, shape, dt=F32, scope=None):
        return (scope or stack).enter_context(nc.sbuf_tensor(name, shape, dt))

    with stack:
        ps = stack.enter_context(nc.psum_tensor("ps", [P, 8, 512], F32))
        x_dram = nc.dram_tensor("x_scratch", [P, KC, TOK], F32, kind="Internal").ap()
        mix_dram = nc.dram_tensor("mix_scratch", [KC, P, TOK], F32, kind="Internal").ap()
        gate_dram = nc.dram_tensor("gate_scratch", [GROWS, SEQ], F32, kind="Internal").ap()

        ident = sb("ident", [P, P])
        ones = sb("ones", [P, P])
        head_ones = sb("head_ones", [P, 2, P])
        later = sb("later", [P, P])
        causal = sb("causal", [P, P])
        level_mask = sb("level_mask", [P, 7, P])
        norms = sb("norms", [P, KC, 3])
        gconv = sb("gconv", [P, 3 * GH, 28])
        fconv = sb("fconv", [P, FT, 20])
        out_norm = sb("out_norm", [P, 1])
        hi = sb("act_hi", [P, KC, TOK], F32R)
        lo = sb("act_lo", [P, KC, TOK], F32R)
        logf_n = sb("logf_n", [P, NBLK + 1, FH])
        beta_n = sb("beta_n", [P, NBLK, GH])
        gcum_n = sb("gcum_n", [P, NBLK, GH])
        page_ids = sb("page_ids", [1, DEC * PAGES], I32)
        dec_bias = sb("dec_bias", [P, DEC * PAGES, FH])
        dec_gates = sb("dec_gates", [P, 2, GH, DEC])

        v = OnChip(sem, mixer_sem, sb, ps, x_dram, mix_dram, gate_dram, ident, ones, head_ones, later,
                   causal, level_mask, norms, gconv, fconv, out_norm, hi, lo,
                   logf_n, beta_n, gcum_n, page_ids, dec_bias, dec_gates)

        past_loaded = [sem("past_loaded_sync"), sem("past_loaded_gpsimd")]
        setup(nc, t, v, past_loaded)
        with ExitStack() as scope:
            tiles = Tiles(t, v, scope)
            gates(nc, t, v, past_loaded, tiles)
            mixer(nc, t, v, tiles)
        nc.clear_and_free_semaphores(mixer_sems)
        nc.all_engine_barrier()
        dense(nc, t, v)


def split_piece(pe, out, w_hi, w_lo, a_hi, a_lo, first, last):
    pe.matmul(out, w_hi, a_hi, start=first, stop=False)
    pe.matmul(out, w_hi, a_lo, start=False, stop=False)
    return pe.matmul(out, w_lo, a_hi, start=False, stop=last)


def load_pages(eng, v, t, loaded, first, end):
    with eng.Fori(first, end) as n:
        page = eng.value_load(v.page_ids[0:1, ds(n, 1)], min_val=0, max_val=t["cache_logf"].shape[1] - 1)
        eng.dma_start(v.dec_bias[:, ds(n, 1), :].rearrange("p a h -> p (a h)"),
                      t["cache_logf"][0, ds(page, 1)].rearrange("a p h -> p (a h)")).then_inc(loaded, 16)


def setup(nc, t, v, past_loaded):
    with ExitStack() as scope:
        def sb(name, shape, dt=F32):
            return v.sb(name, shape, dt, scope)

        xT = sb("xT0", [P, KC, TOK])
        XS = 4
        xn = sb("x_rows", [P, XS, D])
        vec_rows = sb("vec_rows", [3, D])
        gconv_rows = sb("gconv_rows", [28, 3 * GW])
        fconv_rows = sb("fconv_rows", [20, FFN])
        sq = sb("sq0", [P, 2, KC, P])
        sq_sum = sb("sq_sum0", [P, TOK])
        rstd = sb("rstd0", [P, TOK])
        tmp = sb("h_tmp0", [P, KC, TOK])
        ps = v.ps
        x_loaded = [v.sem(f"x_loaded{i}") for i in range(XS)]
        ident_ready = v.sem("ident_ready")
        params_loaded, consts_ready = v.sem("params_loaded"), v.sem("consts_ready")
        x_turned, x_copied = v.sem("x_turned"), v.sem("x_copied")
        par_turned, par_copied = v.sem("par_turned"), v.sem("par_copied")
        blk_squared, blk_summed = v.sem("blk_squared"), v.sem("blk_summed")
        x_saved, ids_loaded = v.sem("x_saved"), v.sem("ids_loaded")
        S = norm_signals(v, "n0")

        block = scope.enter_context(nc.Block())

        @block.sync
        def _(sp):
            sp.dma_start(v.page_ids[:], t["page_table"].rearrange("b p -> (b p)").rearrange("(a n) -> a n", a=1)).then_inc(ids_loaded, 16)
            sp.dma_start(vec_rows[0:1, :], t["norm_mix"]).then_inc(params_loaded, 16)
            sp.dma_start(vec_rows[1:2, :], t["norm_ffn"]).then_inc(params_loaded, 16)
            sp.dma_start(vec_rows[2:3, :], t["norm_final"].rearrange("(a d) -> a d", a=1)).then_inc(params_loaded, 16)
            sp.dma_start(gconv_rows[0:4, :], t["w_gdn_conv"][0]).then_inc(params_loaded, 16)
            sp.dma_start(gconv_rows[4:28, :], t["state_gdn_conv"][0].rearrange("b i c -> (b i) c")).then_inc(params_loaded, 16)
            sp.dma_start(fconv_rows[0:3, :], t["w_ffn_conv"][0]).then_inc(params_loaded, 16)
            sp.dma_start(fconv_rows[3:4, :], t["b_ffn_conv"]).then_inc(params_loaded, 16)
            sp.dma_start(fconv_rows[4:20, :], t["state_ffn_conv"][0].rearrange("b i c -> (b i) c")).then_inc(params_loaded, 16)
            sp.dma_start(v.out_norm[:], t["gdn_out_norm"].rearrange("a d -> d a")).then_inc(params_loaded, 16)
            sp.wait_ge(ids_loaded, 16)
            load_pages(sp, v, t, past_loaded[0], 0, EARLY_PAGES)

        @block.gpsimd
        def _(pool):
            pool.memset(v.ident[:], 0.0)
            pool.drain()
            pool.affine_select(out=v.ident[:], in_=v.ident[:], compare_op=ALU.not_equal, fill=1.0, base=0,
                               pattern=[[-1, P]], channel_multiplier=1).then_inc(ident_ready, 1)
            pool.memset(v.ones[:], 1.0)
            pool.memset(v.later[:], 1.0)
            pool.memset(v.causal[:], 0.0)
            pool.memset(v.head_ones[:], 0.0)
            pool.memset(v.level_mask[:], 0.0)
            pool.drain()
            pool.memset(v.head_ones[0:FD, 0], 1.0)
            pool.drain()
            pool.memset(v.head_ones[FD:P, 1], 1.0)
            pool.drain()
            for l in range(7):
                b = 1 << l
                m = v.level_mask[:, l].rearrange("p (n w) -> p n w", w=2 * b)
                pool.memset(m[:, :, b:2 * b], 1.0)
            pool.affine_select(out=v.later[:], in_=v.later[:], compare_op=ALU.is_ge, fill=0.0, base=-1,
                               pattern=[[-1, P]], channel_multiplier=1)
            pool.affine_select(out=v.causal[:], in_=v.causal[:], compare_op=ALU.is_ge, fill=NEG_BIG / SCALE, base=0,
                               pattern=[[-1, P]], channel_multiplier=1)
            pool.drain()
            for l in range(7):
                b = 1 << l
                m = v.level_mask[:, l].rearrange("p (n w) -> p n w", w=2 * b)
                n = P // (2 * b)
                pool.affine_select(out=m, in_=m, compare_op=ALU.is_ge, fill=0.0, base=0,
                                   pattern=[[-2 * b, n], [0, 2 * b]], channel_multiplier=1)
                pool.drain()
                pool.affine_select(out=m, in_=m, compare_op=ALU.is_ge, fill=0.0, base=b - 1,
                                   pattern=[[2 * b, n], [0, 2 * b]], channel_multiplier=-1)
            pool.drain()
            pool.drain().then_inc(consts_ready, 1)
            pool.wait_ge(ids_loaded, 16)
            load_pages(pool, v, t, past_loaded[1], EARLY_PAGES, EARLY_PAGES + POOL_PAGES)
            pool.wait_ge(x_copied, NBLK + 1)
            pool.dma_start(v.x_dram, xT[:]).then_inc(x_saved, 16)
            norm_pool(pool, v, S, tmp, ALL_TOKENS)
            pool.wait_ge(x_saved, 16)

        def turn(pe, n, width):
            for k in range(KC):
                mm = pe.transpose(ps[:, 2 * (n % 2) + k // 4, (k % 4) * P:(k % 4) * P + width],
                                  xn[0:width, n % XS, k * P:(k + 1) * P], v.ident[0:width, 0:width])
            mm.then_inc(x_turned, 1)

        @block.tensor
        def _(pe):
            pe.wait_ge(ident_ready, 1)
            for n in range(NBLK + 1):
                pe.wait_ge(x_loaded[n % XS], 16 * (n // XS + 1))
                if n >= 2:
                    pe.wait_ge(x_copied, n - 1)
                turn(pe, n, P if n < NBLK else DEC)
            pe.wait_ge(consts_ready, 1)
            pe.wait_ge(params_loaded, 144)
            for k in range(KC):
                pe.transpose(ps[:, 4, k * 3:k * 3 + 3], vec_rows[0:3, k * P:(k + 1) * P], v.ident[0:3, 0:3])
            for k in range(3 * GH):
                pe.transpose(ps[:, 5, k * 28:k * 28 + 28], gconv_rows[:, k * P:(k + 1) * P], v.ident[0:28, 0:28])
            for k in range(FT):
                mm = pe.transpose(ps[:, 6, k * 20:k * 20 + 20], fconv_rows[:, k * P:(k + 1) * P], v.ident[0:20, 0:20])
            mm.then_inc(par_turned, 1)
            norm_pe(pe, v, S, sq_sum)

        def copy_out(dve, slot, n, cols):
            for half in range(2):
                src = ps[:, 2 * slot + half].rearrange("p (k t) -> p k t", k=4)[:, :, 0:n]
                ins = dve.tensor_copy(xT[:, 4 * half:4 * half + 4, cols], src)
            ins.then_inc(x_copied, 1)

        @block.vector
        def _(dve):
            def sum_squares(n, i, cols, width):
                dve.wait_ge(blk_squared, n + 1)
                dve.tensor_reduce(sq_sum[:, cols], sq[:, i, :, 0:width].rearrange("p k t -> p t k"), AX.X, ALU.add).then_inc(blk_summed, 1)

            with dve.Fori(0, NBLK // 2) as it:
                for i in range(2):
                    dve.wait_ge(x_turned, it * 2 + i + 1)
                    copy_out(dve, i, P, ds((it * 2 + i) * P, P))
                for i in range(2):
                    sum_squares(it * 2 + i, i, ds((it * 2 + i) * P, P), P)
            dve.wait_ge(x_turned, NBLK + 1)
            copy_out(dve, 0, DEC, slice(SEQ, TOK))
            sum_squares(NBLK, 0, slice(SEQ, TOK), DEC)
            dve.drain().then_inc(S["squared"], 1)
            dve.wait_ge(par_turned, 1)
            dve.tensor_copy(v.norms[:].rearrange("p k n -> p (k n)"), ps[:, 4, 0:3 * KC])
            dve.tensor_copy(v.gconv[:].rearrange("p k n -> p (k n)"), ps[:, 5, 0:28 * 3 * GH])
            dve.tensor_copy(v.fconv[:].rearrange("p k n -> p (k n)"), ps[:, 6, 0:20 * FT])
            dve.drain()
            dve.wait_ge(S["rstd"], 1)
            norm_dve(dve, v, S, xT, rstd, tmp, 0, ALL_TOKENS)

        @block.scalar
        def _(act):
            def square(n, i, cols, width):
                act.wait_ge(x_copied, n + 1)
                act.activation(sq[:, i, :, 0:width], xT[:, :, cols], ACT.Square).then_inc(blk_squared, 1)

            def load_x(i, rows):
                act.dma_start(xn[:, i], t["x_prompt"][0, rows]).then_inc(x_loaded[i], 16)

            for n in range(XS):
                load_x(n, slice(n * P, (n + 1) * P))
            for n in range(NBLK + 1):
                if n >= 2:
                    act.wait_ge(blk_summed, n - 1)
                square(n, n % 2, slice(n * P, min((n + 1) * P, TOK)), P if n < NBLK else DEC)
                if n + XS < NBLK:
                    load_x((n + XS) % XS, slice((n + XS) * P, (n + XS + 1) * P))
                elif n + XS == NBLK:
                    act.dma_start(xn[0:DEC, 0], t["x_sample"].rearrange("b a d -> (b a) d")).then_inc(x_loaded[0], 16)
            norm_rstd(act, v, S, rstd)
            norm_hi(act, v, S, tmp, ALL_TOKENS)


def norm_signals(v, name):
    return {k: v.sem(f"{name}_{k}") for k in ("squared", "summed", "rstd", "normed", "hi", "even_lo", "odd_lo")}


def add_squares(dve, x, sq):
    dve.tensor_tensor(sq[:, 0], x, x, ALU.mult)
    dve.drain()
    dve.tensor_tensor(sq[:, 1], sq[:, 1], sq[:, 0], ALU.add)


def norm_rstd(act, v, S, rstd):
    for g in range(NG):
        act.wait_ge(S["summed"], g + 1)
        act.activation(rstd[:, g * GRP:(g + 1) * GRP], v.ps[:, g, 0:GRP], ACT.Ln, scale=1.0 / D, bias=EPS)
    act.drain()
    act.activation(rstd[:], rstd[:], ACT.Exp, scale=-0.5).then_inc(S["rstd"], 1)


ALL_TOKENS = ((0, slice(0, TOK)),)
BY_GROUP = tuple((g, slice(g * GRP, (g + 1) * GRP)) for g in range(NG))


def norm_hi(act, v, S, tmp, ranges):
    for r, cols in ranges:
        for k in range(KC):
            act.wait_ge(S["normed"], r * KC + k + 1)
            act.activation(v.hi[:, k, cols], tmp[:, k, cols], ACT.Copy).then_inc(S["hi"], 1)


def norm_pe(pe, v, S, sq_sum):
    pe.wait_ge(S["squared"], 1)
    for g in range(NG):
        pe.matmul(v.ps[:, g, 0:GRP], v.ones[:], sq_sum[:, g * GRP:(g + 1) * GRP], start=True, stop=True).then_inc(S["summed"], 1)


def norm_dve(dve, v, S, xT, rstd, tmp, which, ranges):
    for r, cols in ranges:
        for k in range(KC + 1):
            if k < KC:
                dve.scalar_tensor_tensor(out=tmp[:, k, cols], in0=xT[:, k, cols], scalar=v.norms[:, k, which:which + 1],
                                         in1=rstd[:, cols], op0=ALU.mult, op1=ALU.mult).then_inc(S["normed"], 1)
            if k % 2:
                dve.wait_ge(S["hi"], r * KC + k)
                ins = dve.tensor_tensor(v.lo[:, k - 1, cols], tmp[:, k - 1, cols], v.hi[:, k - 1, cols].bitcast(F32), ALU.subtract)
        ins.then_inc(S["even_lo"], 1)


def norm_pool(pool, v, S, tmp, ranges):
    for r, cols in ranges:
        for k in range(1, KC, 2):
            pool.wait_ge(S["hi"], r * KC + k + 1)
            ins = pool.tensor_tensor(v.lo[:, k, cols], tmp[:, k, cols], v.hi[:, k, cols].bitcast(F32), ALU.subtract)
        ins.then_inc(S["odd_lo"], 1)




def gates(nc, t, v, past_loaded, tiles):
    with ExitStack() as scope:
        def sb(name, shape, dt=F32):
            return v.sb(name, shape, dt, scope)

        w_raw = sb("wg_raw", [P, KC, FH + 2 * GH])
        w_hi = sb("wg_hi", [P, KC, GROWS], F32R)
        w_lo = sb("wg_lo", [P, KC, GROWS], F32R)
        sign, bias, coef = sb("g_sign", [GROWS, 1]), sb("g_bias", [GROWS, 1]), sb("g_coef", [GROWS, 1])
        y, mag, gate = sb("g_y", [GROWS, TOK]), sb("g_mag", [GROWS, TOK]), sb("g_gate", [GROWS, TOK])
        run, keep = sb("g_run", [GROWS, SEQ]), sb("g_keep", [GROWS, SEQ])
        dsel = sb("dec_sel", [GROWS, P])
        total = sb("dec_total", [P, DEC, FH])
        ps = v.ps
        w_loaded, b_loaded = v.sem("wg_loaded"), v.sem("gbias_loaded")
        prepared, bias_set = v.sem("g_prepared"), v.sem("g_bias_zeroed")
        split_hi, split_lo = v.sem("wg_split_hi"), v.sem("wg_split_lo")
        summed, y_ready, mag_ready = v.sem("g_summed"), v.sem("g_y_ready"), v.sem("g_mag_ready")
        coef_ready, gate_ready, beta_ready = v.sem("g_coef_ready"), v.sem("g_gate_ready"), v.sem("g_beta_ready")
        run_ready, turned, sel_ready = v.sem("g_run_ready"), v.sem("g_turned"), v.sem("g_sel_ready")
        dec_done, gates_out, stored, eg_done, dec_copied = v.sem("g_dec_done"), v.sem("g_gates_out"), v.sem("g_stored"), v.sem("g_eg_done"), v.sem("g_dec_copied")
        w_view = t["w_in"][0].rearrange("(k p) n -> p k n", p=P)
        NPG = DEC * PAGES

        block = scope.enter_context(nc.Block())

        @block.sync
        def _(sp):
            sp.dma_start(w_raw[:, :, 0:FH], w_view[:, :, C_FF:C_FF + FH]).then_inc(w_loaded, 16)
            sp.dma_start(w_raw[:, :, FH:], w_view[:, :, C_GA:C_GA + 2 * GH]).then_inc(w_loaded, 16)
            sp.wait_ge(bias_set, 1)
            sp.dma_start(bias[R_F:R_F + FH, :], t["b_forget"].rearrange("a h -> h a")).then_inc(b_loaded, 16)
            sp.dma_start(bias[R_A:R_A + GH, :], t["gdn_dt_bias"].rearrange("a h -> h a")).then_inc(b_loaded, 16)
            sp.dma_start(coef[R_A:R_A + GH, :], t["gdn_a_log"].rearrange("a h -> h a")).then_inc(b_loaded, 16)
            load_pages(sp, v, t, past_loaded[0], EARLY_PAGES + POOL_PAGES, NPG)
            sp.wait_ge(run_ready, 1)
            sp.dma_start(v.gate_dram, run[:]).then_inc(stored, 16)
            sp.wait_ge(gates_out, 1)
            sp.dma_start(t["new_logf_prompt"][0, 0].rearrange("(c p) h -> p c h", p=P),
                         v.logf_n[:, 0:NBLK]).then_inc(stored, 16)
            sp.dma_start(t["new_logf_sample"][0].rearrange("b a h -> b (a h)"),
                         v.logf_n[0:DEC, NBLK]).then_inc(stored, 16)
            sp.wait_ge(stored, 48)

        @block.gpsimd
        def _(pool):
            pool.sem_inc(tiles.w_split_lo.sem, tiles.w_split_lo.credit)
            pool.memset(bias[:], 0.0)
            pool.memset(coef[:], 0.0)
            pool.drain()
            pool.drain().then_inc(bias_set, 1)
            pool.memset(sign[:], -1.0)
            pool.memset(keep[:], 1.0)
            pool.memset(dsel[:], 0.0)
            pool.drain()
            pool.memset(sign[R_A:R_A + 32, :], 1.0)
            pool.drain()
            pool.memset(keep[R_A:R_A + 32, :].rearrange("p (c i) -> p c i", c=NBLK)[:, :, 0:1], 0.0)
            pool.drain()
            pool.memset(w_hi[:].bitcast(F32), 0.0)
            pool.memset(w_lo[:].bitcast(F32), 0.0)
            pool.drain()
            pool.drain().then_inc(prepared, 1)
            for i in range(5):
                tiles.split_lo(pool, 0, i)

        cols = [(0, FH, R_F), (FH, GH, R_A), (FH + GH, GH, R_B)]

        @block.scalar
        def _(act):
            act.sem_inc(tiles.piece_out.sem, tiles.piece_out.credit)
            for i in range(2):
                tiles.load(act, 0, i)
            act.wait_ge(w_loaded, 32)
            act.wait_ge(prepared, 1)
            for a, n, r in cols:
                ins = act.activation(w_hi[:, :, r:r + n], w_raw[:, :, a:a + n], ACT.Copy)
            ins.then_inc(split_hi, 1)
            for i in range(2):
                tiles.split(act, 0, i)
            act.wait_ge(y_ready, 1)
            act.activation(mag[:], y[:], ACT.Abs)
            act.drain()
            act.activation(mag[:], mag[:], ACT.Exp, scale=-1.0)
            act.wait_ge(b_loaded, 48)
            act.activation(coef[R_A:R_A + 32, :], coef[R_A:R_A + 32, :], ACT.Exp).then_inc(coef_ready, 1)
            act.drain()
            act.activation(mag[:], mag[:], ACT.Ln, bias=1.0).then_inc(mag_ready, 1)
            tiles.evacuate(act, 0, 0)
            tiles.evacuate(act, 0, 1)
            act.wait_ge(gate_ready, 1)
            act.activation(gate[R_B:R_B + 32, :], gate[R_B:R_B + 32, :], ACT.Exp).then_inc(beta_ready, 1)
            tiles.evacuate(act, 0, 2)
            act.wait_ge(dec_copied, 1)
            act.activation(v.dec_gates[:, 0], v.dec_gates[:, 0], ACT.Exp).then_inc(eg_done, 1)
            for q in range(3, FOX_PIECES):
                tiles.evacuate(act, 0, q)

        @block.tensor
        def _(pe):
            pe.sem_inc(tiles.piece_done.sem, tiles.piece_done.credit)
            pe.wait_ge(split_lo, 1)
            for g in range(NG):
                for k in range(KC):
                    mm = split_piece(pe, ps[0:GROWS, 3 + g, 0:GRP], w_hi[:, k], w_lo[:, k],
                                     v.hi[:, k, g * GRP:(g + 1) * GRP], v.lo[:, k, g * GRP:(g + 1) * GRP],
                                     k == 0, k == KC - 1)
            mm.then_inc(summed, 1)
            for q in range(3):
                tiles.project(pe, 0, q)
            pe.wait_ge(past_loaded[0], 16 * (NPG - POOL_PAGES))
            pe.wait_ge(past_loaded[1], 16 * POOL_PAGES)
            past_flat = v.dec_bias[:].rearrange("p n h -> p (n h)")
            pe.matmul(ps[:, 6, 0:512], v.later[:], past_flat, start=True, stop=True)
            pe.matmul(ps[:, 7, 0:512], v.ones[:], past_flat, start=True, stop=True)
            pe.wait_ge(sel_ready, 1)
            pe.matmul(ps[:, 2, 0:P], v.ones[0:GROWS, :], dsel[:], start=True, stop=True).then_inc(dec_done, 1)
            for c in range(NBLK):
                pe.transpose(ps[:, 3 + c // 4, (c % 4) * GROWS:(c % 4 + 1) * GROWS], gate[:, c * P:(c + 1) * P],
                             v.ident[0:GROWS, 0:GROWS])
            pe.transpose(ps[0:DEC, 5, 256:256 + GROWS], gate[:, SEQ:TOK], v.ident[0:GROWS, 0:GROWS])
            ra = slice(R_A, R_A + 32)
            for c in range(NBLK):
                mm = pe.transpose(ps[:, 5, c * 32:(c + 1) * 32], run[ra, c * P:(c + 1) * P], v.ident[ra, ra])
            mm.then_inc(turned, 1)
            for q in range(3, FOX_PIECES):
                tiles.project(pe, 0, q)

        @block.vector
        def _(dve):
            dve.wait_ge(split_hi, 1)
            for a, n, r in cols:
                ins = dve.tensor_tensor(w_lo[:, :, r:r + n], w_raw[:, :, a:a + n], w_hi[:, :, r:r + n].bitcast(F32), ALU.subtract)
            ins.then_inc(split_lo, 1)
            dve.wait_ge(summed, 1)
            dve.wait_ge(b_loaded, 48)
            for g in range(NG):
                ins = dve.tensor_scalar(y[:, g * GRP:(g + 1) * GRP], ps[0:GROWS, 3 + g, 0:GRP], bias[:], sign[:], ALU.add, ALU.mult)
            ins.then_inc(y_ready, 1)
            dve.wait_ge(coef_ready, 1)
            dve.tensor_scalar(coef[R_A:R_A + 32, :], coef[R_A:R_A + 32, :], -1.0, None, ALU.mult)
            dve.memset(coef[R_F:R_F + 32, :], -1.0)
            dve.memset(coef[R_B:R_B + 32, :], -1.0)
            dve.wait_ge(mag_ready, 1)
            dve.scalar_tensor_tensor(out=gate[:], in0=y[:], scalar=0.0, in1=mag[:], op0=ALU.max, op1=ALU.add)
            dve.drain()
            dve.tensor_scalar(gate[:], gate[:], coef[:], None, ALU.mult).then_inc(gate_ready, 1)
            dve.drain()
            dve.tensor_tensor_scan(run[0:64, :], keep[0:64, :], gate[0:64, 0:SEQ], 0.0, ALU.mult, ALU.add)
            dve.wait_ge(beta_ready, 1)
            dve.tensor_copy(run[R_B:R_B + 32, :], gate[R_B:R_B + 32, 0:SEQ])
            dve.drain()
            dve.tensor_scalar(run[R_F:R_F + 32, :], run[R_F:R_F + 32, :], -1.0 / SCALE, None, ALU.mult).then_inc(run_ready, 1)
            for r, n in ((R_F, FH), (R_A, GH), (R_B, GH)):
                g_row = gate[r:r + n, SEQ:TOK]
                if r == R_F:
                    out = dsel[r:r + n, 0:64].rearrange("p (b h) -> p b h", b=DEC)
                    a = g_row.unsqueeze(2).broadcast_to([n, DEC, n])
                    b = v.ident[r:r + n, r:r + n].unsqueeze(1).broadcast_to([n, DEC, n])
                else:
                    at = 64 if r == R_A else 96
                    out = dsel[r:r + n, at:at + 32].rearrange("p (h b) -> p h b", h=GH)
                    a = g_row.unsqueeze(1).broadcast_to([n, GH, DEC])
                    b = v.ident[r:r + n, r:r + n].unsqueeze(2).broadcast_to([n, GH, DEC])
                ins = dve.tensor_tensor(out, a, b, ALU.mult)
            ins.then_inc(sel_ready, 1)
            dve.wait_ge(dec_done, 1)
            dve.tensor_copy(v.dec_gates[:].rearrange("p n h b -> p (n h b)"), ps[:, 2, 64:128]).then_inc(dec_copied, 1)
            dve.tensor_copy(total[:].rearrange("p b h -> p (b h)"), ps[:, 2, 0:64])
            within = ps[:, 6].rearrange("p (b g h) -> p b g h", b=DEC, g=PAGES)
            whole = ps[:, 7].rearrange("p (b g h) -> p b g h", b=DEC, g=PAGES)
            bias_v = v.dec_bias[:].rearrange("p (b g) h -> p b g h", b=DEC)
            for pg in reversed(range(PAGES)):
                dve.drain()
                dve.tensor_tensor(bias_v[:, :, pg, :], total[:], within[:, :, pg, :], ALU.add)
                if pg:
                    dve.drain()
                    dve.tensor_tensor(total[:], total[:], whole[:, :, pg, :], ALU.add)
            dve.wait_ge(turned, 1)
            for half in range(2):
                rows_n = ps[:, 3 + half, 0:4 * GROWS].rearrange("p (c r) -> p c r", c=4)
                dve.tensor_copy(v.logf_n[:, 4 * half:4 * half + 4, :], rows_n[:, :, R_F:R_F + FH])
                dve.tensor_copy(v.beta_n[:, 4 * half:4 * half + 4, :], rows_n[:, :, R_B:R_B + GH])
            dve.tensor_copy(v.gcum_n[:], ps[:, 5, 0:256].rearrange("p (c r) -> p c r", c=NBLK)[:, :, 0:GH])
            dve.tensor_copy(v.logf_n[0:DEC, NBLK, :], ps[0:DEC, 5, 256 + R_F:256 + R_F + FH]).then_inc(gates_out, 1)


class Count:

    def __init__(self, sem, per, credit=0):
        self.sem, self.per, self.credit = sem, per, credit

    def at(self, j, n):
        return j * self.per + (n + self.credit)


FOX_PIECES = 3 * NG


class Tiles:

    def __init__(self, t, v, scope):
        self.v = v
        self.w_raw = v.sb("wm_raw", [P, 2, KC, P], F32, scope)
        self.w_hi = v.sb("wm_hi", [P, 2, KC, P], F32R, scope)
        self.w_lo = v.sb("wm_lo", [P, 2, KC, P], F32R, scope)
        self.qT, self.kT, self.vT = (v.sb(n, [P, TOK], F32, scope) for n in ("qT", "kT", "vT"))
        self.ext = v.sb("gdn_ext", [P, 3, EXT], F32, scope)
        self.z_silu = v.sb("z_silu", [P, TOK], F32, scope)
        self.w_view = t["w_in"][0].rearrange("(k p) n -> p k n", p=P)
        self.w_loaded = [Count(v.mixer_sem("m_w_loaded0"), 64), Count(v.mixer_sem("m_w_loaded1"), 48)]
        self.w_split_hi = Count(v.mixer_sem("m_w_split_hi"), NTILE)
        self.w_split_lo = Count(v.mixer_sem("m_w_split_lo"), NTILE, 2)
        self.piece_done = Count(v.mixer_sem("m_piece_done"), 3 * NTILE, 6)
        self.piece_out = Count(v.mixer_sem("m_piece_out"), 3 * NTILE, 2)

    def load(self, act, j, i, ahead=0):
        act.dma_start(self.w_raw[:, i % 2], self.w_view[:, :, ds((j + ahead) * P + TILE_COL[i], P)]).then_inc(self.w_loaded[i % 2].sem, 16)

    def split(self, act, j, i, ahead=0):
        wait(act, self.w_loaded[i % 2], j, 16 * (i // 2 + 1), ahead)
        wait(act, self.piece_done, j, 3 * max(i - 1, 0), ahead)
        act.activation(self.w_hi[:, i % 2], self.w_raw[:, i % 2], ACT.Copy).then_inc(self.w_split_hi.sem, 1)

    def split_lo(self, pool, j, i, ahead=0):
        wait(pool, self.w_split_hi, j, i + 1, ahead)
        pool.tensor_tensor(self.w_lo[:, i % 2], self.w_raw[:, i % 2], self.w_hi[:, i % 2].bitcast(F32), ALU.subtract).then_inc(self.w_split_lo.sem, 1)

    def project(self, pe, j, q, ahead=0):
        v, i, g = self.v, q // NG, q % NG
        if g == 0:
            wait(pe, self.w_split_lo, j, i + 1, ahead)
        wait(pe, self.piece_out, j, max(q - 1, 0), ahead)
        for k in range(KC):
            mm = split_piece(pe, v.ps[:, q % 2, 0:GRP], self.w_hi[:, i % 2, k], self.w_lo[:, i % 2, k],
                             v.hi[:, k, g * GRP:(g + 1) * GRP], v.lo[:, k, g * GRP:(g + 1) * GRP],
                             k == 0, k == KC - 1)
        mm.then_inc(self.piece_done.sem, 1)

    def evacuate(self, act, j, q, ahead=0, last=False):
        i, g = q // NG, q % NG
        wait(act, self.piece_done, j, q + 1, ahead)
        src, a = self.v.ps[:, q % 2, 0:GRP], g * GRP
        if 3 <= i < 6:
            n = min(GRP, SEQ - a)
            ins = act.activation(self.ext[:, i - 3, TAPS - 1 + a:TAPS - 1 + a + n], src[:, 0:n], ACT.Copy)
            if n < GRP:
                new = self.ext[:, i - 3, TAPS - 1 + SEQ:].rearrange("p (b i) -> p b i", b=DEC)[:, :, TAPS - 1]
                ins = act.activation(new, src[:, n:GRP], ACT.Copy)
            ins.then_inc(self.piece_out.sem, 1)
        else:
            dst = {0: self.qT, 1: self.kT, 2: self.vT, 6: self.z_silu}[i]
            act.activation(dst[:, a:a + GRP], src, ACT.Copy).then_inc(self.piece_out.sem, 1)
        if g == 0 and (i + 2 < NTILE or not last):
            wait(act, self.w_split_lo, j, i + 1, ahead)
            if i + 2 < NTILE:
                self.load(act, j, i + 2, ahead)
            else:
                self.load(act, j, {5: 1, 6: 0}[i], ahead + 1)
        if g == NG - 1 and i + 2 < NTILE:
            self.split(act, j, i + 2, ahead)
        if q == 3 * NTILE - 1 and not last:
            self.split(act, j, 0, ahead + 1)
            self.split(act, j, 1, ahead + 1)


def wait(eng, c, j, n=None, ahead=0):
    eng.wait_ge(c.sem, c.at(j, (c.per if n is None else n) + ahead * c.per))


def mixer(nc, t, v, tiles):
    with ExitStack() as scope:
        def sb(name, shape, dt=F32):
            return v.sb(name, shape, dt, scope)

        ps = v.ps
        qT, kT, vT, ext, z_silu = tiles.qT, tiles.kT, tiles.vT, tiles.ext, tiles.z_silu
        piece_out = tiles.piece_out
        mix = sb("mix", [P, TOK])
        small = sb("mix_small", [P, 640])
        REGION = 7 * CONV + 9 * SEQ
        region = sb("region", [P, REGION])
        at = [0]

        def view(width):
            at[0] += width
            assert at[0] <= REGION
            return region[:, at[0] - width:at[0]]

        def blocks(ap):
            return ap.rearrange("p (c i) -> p c i", i=P)

        def halves(ap, level):
            return ap.rearrange("p (n h w) -> p n h w", h=2, w=1 << level)

        k_nat, v_nat = blocks(view(SEQ)), blocks(view(SEQ))
        q_wide = blocks(z_silu[:, 0:SEQ])
        ck_row = view(2 * SEQ).rearrange("p (h s) -> p h s", h=2)
        ck_diag = view(2 * SEQ).rearrange("p (h s) -> p h s", h=2)
        prob = view(2 * SEQ).rearrange("p (u s) -> p u s", u=2)
        probT = view(2 * SEQ).rearrange("p (u c i) -> p u c i", u=2, i=P)
        o_nat = k_nat
        v_past = view(4 * SEQ).rearrange("p (b g d) -> p b g d", b=4, d=P)
        k_past = view(2 * SEQ).rearrange("p (b g d) -> p b g d", b=2, d=P)
        at[0] = 0
        conv = view(3 * CONV).rearrange("p (y e) -> p y e", y=3)
        rs_qk = view(2 * CONV).rearrange("p (y e) -> p y e", y=2)
        squares = view(2 * CONV).rearrange("p (y e) -> p y e", y=2)
        decayT, k_dec = region[:, 5 * CONV:5 * CONV + SEQ], region[:, 5 * CONV + SEQ:5 * CONV + 2 * SEQ]
        gc_row, beta_row, k_beta, v_beta, aT, qkT, eg_row, k_scaled, s_dec = (view(SEQ) for _ in range(9))
        levelT = [blocks(decayT), blocks(gc_row)]
        inv, invT, z_mat = blocks(k_scaled), blocks(beta_row), blocks(eg_row)
        wT = blocks(conv[:, 1, 0:SEQ])
        oT = rs_qk[:, 1, 0:TOK]
        o_sq, o_rstd = region[:, 5 * CONV:5 * CONV + TOK], region[:, 5 * CONV + 2 * SEQ:5 * CONV + 2 * SEQ + TOK]
        state = sb("state", [P, GD])
        v_new = sb("v_new", [P, 2, GD])

        off = [0]

        def sm(n):
            off[0] += n
            assert off[0] <= 640
            return small[:, off[0] - n:off[0]]

        kv_dec = sb("kv_dec", [DEC, 2, P])
        neg_max, row_sum, row_inv, max_part = sm(16), sm(16), sm(16), sm(16)
        bias_j = sm(2 * DEC * PAGES).rearrange("p (b g h) -> p b g h", b=DEC, g=PAGES)
        score = sm(2 * 64).rearrange("p (b g h) -> p b g h", b=DEC, g=PAGES)
        d_max, d_all, d_self, d_pself, d_den = (sm(2 * DEC).rearrange("p (b h) -> p b h", b=DEC) for _ in range(5))
        qk_self = sm(DEC)
        conv_j = sm(3 * 28).rearrange("p (y n) -> p y n", y=3)
        gs = sm(7 * NBLK).rearrange("p (n c) -> p n c", n=7)
        BETA, GCUM, GLAST, EG, KB, KD, EGL = range(7)
        dg = sm(2 * DEC).rearrange("p (n b) -> p n b", n=2)
        kq = sm(2 * DEC).rearrange("p (b n) -> p b n", n=2)
        kq_dot, kq_prod, delta, d_tmp = sm(DEC), sm(DEC), sm(DEC), sm(DEC)
        tail = sb("conv_tail", [P, 3, TAPS - 1 + DEC])
        tail_rows = sb("conv_tail_rows", [TAPS - 1 + DEC, 3, P])
        nat_dec = v_beta[0:DEC, 0:2 * P].rearrange("p (n d) -> p n d", n=2)
        delta_diag = blocks(k_beta[0:DEC, :])

        C = {}

        def count(name, per, credit=0):
            C[name] = Count(v.mixer_sem("m_" + name), per, credit)
            return C[name]

        nat_turned, nat_out = count("nat_turned", 1), count("nat_out", 1)
        ck_loaded = count("ck_loaded", 16)
        qk_done, scored, expd = count("qk_done", 16), count("scored", 16), count("expd", 16)
        p_turned, p_out_a, p_out_b = count("p_turned", 16), count("p_out_a", 16), count("p_out_b", 8)
        pv_done, pv_out = count("pv_done", 16), count("pv_out", 16)
        o_turned, mix_ready = count("o_turned", 1), count("mix_ready", 1)
        nat_stored = count("nat_stored", 16 * 4)
        k_loaded = [count("kpast_loaded0", 128 * 4), count("kpast_loaded1", 128 * 4)]
        v_loaded = count("vpast_loaded", 512 * 2)
        k_used = count("kpast_used", 8)
        self_ready, self_done, q_wide_done, q_wide_out = count("self_ready", 1), count("self_done", 1), count("q_wide_done", 1), count("q_wide_out", 1)
        dmax_ready, dmax_all, dsub_ready, dexp = count("dmax_ready", 2), count("dmax_all", 2), count("dsub_ready", 2), count("dexp", 2)
        v_weighed, v_summed = count("v_weighed", 2), count("v_summed", 2)
        dself_out, dpv_done, dec_out = count("dself_out", 1), count("dpv_done", 2), count("dec_out", 2)
        mix_stored = count("mix_stored", 32, 16)
        rows_loaded, s_loaded = count("rows_loaded", 32), count("s_loaded", 16)
        tap_done = count("tap_done", 3)
        g_ready, conv_done, conv_silu = count("g_ready", 1), count("conv_done", 3), count("conv_silu", 3)
        tail_ready, tail_turned, tail_out = count("tail_ready", 1), count("tail_turned", 1), count("tail_out", 1)
        tail_stored = count("tail_stored", 32, 16)
        sq_ready, l2_done, l2_rstd, l2_out = count("sq_ready", 1), count("l2_done", 1), count("l2_rstd", 2), count("l2_out", 2)
        dif_ready, dec_exp, dec_masked, eg_row_ready = count("dif_ready", 1), count("dec_exp", 1), count("dec_masked", 1), count("eg_row_ready", 1)
        gs_exp, k_scaled_ready = count("gs_exp", 1), count("k_scaled_ready", 1)
        gnat_turned, gnat_out, kk_done, a_ready = count("gnat_turned", 1), count("gnat_out", 1), count("kk_done", 1), count("a_ready", 1)
        gqk_done, q_ready = count("gqk_done", 1), count("q_ready", 1)
        level_ready, y0_ready, y0_turned, x0_ready = count("level_ready", 7), count("y0_ready", 1), count("y0_turned", 1), count("x0_ready", 1)
        z_done, z_out, xy_done, xy_out = count("z_done", 12), count("z_out", 12), count("xy_done", 12), count("xy_out", 12)
        w_done, w_out_ = count("wT_done", 1), count("wT_out", 1)
        state_zero = count("state_zero", 1)
        vn_done, vn_out = count("vn_done", NBLK), count("vn_out", NBLK)
        oc_done, oc_out, sc_done, sc_out = count("oc_done", NBLK), count("oc_out", NBLK), count("sc_done", NBLK), count("sc_out", NBLK)
        kq_ready, sdec_done, delta_ready, rows_turned = count("kq_ready", 1), count("sdec_done", 1), count("delta_ready", 1), count("rows_turned", 1)
        diag_ready, outer_done, sdec_ready = count("diag_ready", 1), count("outer_done", 1), count("sdec_ready", 1, 1)
        osq_ready, osum_done, orstd_ready, o_ready = count("osq_ready", 1), count("osum_done", 1), count("orstd_ready", 1, 1), count("o_ready", 1)
        state_stored = count("state_stored", 32, 16)
        ctx_copied = v.mixer_sem("ctx_copied")
        credits = {"act": (orstd_ready,),
                   "dve": (mix_stored, tail_stored, state_stored, sdec_ready)}

        def give_credits(eng, name):
            for c in credits[name]:
                eng.sem_inc(c.sem, c.credit)

        def each_step(eng, step):
            with eng.Fori(0, STEPS - 1) as j:
                step(j, False)
            step(STEPS - 1, True)

        passed = {e: v.mixer_sem("m_passed_" + e) for e in ("dve", "pool", "sp")}

        def settle(eng, name):
            eng.sem_inc(passed[name], 1)

        PIECE_AT = (0, 1, 3, 5, 7, 9, 11, 13)
        DEC_SCORE_AT = (1, 2, 4, 6, 10, 12, 14)
        DEC_PV_AT = 9
        NP_ = t["cache_k"].shape[1]
        def weigh(eng, half, sequences):
            for b in sequences:
                vb = v_past[:, b].rearrange("p g (h d) -> p (g h) d", h=2)
                probs = score[:, 4 * half + b].rearrange("p g h -> p (g h)")
                ins = eng.tensor_tensor(vb, vb, probs.unsqueeze(2).broadcast_to([P, 2 * PAGES, FD]), ALU.mult)
            return ins

        def l2_sums(y):
            rest = CONV - 1024
            return ((0, 512, ps[:, 3 + 3 * y]), (512, 512, ps[:, 4 + 3 * y]), (1024, rest, ps[:, 5, y * rest:(y + 1) * rest]))

        block = scope.enter_context(nc.Block())

        @block.sync
        def _(sp):
            sp.dma_start(t["new_gdn_conv_sample"][0, :, 0:2, :], t["state_gdn_conv"][0, :, 1:3, :]).then_inc(ctx_copied, 16)

            def load_past(j, dst, cache, b, loaded, pages):
                for g, page in enumerate(pages):
                    sp.dma_start(dst[:, b, g], cache[0, ds(page, 1)].rearrange("a p h d -> p (a h d)")[:, ds(j * P, P)]).then_inc(loaded.sem, 16)

            def pages(b):
                settle(sp, "sp")
                return [sp.value_load(v.page_ids[0:1, b * PAGES + g:b * PAGES + g + 1], min_val=0, max_val=NP_ - 1)
                        for g in range(PAGES)]

            def load_k(j, b, ids):
                load_past(j, k_past, t["cache_k"], b % 2, k_loaded[b % 2], ids)

            def load_v(j, b, ids):
                load_past(j, v_past, t["cache_v"], b % 4, v_loaded, ids)

            def load_first(j, b):
                if b == 0:
                    sp.dma_start(ck_row, v.gate_dram[ds(R_F + 2 * j, 2), :].unsqueeze(0).broadcast_to([P, 2, SEQ])).then_inc(ck_loaded.sem, 16)
                ids = pages(b)
                load_k(j, b, ids)
                load_v(j, b, ids)

            sp.dma_start(ck_row, v.gate_dram[R_F:R_F + 2, :].unsqueeze(0).broadcast_to([P, 2, SEQ])).then_inc(ck_loaded.sem, 16)
            ids = [pages(0)]
            load_k(0, 0, ids[0])
            ids.append(pages(1))
            load_k(0, 1, ids[1])
            for b in range(2):
                load_v(0, b, ids[b])

            def step(j, last):
                def k_free(b):
                    wait(sp, k_used, j, b - 1)

                early = {}
                for b in range(2, DEC):
                    k_free(b)
                    early[b] = pages(b)
                    load_k(j, b, early[b])
                    if b == 4:
                        continue
                    if b == 5:
                        wait(sp, dpv_done, j, 1)
                        settle(sp, "sp")
                        load_v(j, 4, early[4])
                    load_v(j, b, early[b])
                wait(sp, mix_ready, j)
                settle(sp, "sp")
                sp.dma_start(gc_row, v.gate_dram[ds(R_A + j, 1), :].broadcast_to([P, SEQ])).then_inc(rows_loaded.sem, 16)
                sp.dma_start(beta_row, v.gate_dram[ds(R_B + j, 1), :].broadcast_to([P, SEQ])).then_inc(rows_loaded.sem, 16)
                wait(sp, dec_out, j)
                settle(sp, "sp")
                sp.dma_start(blocks(s_dec), t["state_gdn"][0, :, ds(j, 1)].rearrange("b a k e -> k (b a) e")).then_inc(s_loaded.sem, 16)
                sp.dma_start(v.mix_dram[ds(j, 1)].rearrange("a p n -> p (a n)"), mix[:]).then_inc(mix_stored.sem, 16)
                wait(sp, tail_out, j)
                settle(sp, "sp")
                tp = t["new_gdn_conv_prompt"][0, 0].rearrange("i (y n) -> i y n", y=3)
                ts = t["new_gdn_conv_sample"][0, :, TAPS - 2, :].rearrange("b (y n) -> b y n", y=3)
                sp.dma_start(tp[:, :, ds(j * P, P)], tail_rows[0:3]).then_inc(tail_stored.sem, 16)
                sp.dma_start(ts[:, :, ds(j * P, P)], tail_rows[3:3 + DEC]).then_inc(tail_stored.sem, 16)
                wait(sp, sc_out, j)
                sp.dma_start(t["new_gdn_prompt"][0, 0, ds(j, 1)].rearrange("a k e -> k (a e)"), state[:]).then_inc(state_stored.sem, 16)
                wait(sp, sdec_ready, j)
                sp.dma_start(t["new_gdn_sample"][0, :, ds(j, 1)].rearrange("b a k e -> k (b a) e"), blocks(s_dec)).then_inc(state_stored.sem, 16)
                if not last:
                    settle(sp, "sp")
                    load_first(j + 1, 0)
                if not last:
                    wait(sp, state_stored, j)
                    load_first(j + 1, 1)

            each_step(sp, step)
            sp.wait_ge(ctx_copied, 16)

        @block.tensor
        def _(pe):

            def step(j, last):
                def project_next(q):
                    if not last:
                        tiles.project(pe, j, q, 1)

                wait(pe, piece_out, j, 9)
                wait(pe, sdec_ready, j, 0)
                for b in range(DEC):
                    mm = pe.matmul(ps[:, b // 4, (b % 4) * P:(b % 4 + 1) * P], qT[:, SEQ + b:SEQ + b + 1].broadcast_to([P, P]), v.ident[:], start=True, stop=True)
                mm.then_inc(q_wide_done.sem, 1)
                wait(pe, self_ready, j)
                for h in range(2):
                    mm = pe.matmul(ps[:, 2, DEC * h:DEC * (h + 1)], v.head_ones[:, h], qk_self, start=True, stop=True)
                mm.then_inc(self_done.sem, 1)
                wait(pe, orstd_ready, j, 0)
                for src, bank in ((kT, 3), (vT, 5)):
                    for c in range(NBLK):
                        pe.transpose(ps[:, bank + c // 4, (c % 4) * P:(c % 4 + 1) * P], src[:, c * P:(c + 1) * P], v.ident[:])
                pe.transpose(ps[0:DEC, 7, 0:P], kT[:, SEQ:TOK], v.ident[:])
                pe.transpose(ps[0:DEC, 7, P:2 * P], vT[:, SEQ:TOK], v.ident[:]).then_inc(nat_turned.sem, 1)
                wait(pe, q_wide_out, j)
                tiles.project(pe, j, FOX_PIECES)
                wait(pe, nat_out, j)

                def scores(u):
                    h, i = u // NBLK, u % NBLK
                    if u:
                        wait(pe, scored, j, u)
                    rows = slice(h * FD, (h + 1) * FD)
                    n = (i + 1) * P
                    for a in range(0, n, 512):
                        b = min(n, a + 512)
                        mm = pe.matmul(ps[:, 3 + a // 512, 0:b - a], qT[rows, i * P:(i + 1) * P], kT[rows, a:b], start=True, stop=True)
                    mm.then_inc(qk_done.sem, 1)

                def turn_probs(u):
                    i = u % NBLK
                    wait(pe, expd, j, u + 1)
                    if u:
                        wait(pe, p_out_a, j, u)
                        if (u - 1) % NBLK >= 4:
                            wait(pe, p_out_b, j, 4 * ((u - 1) // NBLK) + (u - 1) % NBLK - 3)
                    for c in range(i + 1):
                        mm = pe.transpose(ps[:, 5 + c // 4, (c % 4) * P:(c % 4 + 1) * P], prob[:, u % 2, c * P:(c + 1) * P], v.ident[:])
                    mm.then_inc(p_turned.sem, 1)

                def weigh_values(u):
                    h, i = u // NBLK, u % NBLK
                    wait(pe, p_out_a, j, u + 1)
                    if i >= 4:
                        wait(pe, p_out_b, j, 4 * h + i - 3)
                    if u:
                        wait(pe, pv_out, j, u)
                    for c in range(i + 1):
                        mm = pe.matmul(ps[:, 7, 0:FD], probT[:, u % 2, c], v_nat[:, c, h * FD:(h + 1) * FD],
                                       start=(c == 0), stop=(c == i))
                    mm.then_inc(pv_done.sem, 1)

                def dec_values(half):
                    wait(pe, dexp, j, half + 1)
                    if half:
                        wait(pe, dec_out, j, half)
                    else:
                        wait(pe, dself_out, j)
                    r = slice(4 * half, 4 * half + 4)
                    pe.matmul(ps[:, 2, 0:64], v.ones[:], score[:, r].rearrange("p b g h -> p (b g h)"), start=True, stop=True)
                    wait(pe, v_summed, j, half + 1)
                    for b in range(4):
                        mm = pe.matmul(ps[:, 2, 64 + b:65 + b], v_past[:, b, 0], v.ones[:, 0:1], start=True, stop=True)
                    mm.then_inc(dpv_done.sem, 1)

                for u in range(-1, 2 * NBLK + 1):
                    if u + 1 < 2 * NBLK:
                        scores(u + 1)
                    if u in PIECE_AT:
                        tiles.project(pe, j, FOX_PIECES + 1 + PIECE_AT.index(u))
                    if 0 <= u < 2 * NBLK:
                        turn_probs(u)
                    if u >= 1:
                        weigh_values(u - 1)
                    if u == DEC_PV_AT + 1:
                        dec_values(0)
                wait(pe, pv_out, j)
                for c in range(NBLK):
                    mm = pe.transpose(ps[:, 3 + c // 4, (c % 4) * P:(c % 4 + 1) * P], o_nat[:, c], v.ident[:])
                mm.then_inc(o_turned.sem, 1)
                tiles.project(pe, j, 18)
                tiles.project(pe, j, 19)
                tiles.project(pe, j, 20)
                wait(pe, tail_ready, j)
                for y in range(3):
                    mm = pe.transpose(ps[0:TAPS - 1 + DEC, 7, y * P:(y + 1) * P], tail[:, y], v.ident[:])
                mm.then_inc(tail_turned.sem, 1)
                wait(pe, tail_out, j)
                wait(pe, sq_ready, j)
                for y in range(2):
                    for a, w, out in l2_sums(y):
                        mm = pe.matmul(out, v.ones[:], squares[:, y, a:a + w], start=True, stop=True)
                mm.then_inc(l2_done.sem, 1)
                project_next(0)
                dec_values(1)
                project_next(1)
                wait(pe, l2_rstd, j, 1)
                for y, bank in ((2, 4), (1, 2)):
                    if y == 1:
                        wait(pe, dec_out, j)
                        wait(pe, l2_out, j, 1)
                    for c in range(NBLK):
                        mm = pe.transpose(ps[:, bank + c // 4, (c % 4) * P:(c % 4 + 1) * P], conv[:, y, c * P:(c + 1) * P], v.ident[:])
                mm.then_inc(gnat_turned.sem, 1)
                qn, kn = blocks(conv[:, 0, 0:SEQ]), blocks(conv[:, 1, 0:SEQ])

                def per_chunk(bank, lhs, rhs):
                    for c in range(NBLK):
                        mm = pe.matmul(ps[:, bank + c // 4, (c % 4) * P:(c % 4 + 1) * P], lhs[:, c], rhs[:, c], start=True, stop=True)
                    return mm

                wait(pe, k_scaled_ready, j)
                per_chunk(6, kn, blocks(k_scaled)).then_inc(kk_done.sem, 1)
                project_next(2)
                wait(pe, gnat_out, j)
                wait(pe, l2_out, j)
                per_chunk(2, kn, qn).then_inc(gqk_done.sem, 1)
                project_next(3)
                wait(pe, y0_ready, j)
                for c in range(NBLK):
                    mm = pe.transpose(ps[:, 4 + c // 4, (c % 4) * P:(c % 4 + 1) * P], invT[:, c], v.ident[:])
                mm.then_inc(y0_turned.sem, 1)
                wait(pe, x0_ready, j)
                wait(pe, q_ready, j)
                for l in range(1, 7):
                    for hf in range(2):
                        n = 2 * (l - 1) + hf
                        wait(pe, level_ready, j, l + 1)
                        if l > 1:
                            wait(pe, xy_out, j, n - 1)
                        for c in range(4 * hf, 4 * hf + 4):
                            mm = pe.matmul(ps[:, 2 + hf, (c % 4) * P:(c % 4 + 1) * P], levelT[l % 2][:, c], inv[:, c], start=True, stop=True)
                        mm.then_inc(z_done.sem, 1)
                    if l in (2, 4):
                        project_next(3 + l // 2)
                    for hf in range(2):
                        n = 2 * (l - 1) + hf
                        wait(pe, z_out, j, n + 1)
                        if l < 6:
                            for c in range(4 * hf, 4 * hf + 4):
                                pe.matmul(ps[:, 4 + hf, (c % 4) * P // 2:(c % 4 + 1) * P // 2], invT[:, c], halves(z_mat[:, c], l)[:, :, 0], start=True, stop=True)
                        for c in range(4 * hf, 4 * hf + 4):
                            mm = pe.matmul(ps[:, 6 + hf, (c % 4) * P // 2:(c % 4 + 1) * P // 2], z_mat[:, c], halves(invT[:, c], l)[:, :, 1], start=True, stop=True)
                        mm.then_inc(xy_done.sem, 1)
                wait(pe, xy_out, j)
                per_chunk(2, blocks(k_beta), invT).then_inc(w_done.sem, 1)
                wait(pe, w_out_, j)
                wait(pe, state_zero, j)
                qd = qn
                for c in range(NBLK):
                    if c:
                        wait(pe, vn_out, j, c)
                    pe.matmul(ps[:, 4, 0:GD], invT[:, c], blocks(v_beta)[:, c], start=True, stop=False)
                    if c:
                        wait(pe, sc_out, j, c)
                    pe.matmul(ps[:, 4, 0:GD], wT[:, c], state[:], start=False, stop=True).then_inc(vn_done.sem, 1)
                    if c >= 2:
                        wait(pe, oc_out, j, c - 1)
                    pe.matmul(ps[:, 6 + c % 2, 0:P], state[:], qd[:, c], start=True, stop=False)
                    wait(pe, vn_out, j, c + 1)
                    pe.matmul(ps[:, 2 + c % 2, 0:GD], blocks(k_dec)[:, c], v_new[:, c % 2], start=True, stop=True).then_inc(sc_done.sem, 1)
                    pe.matmul(ps[:, 6 + c % 2, 0:P], v_new[:, c % 2], blocks(qkT)[:, c], start=False, stop=True).then_inc(oc_done.sem, 1)
                    if c == 3:
                        project_next(6)
                wait(pe, kq_ready, j)
                wait(pe, vn_out, j)
                wait(pe, sc_out, j)
                for b in range(DEC):
                    pe.matmul(ps[:, 4, 2 * b:2 * b + 2], blocks(s_dec)[:, b], kq[:, b], start=True, stop=True)
                pe.matmul(ps[:, 5, 0:DEC], v.ones[:], kq_prod, start=True, stop=True).then_inc(sdec_done.sem, 1)
                project_next(7)
                wait(pe, delta_ready, j)
                pe.transpose(ps[0:DEC, 4, 0:P], kq[:, :, 0], v.ident[:])
                pe.transpose(ps[0:DEC, 4, P:2 * P], delta, v.ident[:]).then_inc(rows_turned.sem, 1)
                wait(pe, diag_ready, j)
                for hf in range(2):
                    mm = pe.matmul(ps[:, 2 + hf, 0:512], nat_dec[:, 0], delta_diag[:, 4 * hf:4 * hf + 4].rearrange("q b e -> q (b e)"), start=True, stop=True)
                mm.then_inc(outer_done.sem, 1)
                wait(pe, osq_ready, j)
                for g in range(NG):
                    mm = pe.matmul(ps[:, 5 + g, 0:GRP], v.ones[:], o_sq[:, g * GRP:(g + 1) * GRP], start=True, stop=True)
                mm.then_inc(osum_done.sem, 1)
                project_next(8)

            each_step(pe, step)

        @block.scalar
        def _(act):
            give_credits(act, "act")

            def step(j, last):
                def evacuate_next(q):
                    if not last:
                        tiles.evacuate(act, j, q, 1)

                wait(act, q_wide_done, j)
                for hf in range(2):
                    ins = act.activation(q_wide[:, 4 * hf:4 * hf + 4], ps[:, hf].rearrange("p (c i) -> p c i", c=4), ACT.Copy)
                ins.then_inc(q_wide_out.sem, 1)
                tiles.evacuate(act, j, FOX_PIECES, 0, last)
                wait(act, nat_out, j)
                kp, vp = (t[n][0, 0].rearrange("(c p) h d -> p c (h d)", p=P) for n in ("new_k_prompt", "new_v_prompt"))
                ks, vs = (t[n][0].rearrange("b a h d -> b (a h d)") for n in ("new_k_sample", "new_v_sample"))
                act.dma_start(kp[:, :, ds(j * P, P)], k_nat).then_inc(nat_stored.sem, 16)
                act.dma_start(vp[:, :, ds(j * P, P)], v_nat).then_inc(nat_stored.sem, 16)
                act.dma_start(ks[:, ds(j * P, P)], kv_dec[:, 0]).then_inc(nat_stored.sem, 16)
                act.dma_start(vs[:, ds(j * P, P)], kv_dec[:, 1]).then_inc(nat_stored.sem, 16)

                def exp_scores(u):
                    wait(act, scored, j, u + 1)
                    p = prob[:, u % 2, 0:(u % NBLK + 1) * P]
                    act.activation(p, p, ACT.Exp, bias=neg_max[:, u:u + 1], scale=-1.0,
                                   accum_out=row_sum[:, u:u + 1]).then_inc(expd.sem, 1)

                def probs_out(u):
                    n = min(4, u % NBLK + 1)
                    wait(act, p_turned, j, u + 1)
                    if u >= 2:
                        wait(act, pv_done, j, u - 1)
                    act.activation(probT[:, u % 2, 0:n], ps[:, 5, 0:n * P].rearrange("p (c i) -> p c i", c=n), ACT.Copy).then_inc(p_out_a.sem, 1)

                def exp_decode(half):
                    r = slice(4 * half, 4 * half + 4)
                    wait(act, dsub_ready, j, half + 1)
                    act.activation(score[:, r], score[:, r], ACT.Exp)
                    act.activation(d_pself[:, r], d_self[:, r], ACT.Exp).then_inc(dexp.sem, 1)

                for u in range(-1, 2 * NBLK):
                    if u + 1 < 2 * NBLK:
                        exp_scores(u + 1)
                    if u in PIECE_AT:
                        tiles.evacuate(act, j, FOX_PIECES + 1 + PIECE_AT.index(u), 0, last)
                    if u >= 0:
                        probs_out(u)
                    if u == DEC_PV_AT - 1:
                        exp_decode(0)
                wait(act, o_turned, j)
                wait(act, tail_ready, j)
                for y in range(3):
                    act.activation(conv[:, y], ext[:, y, 0:CONV], ACT.Copy, scale=conv_j[:, y, 0:1]).then_inc(tap_done.sem, 1)
                wait(act, k_used, j)
                tiles.evacuate(act, j, 18, 0, last)
                tiles.evacuate(act, j, 19, 0, last)
                exp_decode(1)
                for y in range(3):
                    wait(act, conv_done, j, y + 1)
                    act.activation(conv[:, y], conv[:, y], ACT.Silu).then_inc(conv_silu.sem, 1)
                    if y == 0:
                        tiles.evacuate(act, j, 20, 0, last)
                    act.drain()
                    if y < 2:
                        ins = act.activation(squares[:, y], conv[:, y], ACT.Square)
                    if y == 1:
                        ins.then_inc(sq_ready.sem, 1)
                act.activation(z_silu[:], z_silu[:], ACT.Silu)
                wait(act, l2_done, j)
                for y in range(2):
                    for a, w, sums in l2_sums(y):
                        act.activation(rs_qk[:, y, a:a + w], sums, ACT.Ln, bias=EPS)
                act.drain()
                act.activation(rs_qk[:, 1], rs_qk[:, 1], ACT.Exp, scale=-0.5).then_inc(l2_rstd.sem, 1)
                act.activation(rs_qk[:, 0], rs_qk[:, 0], ACT.Exp, scale=-0.5, bias=LN_GSCALE).then_inc(l2_rstd.sem, 1)
                wait(act, rows_loaded, j)
                wait(act, dec_out, j)
                act.activation(eg_row, gc_row, ACT.Exp).then_inc(eg_row_ready.sem, 1)
                evacuate_next(0)
                wait(act, g_ready, j)
                act.activation(gs[:, EG], gs[:, GCUM], ACT.Exp)
                act.activation(gs[:, KD], gs[:, KD], ACT.Exp)
                act.activation(gs[:, EGL], gs[:, GLAST], ACT.Exp).then_inc(gs_exp.sem, 1)
                evacuate_next(1)
                wait(act, dif_ready, j)
                act.activation(decayT, decayT, ACT.Exp).then_inc(dec_exp.sem, 1)
                evacuate_next(2)
                evacuate_next(3)
                for n in range(12):
                    hf = n % 2
                    wait(act, z_done, j, n + 1)
                    if n >= 2:
                        wait(act, xy_done, j, n - 1)
                    act.activation(z_mat[:, 4 * hf:4 * hf + 4], ps[:, 2 + hf].rearrange("p (c i) -> p c i", c=4), ACT.Copy).then_inc(z_out.sem, 1)
                    if n in (3, 7):
                        evacuate_next(4 + n // 4)
                for c in range(NBLK):
                    wait(act, vn_done, j, c + 1)
                    if c >= 2:
                        wait(act, oc_done, j, c - 1)
                    act.activation(v_new[:, c % 2], ps[:, 4, 0:GD], ACT.Copy).then_inc(vn_out.sem, 1)
                    wait(act, oc_done, j, c + 1)
                    act.activation(oT[:, c * P:(c + 1) * P], ps[:, 6 + c % 2, 0:P], ACT.Copy).then_inc(oc_out.sem, 1)
                    if c == 3:
                        evacuate_next(6)
                evacuate_next(7)
                act.drain()
                wait(act, delta_ready, j)
                act.activation(o_sq, oT, ACT.Square).then_inc(osq_ready.sem, 1)
                wait(act, osum_done, j)
                for g in range(NG):
                    act.activation(o_rstd[:, g * GRP:(g + 1) * GRP], ps[:, 5 + g, 0:GRP], ACT.Ln, scale=1.0 / GD, bias=EPS)
                act.drain()
                act.activation(o_rstd, o_rstd, ACT.Exp, scale=-0.5).then_inc(orstd_ready.sem, 1)
                evacuate_next(8)
                wait(act, o_ready, j)
                act.dma_start(v.mix_dram[ds(GH + j, 1)].rearrange("a p n -> p (a n)"), oT).then_inc(mix_stored.sem, 16)

            each_step(act, step)

        @block.gpsimd
        def _(pool):
            pool.memset(ext[:, :, 0:TAPS - 1], 0.0)
            pool.drain()

            def step(j, last):
                def split_next(i):
                    if not last:
                        tiles.split_lo(pool, j, i, 1)

                tiles.split_lo(pool, j, 5)
                for half in range(2):
                    r = slice(4 * half, 4 * half + 4)
                    wait(pool, dmax_ready, j, half + 1)
                    settle(pool, "pool")
                    pool.partition_all_reduce(d_all[:, r].rearrange("p b h -> p (b h)"), d_max[:, r].rearrange("p b h -> p (b h)"), P, RMAX).then_inc(dmax_all.sem, 1)
                    wait(pool, dexp, j, half + 1)
                    wait(pool, v_loaded, j, 512 * (half + 1))
                    weigh(pool, half, range(4)).then_inc(v_weighed.sem, 1)
                    if half == 0:
                        tiles.split_lo(pool, j, 6)
                split_next(0)
                split_next(1)
                wait(pool, dec_exp, j)
                settle(pool, "pool")
                pool.affine_select(out=blocks(decayT), in_=blocks(decayT), compare_op=ALU.is_ge, fill=0.0, base=0,
                                   pattern=[[0, NBLK], [1, P]], channel_multiplier=-1).then_inc(dec_masked.sem, 1)
                for l in range(7):
                    if l == 0:
                        wait(pool, a_ready, j)
                        wait(pool, q_ready, j)
                    if l == 2:
                        wait(pool, y0_ready, j)
                    if l >= 3:
                        wait(pool, z_done, j, 2 * (l - 2))
                    pool.tensor_tensor(levelT[l % 2], blocks(aT), v.level_mask[:, l].unsqueeze(1).broadcast_to([P, NBLK, P]),
                                       ALU.mult).then_inc(level_ready.sem, 1)
                    if l == 1:
                        split_next(2)
                split_next(3)
                split_next(4)

            each_step(pool, step)

        @block.vector
        def _(dve):
            give_credits(dve, "dve")

            def step(j, last):
                wait(dve, piece_out, j, 9)
                dve.tensor_tensor(qk_self, qT[:, SEQ:TOK], kT[:, SEQ:TOK], ALU.mult).then_inc(self_ready.sem, 1)
                dve.tensor_copy(bias_j, v.dec_bias[:].rearrange("p (b g) h -> p b g h", b=DEC)[:, :, :, ds(2 * j, 2)])
                dve.tensor_copy(conv_j.unsqueeze(2), v.gconv[:].rearrange("p (y h) n -> p y h n", y=3)[:, :, ds(j, 1), :])
                dve.tensor_copy(dg.unsqueeze(2), v.dec_gates[:, :, ds(j, 1), :])
                dve.tensor_copy(gs[:, BETA].unsqueeze(2), v.beta_n[:, :, ds(j, 1)])
                dve.tensor_copy(gs[:, GCUM].unsqueeze(2), v.gcum_n[:, :, ds(j, 1)])
                wait(dve, nat_turned, j)
                for dst, bank in ((k_nat, 3), (v_nat, 5)):
                    for hf in range(2):
                        dve.tensor_copy(dst[:, 4 * hf:4 * hf + 4], ps[:, bank + hf].rearrange("p (c i) -> p c i", c=4))
                dve.tensor_copy(kv_dec[:].rearrange("p n d -> p (n d)"), ps[0:DEC, 7, 0:2 * P]).then_inc(nat_out.sem, 1)
                wait(dve, ck_loaded, j)
                wait(dve, mix_stored, j, 0)
                dve.tensor_tensor(ck_diag.rearrange("p h (c s) -> p (h c) s", c=NBLK),
                                  ck_row.rearrange("p h (c s) -> p (h c) s", c=NBLK),
                                  v.causal[:].unsqueeze(1).broadcast_to([P, 2 * NBLK, P]), ALU.add)
                wait(dve, self_done, j)
                dve.tensor_scalar(d_self, ps[:, 2, 0:2 * DEC].rearrange("p (h b) -> p b h", h=2), SCALE, None, ALU.mult).then_inc(dself_out.sem, 1)
                dve.drain()

                def score_unit(u):
                    h, i = u // NBLK, u % NBLK
                    wait(dve, qk_done, j, u + 1)
                    if u >= 2:
                        wait(dve, p_turned, j, u - 1)
                    settle(dve, "dve")
                    first = -NEG_BIG
                    if i:
                        dve.tensor_tensor_reduce(out=prob[:, u % 2, 0:i * P], in0=ps[:, 3:5].rearrange("p a n -> p (a n)")[:, 0:i * P],
                                                 in1=ck_row[:, h, 0:i * P], scale=-SCALE, scalar=-NEG_BIG, op0=ALU.add,
                                                 op1=ALU.min, accum_out=max_part[:, u:u + 1])
                        dve.drain()
                        first = max_part[:, u:u + 1]
                    dve.tensor_tensor_reduce(out=prob[:, u % 2, i * P:(i + 1) * P], in0=ps[:, 3 + i // 4, (i % 4) * P:(i % 4 + 1) * P],
                                             in1=ck_diag[:, h, i * P:(i + 1) * P], scale=-SCALE, scalar=first, op0=ALU.add,
                                             op1=ALU.min, accum_out=neg_max[:, u:u + 1]).then_inc(scored.sem, 1)

                def probs_out(u):
                    i = u % NBLK
                    if i < 4:
                        return
                    wait(dve, p_turned, j, u + 1)
                    if u >= 2:
                        wait(dve, pv_done, j, u - 1)
                    n = i - 3
                    dve.tensor_copy(probT[:, u % 2, 4:4 + n], ps[:, 6, 0:n * P].rearrange("p (c i) -> p c i", c=n)).then_inc(p_out_b.sem, 1)

                def unit_out(u):
                    h, i = u // NBLK, u % NBLK
                    wait(dve, expd, j, u + 1)
                    if u == 0:
                        wait(dve, nat_stored, j)
                    dve.reciprocal(row_inv[:, u:u + 1], row_sum[:, u:u + 1])
                    dve.drain()
                    wait(dve, pv_done, j, u + 1)
                    dve.tensor_scalar(o_nat[:, i, h * FD:(h + 1) * FD], ps[:, 7, 0:FD], row_inv[:, u:u + 1], None,
                                      ALU.mult).then_inc(pv_out.sem, 1)

                def dec_score(b):
                    if b == 0:
                        wait(dve, q_wide_out, j)
                    wait(dve, k_loaded[b % 2], j, 128 * (b // 2 + 1))
                    k = k_past[:, b % 2]
                    dve.tensor_tensor(k, k, q_wide[:, b:b + 1].broadcast_to([P, PAGES, P]), ALU.mult)
                    dve.drain()
                    dve.tensor_reduce(score[:, b].rearrange("p g h -> p (g h)"), k.rearrange("p g (h d) -> p (g h) d", h=2), AX.X, ALU.add).then_inc(k_used.sem, 1)

                def dec_max(half):
                    r = slice(4 * half, 4 * half + 4)
                    dve.drain()
                    s = score[:, r].rearrange("p b g h -> p (b g) h")
                    dve.scalar_tensor_tensor(out=s, in0=s, scalar=SCALE, in1=bias_j[:, r].rearrange("p b g h -> p (b g) h"), op0=ALU.mult, op1=ALU.add)
                    dve.drain()
                    dve.tensor_reduce(d_max[:, r], score[:, r].rearrange("p b g h -> p b h g"), AX.X, ALU.max).then_inc(dmax_ready.sem, 1)

                def dec_less_max(half):
                    r = slice(4 * half, 4 * half + 4)
                    wait(dve, dmax_all, j, half + 1)
                    dve.tensor_tensor(d_max[:, r], d_all[:, r], d_self[:, r], ALU.max)
                    dve.drain()
                    dve.tensor_tensor(score[:, r], score[:, r], d_max[:, r].unsqueeze(2).broadcast_to([P, 4, PAGES, 2]), ALU.subtract)
                    dve.tensor_tensor(d_self[:, r], d_self[:, r], d_max[:, r], ALU.subtract).then_inc(dsub_ready.sem, 1)

                def dec_sum_pages(half):
                    wait(dve, v_weighed, j, half + 1)
                    for n in (4, 2, 1):
                        ins = dve.tensor_tensor(v_past[:, :, 0:n], v_past[:, :, 0:n], v_past[:, :, n:2 * n], ALU.add)
                        if n > 1:
                            dve.drain()
                    ins.then_inc(v_summed.sem, 1)

                def dec_result(half):
                    r4 = slice(4 * half, 4 * half + 4)
                    wait(dve, dpv_done, j, half + 1)
                    dve.tensor_reduce(d_den[:, r4], ps[:, 2, 0:64].rearrange("p (b g h) -> p b h g", b=4, g=PAGES), AX.X, ALU.add)
                    dve.drain()
                    dve.tensor_tensor(d_den[:, r4], d_den[:, r4], d_pself[:, r4], ALU.add)
                    dve.drain()
                    dve.reciprocal(d_den[:, r4], d_den[:, r4])
                    for h in range(2):
                        r = slice(h * FD, (h + 1) * FD)
                        cols = slice(SEQ + 4 * half, SEQ + 4 * half + 4)
                        dve.drain()
                        dve.tensor_tensor(d_tmp[r, 0:4], vT[r, cols], d_pself[r, r4, h], ALU.mult)
                        dve.drain()
                        dve.tensor_tensor(d_tmp[r, 0:4], d_tmp[r, 0:4], ps[r, 2, 64:68], ALU.add)
                        dve.drain()
                        ins = dve.tensor_tensor(mix[r, cols], d_tmp[r, 0:4], d_den[r, r4, h], ALU.mult)
                    ins.then_inc(dec_out.sem, 1)

                for u in range(-1, 2 * NBLK + 1):
                    if u + 1 < 2 * NBLK:
                        score_unit(u + 1)
                    if 0 <= u < 2 * NBLK:
                        probs_out(u)
                    if u >= 1:
                        unit_out(u - 1)
                    if u in DEC_SCORE_AT:
                        dec_score(DEC_SCORE_AT.index(u))
                    if u == DEC_SCORE_AT[3]:
                        dec_max(0)
                    if u == DEC_PV_AT - 2:
                        dec_less_max(0)
                    if u == DEC_PV_AT:
                        dec_sum_pages(0)
                    if u == DEC_PV_AT + 1:
                        dec_result(0)
                wait(dve, piece_out, j, 18)
                dve.tensor_copy(ext[:, :, TAPS - 1 + SEQ:].rearrange("p y (b i) -> p y b i", b=DEC)[:, 0, :, 0:3],
                                conv_j[:, 0, 4:28].rearrange("p (b i) -> p b i", b=DEC))
                for y in range(1, 3):
                    dve.tensor_copy(ext[:, y, TAPS - 1 + SEQ:].rearrange("p (b i) -> p b i", b=DEC)[:, :, 0:3],
                                    conv_j[:, y, 4:28].rearrange("p (b i) -> p b i", b=DEC))
                dve.tensor_copy(tail[:, :, 0:3], ext[:, :, SEQ:SEQ + 3])
                for y in range(3):
                    ins = dve.tensor_copy(tail[:, y, 3:3 + DEC], ext[:, y, TAPS - 1 + SEQ:].rearrange("p (b i) -> p b i", b=DEC)[:, :, TAPS - 1])
                ins.then_inc(tail_ready.sem, 1)
                wait(dve, o_turned, j)
                for hf in range(2):
                    ins = dve.tensor_copy(mix[:, 512 * hf:512 * (hf + 1)], ps[:, 3 + hf])
                ins.then_inc(mix_ready.sem, 1)
                for b in range(len(DEC_SCORE_AT), DEC):
                    dec_score(b)
                dec_max(1)
                dve.drain()
                for y in range(3):
                    if y == 1:
                        dec_less_max(1)
                    wait(dve, tap_done, j, y + 1)
                    for i in range(1, TAPS):
                        if i > 1:
                            dve.drain()
                        ins = dve.scalar_tensor_tensor(out=conv[:, y], in0=ext[:, y, i:i + CONV], scalar=conv_j[:, y, i:i + 1], in1=conv[:, y],
                                                       op0=ALU.mult, op1=ALU.add)
                    ins.then_inc(conv_done.sem, 1)
                wait(dve, tail_turned, j)
                wait(dve, tail_stored, j, 0)
                dve.tensor_copy(tail_rows[:].rearrange("p y n -> p (y n)"), ps[0:TAPS - 1 + DEC, 7, 0:3 * P]).then_inc(tail_out.sem, 1)
                dec_sum_pages(1)
                dec_result(1)
                wait(dve, rows_loaded, j)
                dve.tensor_copy(gs[:, GLAST], blocks(gc_row)[:, :, P - 1])
                dve.drain()
                dve.tensor_tensor(gs[:, KD], gs[:, GLAST], gs[:, GCUM], ALU.subtract).then_inc(g_ready.sem, 1)
                wait(dve, l2_done, j)
                dve.tensor_tensor(blocks(decayT), blocks(gc_row), gs[:, GCUM].unsqueeze(2).broadcast_to([P, NBLK, P]), ALU.subtract)
                dve.drain()
                dve.tensor_scalar(decayT, decayT, 0.0, None, ALU.min).then_inc(dif_ready.sem, 1)
                wait(dve, l2_rstd, j, 1)
                dve.tensor_tensor(conv[:, 1], conv[:, 1], rs_qk[:, 1], ALU.mult).then_inc(l2_out.sem, 1)
                dve.drain()
                dve.tensor_tensor(k_scaled, conv[:, 1, 0:SEQ], beta_row, ALU.mult).then_inc(k_scaled_ready.sem, 1)
                wait(dve, l2_rstd, j, 2)
                dve.tensor_tensor(conv[:, 0], conv[:, 0], rs_qk[:, 0], ALU.mult).then_inc(l2_out.sem, 1)
                wait(dve, gs_exp, j)
                dve.scalar_tensor_tensor(out=gs[:, KB], in0=gs[:, BETA], scalar=-1.0, in1=gs[:, EG], op0=ALU.mult, op1=ALU.mult)
                dve.drain()
                wait(dve, gnat_turned, j)
                for hf in range(2):
                    cs = slice(4 * hf, 4 * hf + 4)
                    kps, vps = (ps[:, bank + hf].rearrange("p (c i) -> p c i", c=4) for bank in (2, 4))
                    for out, src, which in ((k_dec, kps, KD), (k_beta, kps, KB), (v_beta, vps, BETA)):
                        ins = dve.tensor_tensor(blocks(out)[:, cs], src, gs[:, which, cs].unsqueeze(2).broadcast_to([P, 4, P]), ALU.mult)
                ins.then_inc(gnat_out.sem, 1)
                wait(dve, kk_done, j)
                wait(dve, dec_masked, j)
                for hf in range(2):
                    ins = dve.tensor_tensor(aT[:, 512 * hf:512 * (hf + 1)], ps[:, 6 + hf], decayT[:, 512 * hf:512 * (hf + 1)], ALU.mult)
                ins.then_inc(a_ready.sem, 1)
                wait(dve, gqk_done, j)
                for hf in range(2):
                    dve.tensor_tensor(qkT[:, 512 * hf:512 * (hf + 1)], ps[:, 2 + hf], decayT[:, 512 * hf:512 * (hf + 1)], ALU.mult)
                wait(dve, eg_row_ready, j)
                dve.tensor_tensor(conv[:, 0, 0:SEQ], conv[:, 0, 0:SEQ], eg_row, ALU.mult).then_inc(q_ready.sem, 1)
                wait(dve, level_ready, j, 1)
                dve.tensor_tensor(invT, v.ident[:].unsqueeze(1).broadcast_to([P, NBLK, P]), levelT[0], ALU.subtract).then_inc(y0_ready.sem, 1)
                wait(dve, y0_turned, j)
                for hf in range(2):
                    ins = dve.tensor_copy(inv[:, 4 * hf:4 * hf + 4], ps[:, 4 + hf].rearrange("p (c i) -> p c i", c=4))
                ins.then_inc(x0_ready.sem, 1)
                for n in range(12):
                    hf = n % 2
                    cs = slice(4 * hf, 4 * hf + 4)
                    l = 1 + n // 2
                    wait(dve, xy_done, j, n + 1)
                    if n < 10:
                        x = halves(inv[:, cs].rearrange("p c i -> p (c i)"), l)[:, :, 0]
                        dve.tensor_tensor(x, x, ps[:, 4 + hf, 0:256].rearrange("p (n w) -> p n w", w=1 << l), ALU.subtract)
                    y = halves(invT[:, cs].rearrange("p c i -> p (c i)"), l)[:, :, 1]
                    dve.tensor_tensor(y, y, ps[:, 6 + hf, 0:256].rearrange("p (n w) -> p n w", w=1 << l), ALU.subtract).then_inc(xy_out.sem, 1)
                wait(dve, w_done, j)
                for hf in range(2):
                    ins = dve.tensor_copy(wT[:, 4 * hf:4 * hf + 4], ps[:, 2 + hf].rearrange("p (c i) -> p c i", c=4))
                ins.then_inc(w_out_.sem, 1)
                wait(dve, state_stored, j, 0)
                dve.memset(state[:], 0.0).then_inc(state_zero.sem, 1)
                for c in range(NBLK):
                    dve.drain()
                    wait(dve, sc_done, j, c + 1)
                    dve.scalar_tensor_tensor(out=state[:], in0=state[:], scalar=gs[:, EGL, c:c + 1], in1=ps[:, 2 + c % 2, 0:GD],
                                             op0=ALU.mult, op1=ALU.add).then_inc(sc_out.sem, 1)
                dec = conv[:, :, SEQ:CONV].rearrange("p y (b i) -> p y b i", i=TAPS)[:, :, :, TAPS - 1]
                dve.tensor_copy(kq[:, :, 0], dec[:, 1])
                dve.tensor_copy(kq[:, :, 1], dec[:, 0])
                dve.tensor_tensor(kq_prod, dec[:, 0], dec[:, 1], ALU.mult)
                wait(dve, s_loaded, j)
                dve.tensor_tensor(blocks(s_dec), blocks(s_dec), dg[:, 0].unsqueeze(2).broadcast_to([P, DEC, GD]), ALU.mult).then_inc(kq_ready.sem, 1)
                wait(dve, sdec_done, j)
                dve.tensor_copy(kq_dot, ps[:, 5, 0:DEC])
                sk = ps[:, 4, 0:2 * DEC].rearrange("p (b n) -> p b n", n=2)
                dve.tensor_tensor(delta, dec[:, 2], sk[:, :, 0], ALU.subtract)
                dve.drain()
                dve.tensor_tensor(delta, delta, dg[:, 1], ALU.mult)
                dve.drain()
                dve.tensor_tensor(d_tmp, delta, kq_dot, ALU.mult)
                dve.drain()
                dve.tensor_tensor(oT[:, SEQ:TOK], d_tmp, sk[:, :, 1], ALU.add).then_inc(delta_ready.sem, 1)
                wait(dve, rows_turned, j)
                dve.tensor_copy(nat_dec.rearrange("p n d -> p (n d)"), ps[0:DEC, 4, 0:2 * P])
                dve.drain()
                dve.tensor_tensor(delta_diag, nat_dec[:, 1].unsqueeze(1).broadcast_to([DEC, DEC, P]),
                                  v.ident[0:DEC, 0:DEC].unsqueeze(2).broadcast_to([DEC, DEC, P]), ALU.mult).then_inc(diag_ready.sem, 1)
                wait(dve, outer_done, j)
                for hf in range(2):
                    ins = dve.tensor_tensor(s_dec[:, 512 * hf:512 * (hf + 1)], s_dec[:, 512 * hf:512 * (hf + 1)], ps[:, 2 + hf], ALU.add)
                ins.then_inc(sdec_ready.sem, 1)
                wait(dve, orstd_ready, j)
                dve.scalar_tensor_tensor(out=oT, in0=oT, scalar=v.out_norm[:], in1=o_rstd, op0=ALU.mult, op1=ALU.mult)
                dve.drain()
                dve.tensor_tensor(oT, oT, z_silu[:], ALU.mult).then_inc(o_ready.sem, 1)

            each_step(dve, step)
            for c in (nat_stored, mix_stored, tail_stored, state_stored):
                wait(dve, c, STEPS - 1)


def out_projection(nc, t, v, act_t, w, up, S):
    with ExitStack() as scope:
        ps = v.ps
        xT = act_t[:, 0:KC]
        mix = act_t[:, KC:2 * KC]
        sq = act_t[:, 2 * KC:2 * KC + 2]
        rstd = act_t[:, 2 * KC + 2]
        w_raw, w_hi, w_lo = w
        mix_loaded = [v.sem(f"mix_loaded{k}") for k in range(KC)]
        w_loaded = [v.sem("wo_loaded0"), v.sem("wo_loaded1")]
        x_loaded, mix_hi, mix_lo = v.sem("x1_loaded"), v.sem("mix_hi"), v.sem("mix_lo")
        w_split_hi, w_split_lo = v.sem("wo_split_hi"), v.sem("wo_split_lo")
        piece_done, piece_out, x_saved = v.sem("wo_piece_done"), v.sem("wo_piece_out"), v.sem("x1_saved")
        w_view = t["w_out"][0].rearrange("(k p) n -> p k n", p=P)

        block = scope.enter_context(nc.Block())

        @block.sync
        def _(sp):
            for i in range(2):
                sp.dma_start(w_raw[:, i], w_view[:, :, i * P:(i + 1) * P]).then_inc(w_loaded[i], 16)
            for k in range(KC):
                sp.dma_start(mix[:, k], v.mix_dram[k]).then_inc(mix_loaded[k], 16)
            sp.dma_start(xT, v.x_dram).then_inc(x_loaded, 16)
            with sp.Fori(1, KC // 2) as it:
                for i in range(2):
                    sp.wait_ge(w_split_lo, it * 2 + i - 1)
                    sp.dma_start(w_raw[:, i], w_view[:, :, ds((it * 2 + i) * P, P)]).then_inc(w_loaded[i], 16)
            w_up = t["w_up"][0].rearrange("(k p) n -> p k n", p=P)
            for i in range(2):
                sp.wait_ge(w_split_lo, KC - 1 + i)
                sp.dma_start(w_raw[:, i], w_up[:, :, FFN * i:FFN * i + P]).then_inc(up["loaded"][i], 16)
            sp.wait_ge(piece_out, NG * KC)
            sp.dma_start(v.x_dram, xT).then_inc(x_saved, 16)
            sp.wait_ge(x_saved, 16)

        @block.scalar
        def _(act):
            for i in range(2):
                act.wait_ge(w_loaded[i], 16)
                act.activation(w_hi[:, i], w_raw[:, i], ACT.Copy).then_inc(w_split_hi, 1)
            for k in range(KC):
                act.wait_ge(mix_loaded[k], 16)
                act.activation(v.hi[:, k], mix[:, k], ACT.Copy).then_inc(mix_hi, 1)
            with act.Fori(1, KC // 2) as it:
                for i in range(2):
                    act.wait_ge(w_loaded[i], it * 16 + 16)
                    act.wait_ge(piece_done, it * 6 + 3 * (i - 1))
                    act.activation(w_hi[:, i], w_raw[:, i], ACT.Copy).then_inc(w_split_hi, 1)
            for i in range(2):
                act.wait_ge(up["loaded"][i], 16)
                act.wait_ge(piece_done, NG * (KC - 1 + i))
                act.activation(w_hi[:, i], w_raw[:, i], ACT.Copy).then_inc(up["hi"], 1)
            norm_rstd(act, v, S, rstd)
            norm_hi(act, v, S, mix, BY_GROUP[:1])

        @block.gpsimd
        def _(pool):
            with pool.Fori(0, KC // 2) as it:
                for i in range(2):
                    pool.wait_ge(w_split_hi, it * 2 + i + 1)
                    pool.tensor_tensor(w_lo[:, i], w_raw[:, i], w_hi[:, i].bitcast(F32), ALU.subtract).then_inc(w_split_lo, 1)
            for i in range(2):
                pool.wait_ge(up["hi"], i + 1)
                pool.tensor_tensor(w_lo[:, i], w_raw[:, i], w_hi[:, i].bitcast(F32), ALU.subtract).then_inc(up["lo"], 1)
            norm_pool(pool, v, S, mix, BY_GROUP[:1])

        @block.tensor
        def _(pe):
            pe.wait_ge(w_split_lo, 1)
            for k in range(KC):
                pe.wait_ge(mix_lo, k + 1)
                for g in range(NG):
                    mm = split_piece(pe, ps[:, g, 0:GRP], w_hi[:, 0, k], w_lo[:, 0, k],
                                     v.hi[:, k, g * GRP:(g + 1) * GRP], v.lo[:, k, g * GRP:(g + 1) * GRP],
                                     k == 0, k == KC - 1)
                    if k == KC - 1:
                        mm.then_inc(piece_done, 1)

            def tile(n, i, first):
                pe.wait_ge(w_split_lo, n + 1)
                for g in range(NG):
                    if not first:
                        pe.wait_ge(piece_out, n * NG + (g + 1 - 2 * NG))
                    for k in range(KC):
                        mm = split_piece(pe, ps[:, NG * i + g, 0:GRP], w_hi[:, i, k], w_lo[:, i, k],
                                         v.hi[:, k, g * GRP:(g + 1) * GRP], v.lo[:, k, g * GRP:(g + 1) * GRP],
                                         k == 0, k == KC - 1)
                    mm.then_inc(piece_done, 1)

            tile(1, 1, True)
            with pe.Fori(1, KC // 2) as it:
                for i in range(2):
                    tile(it * 2 + i, i, False)
            norm_pe(pe, v, S, sq[:, 1])

        @block.vector
        def _(dve):
            for k in range(KC):
                dve.wait_ge(mix_hi, k + 1)
                dve.tensor_tensor(v.lo[:, k], mix[:, k], v.hi[:, k].bitcast(F32), ALU.subtract).then_inc(mix_lo, 1)
            dve.memset(sq[:, 1], 0.0)
            dve.wait_ge(x_loaded, 16)
            with dve.Fori(0, KC // 2) as it:
                for i in range(2):
                    for g in range(NG):
                        dve.wait_ge(piece_done, it * (2 * NG) + (NG * i + g + 1))
                        x = xT[:, ds(it * 2 + i, 1), g * GRP:(g + 1) * GRP].rearrange("p a n -> p (a n)")
                        dve.tensor_tensor(x, x, ps[:, NG * i + g, 0:GRP], ALU.add).then_inc(piece_out, 1)
                    dve.drain()
                    add_squares(dve, xT[:, ds(it * 2 + i, 1)].rearrange("p a n -> p (a n)"), sq)
            dve.drain().then_inc(S["squared"], 1)
            dve.wait_ge(S["rstd"], 1)
            norm_dve(dve, v, S, xT, rstd, mix, 1, BY_GROUP[:1])


def dense(nc, t, v):
    with ExitStack() as outer:
        act_t = v.sb("ffn_act", [P, FT, TOK], F32, outer)
        with ExitStack() as scope:
            w = [v.sb(name, [P, 2, KC, P], dt, scope) for name, dt in (("w2_raw", F32), ("w2_hi", F32R), ("w2_lo", F32R))]
            up = {"loaded": [v.sem("wu_loaded0"), v.sem("wu_loaded1")], "hi": v.sem("wu_split_hi"), "lo": v.sem("wu_split_lo")}
            S = norm_signals(v, "n1")
            out_projection(nc, t, v, act_t, w, up, S)
            ffn_up(nc, t, v, act_t, w, up, S)
        xT = v.sb("xT2", [P, KC, TOK], F32, outer)
        sq = act_t[:, 0:2]
        S = norm_signals(v, "n2")
        ffn_down(nc, t, v, act_t, xT, sq, S)
        finish(nc, t, v, act_t, xT, sq, S)


def ffn_up(nc, t, v, act_t, w, up, S):
    with ExitStack() as scope:
        def sb(name, shape, dt=F32):
            return v.sb(name, shape, dt, scope)

        ps = v.ps
        w_raw, w_hi, w_lo = w
        xT, normed, rstd = act_t[:, 0:KC], act_t[:, KC:2 * KC], act_t[:, 2 * KC + 2]
        gate = sb("gate_ext", [P, FEXT])
        y = sb("gate_conv", [P, FCONV])
        par = sb("fconv_f", [P, 20])
        tail = sb("gate_tail", [P, FTAPS - 1 + DEC])
        tail_rows = sb("gate_tail_rows", [FTAPS - 1 + DEC, P])
        w_loaded, w_split_hi, w_split_lo = up["loaded"], up["hi"], up["lo"]
        piece_done, gate_out, up_out = v.sem("wu_piece_done"), v.sem("gate_out"), v.sem("up_out")
        conv_done, silu_done = v.sem("gate_conv_done"), v.sem("gate_silu_done")
        tail_ready, tail_turned, tail_out, tail_stored = v.sem("gt_ready"), v.sem("gt_turned"), v.sem("gt_out"), v.sem("gt_stored")
        ctx_copied, gate_zeroed = v.sem("gate_ctx_copied"), v.sem("gate_zeroed")
        w_view = t["w_up"][0].rearrange("(k p) n -> p k n", p=P)

        block = scope.enter_context(nc.Block())

        @block.sync
        def _(sp):
            sp.dma_start(t["new_ffn_conv_sample"][0, :, 0:1, :], t["state_ffn_conv"][0, :, 1:2, :]).then_inc(ctx_copied, 16)
            with sp.Fori(1, FT) as f:
                for i in range(2):
                    sp.wait_ge(w_split_lo, f * 2 + (i + 1 - 2))
                    sp.dma_start(w_raw[:, i], w_view[:, :, ds(f * P + FFN * i, P)]).then_inc(w_loaded[i], 16)
            sp.wait_ge(ctx_copied, 16)

        @block.gpsimd
        def _(pool):
            pool.memset(gate[:, 0:FTAPS - 1], 0.0).then_inc(gate_zeroed, 1)
            norm_pool(pool, v, S, normed, BY_GROUP[1:])
            with pool.Fori(1, FT) as f:
                for i in range(2):
                    pool.wait_ge(w_split_hi, f * 2 + (i + 1))
                    pool.tensor_tensor(w_lo[:, i], w_raw[:, i], w_hi[:, i].bitcast(F32), ALU.subtract).then_inc(w_split_lo, 1)

        @block.tensor
        def _(pe):
            pe.sem_inc(piece_done, 2 * NG)
            pe.sem_inc(tail_turned, 1)
            with pe.Fori(0, FT) as f:
                for i in range(2):
                    pe.wait_ge(w_split_lo, f * 2 + (i + 1))
                    for g in range(NG):
                        pe.wait_ge(S["even_lo"], g + 1)
                        pe.wait_ge(S["odd_lo"], g + 1)
                        pe.wait_ge((gate_out, up_out)[i], f * NG + (g + 1))
                        for k in range(KC):
                            mm = split_piece(pe, ps[:, NG * i + g, 0:GRP], w_hi[:, i, k], w_lo[:, i, k],
                                             v.hi[:, k, g * GRP:(g + 1) * GRP], v.lo[:, k, g * GRP:(g + 1) * GRP],
                                             k == 0, k == KC - 1)
                        mm.then_inc(piece_done, 1)
                        if i == 1 and g == 0:
                            pe.wait_ge(tail_ready, f + 1)
                            pe.transpose(ps[0:FTAPS - 1 + DEC, 6, 0:P], tail[:], v.ident[:]).then_inc(tail_turned, 1)

        @block.scalar
        def _(act):
            act.sem_inc(gate_out, NG)
            act.sem_inc(tail_stored, 32)
            norm_hi(act, v, S, normed, BY_GROUP[1:])
            act.wait_ge(gate_zeroed, 1)
            def split(f, i):
                act.wait_ge(w_loaded[i], f * 16 + 32)
                act.wait_ge(piece_done, f * (2 * NG) + NG * (i + 3))
                act.activation(w_hi[:, i], w_raw[:, i], ACT.Copy).then_inc(w_split_hi, 1)

            def channel_tile(f):
                act.wait_ge(conv_done, f + 1)
                for g in range(NG):
                    act.wait_ge(piece_done, f * (2 * NG) + (2 * NG + g + 1))
                    a = g * GRP
                    n = min(GRP, SEQ - a)
                    ins = act.activation(gate[:, FTAPS - 1 + a:FTAPS - 1 + a + n], ps[:, g, 0:n], ACT.Copy)
                    if n < GRP:
                        ins = act.activation(gate[:, FTAPS - 1 + SEQ:].rearrange("p (b i) -> p b i", b=DEC)[:, :, FTAPS - 1], ps[:, g, n:GRP], ACT.Copy)
                    ins.then_inc(gate_out, 1)
                act.wait_ge(conv_done, f + 2)
                act.activation(y[:], y[:], ACT.Silu).then_inc(silu_done, 1)
                act.wait_ge(tail_out, f + 2)
                act.dma_start(t["new_ffn_conv_prompt"][0, 0, :, ds(f * P, P)], tail_rows[0:FTAPS - 1]).then_inc(tail_stored, 16)
                act.dma_start(t["new_ffn_conv_sample"][0, :, FTAPS - 2, ds(f * P, P)], tail_rows[FTAPS - 1:]).then_inc(tail_stored, 16)

            with act.Fori(0, FT - 1) as f:
                channel_tile(f)
                split(f, 0)
                split(f, 1)
            channel_tile(FT - 1)
            act.wait_ge(tail_stored, 32 * (FT + 1))

        @block.vector
        def _(dve):
            dve.sem_inc(up_out, NG)
            dve.sem_inc(conv_done, 1)
            dve.sem_inc(tail_out, 1)
            norm_dve(dve, v, S, xT, rstd, normed, 1, BY_GROUP[1:])
            with dve.Fori(0, FT) as f:
                dve.tensor_copy(par[:].unsqueeze(1), v.fconv[:, ds(f, 1), :])
                dve.drain()
                decode = gate[:, FTAPS - 1 + SEQ:].rearrange("p (b i) -> p b i", b=DEC)
                dve.tensor_copy(decode[:, :, 0:FTAPS - 1], par[:, 4:20].rearrange("p (b i) -> p b i", b=DEC))
                dve.wait_ge(gate_out, f * NG + 2 * NG)
                dve.wait_ge(tail_turned, f + 1)
                dve.tensor_copy(tail[:, 0:FTAPS - 1], gate[:, SEQ:SEQ + FTAPS - 1])
                dve.tensor_copy(tail[:, FTAPS - 1:], decode[:, :, FTAPS - 1]).then_inc(tail_ready, 1)
                dve.drain()
                dve.tensor_scalar(y[:], gate[:, 0:FCONV], par[:, 0:1], par[:, 3:4], ALU.mult, ALU.add)
                for i in range(1, FTAPS):
                    dve.drain()
                    ins = dve.scalar_tensor_tensor(out=y[:], in0=gate[:, i:i + FCONV], scalar=par[:, i:i + 1], in1=y[:], op0=ALU.mult, op1=ALU.add)
                ins.then_inc(conv_done, 1)
                dve.wait_ge(tail_turned, f + 2)
                dve.wait_ge(tail_stored, f * 32 + 32)
                dve.tensor_copy(tail_rows[:], ps[0:FTAPS - 1 + DEC, 6, 0:P]).then_inc(tail_out, 1)
                dve.wait_ge(silu_done, f + 1)
                for g in range(NG):
                    dve.wait_ge(piece_done, f * (2 * NG) + (3 * NG + g + 1))
                    a = g * GRP
                    n = min(GRP, SEQ - a)
                    ins = dve.tensor_tensor(act_t[:, ds(f, 1), a:a + n].rearrange("p a n -> p (a n)"), y[:, a:a + n], ps[:, NG + g, 0:n], ALU.mult)
                    if n < GRP:
                        yd = y[:, SEQ:FCONV].rearrange("p (b i) -> p b i", b=DEC)[:, :, FTAPS - 1]
                        ins = dve.tensor_tensor(act_t[:, ds(f, 1), SEQ:TOK].rearrange("p a n -> p (a n)"), yd, ps[:, NG + g, n:GRP], ALU.mult)
                    ins.then_inc(up_out, 1)


def ffn_down(nc, t, v, act_t, xT, sq, S):
    with ExitStack() as scope:
        def sb(name, shape, dt=F32):
            return v.sb(name, shape, dt, scope)

        ps = v.ps
        COLS = 2
        PASSES = KC // COLS
        w_raw = sb("wd_raw", [P, 2, COLS * P])
        w_hi = sb("wd_hi", [P, 2, COLS * P], F32R)
        w_lo = sb("wd_lo", [P, 2, COLS * P], F32R)
        w_loaded = [v.sem("wd_loaded0"), v.sem("wd_loaded1")]
        w_split_hi, w_split_lo, used = v.sem("wd_split_hi"), v.sem("wd_split_lo"), v.sem("wd_used")
        a_hi, a_lo = v.sem("ffn_act_hi"), v.sem("ffn_act_lo")
        pass_out = v.sem("down_pass_out")
        x_loaded = v.sem("x2_loaded")
        CREDIT = 2
        KEPT = 6

        block = scope.enter_context(nc.Block())

        def over_chunks(eng, c, step):
            def pair(k, kept, first, last):
                for i in range(2):
                    step(c * FT + (k + i), k + i, i, 2 + k + i if kept else i, first and i == 0, last and i == 1)
            for k in range(0, KEPT, 2):
                pair(k, True, k == 0, False)
            with eng.Fori(KEPT // 2, FT // 2 - 1) as it:
                pair(it * 2, False, False, False)
            pair(FT - 2, False, False, True)

        @block.sync
        def _(sp):
            with sp.Fori(0, PASSES) as c:
                def load(n, k, i, slot, first, last):
                    sp.wait_ge(w_split_lo, n + (1 - 2 + CREDIT))
                    sp.dma_start(w_raw[:, i], t["w_down"][0, ds(k * P, P), ds(c * (COLS * P), COLS * P)]).then_inc(w_loaded[i], 16)

                over_chunks(sp, c, load)

        @block.gpsimd
        def _(pool):
            pool.sem_inc(w_split_lo, CREDIT)
            pool.dma_start(xT[:], v.x_dram).then_inc(x_loaded, 16)
            with pool.Fori(0, PASSES) as c:
                def split(n, k, i, slot, first, last):
                    pool.wait_ge(w_split_hi, n + 1)
                    pool.tensor_tensor(w_lo[:, i], w_raw[:, i], w_hi[:, i].bitcast(F32), ALU.subtract).then_inc(w_split_lo, 1)

                over_chunks(pool, c, split)

        @block.scalar
        def _(act):
            for k in range(KEPT):
                act.activation(v.hi[:, 2 + k], act_t[:, k], ACT.Copy).then_inc(a_hi, 1)
            with act.Fori(0, PASSES) as c:
                def split(n, k, i, slot, first, last):
                    act.wait_ge(used, n + (1 - 2 + CREDIT))
                    if slot < 2:
                        act.activation(v.hi[:, slot], act_t[:, ds(k, 1)].rearrange("p a n -> p (a n)"), ACT.Copy).then_inc(a_hi, 1)
                    act.wait_ge(w_loaded[i], c * (8 * FT) + (k - i) * 8 + 16)
                    act.activation(w_hi[:, i], w_raw[:, i], ACT.Copy).then_inc(w_split_hi, 1)

                over_chunks(act, c, split)

        @block.tensor
        def _(pe):
            pe.sem_inc(used, CREDIT)
            with pe.Fori(0, PASSES) as c:
                def multiply(n, k, i, slot, first, last):
                    if slot < 2:
                        pe.wait_ge(a_lo, c * (FT - KEPT) + (k + 1))
                    else:
                        pe.wait_ge(a_lo, k + 1)
                    pe.wait_ge(w_split_lo, n + (1 + CREDIT))
                    for m in range(COLS):
                        for g in range(NG):
                            if first:
                                pe.wait_ge(pass_out, c * (COLS * NG) + (m * NG + g + 1))
                            cols = slice(m * P, (m + 1) * P)
                            mm = split_piece(pe, ps[:, m * NG + g, 0:GRP], w_hi[:, i, cols], w_lo[:, i, cols],
                                             v.hi[:, slot, g * GRP:(g + 1) * GRP], v.lo[:, slot, g * GRP:(g + 1) * GRP],
                                             first, last)
                    mm.then_inc(used, 1)

                over_chunks(pe, c, multiply)

        @block.vector
        def _(dve):
            dve.sem_inc(pass_out, COLS * NG)
            for k in range(KEPT):
                dve.wait_ge(a_hi, k + 1)
                dve.tensor_tensor(v.lo[:, 2 + k], act_t[:, k], v.hi[:, 2 + k].bitcast(F32), ALU.subtract).then_inc(a_lo, 1)
            dve.drain()
            dve.memset(sq[:, 1], 0.0)
            with dve.Fori(0, PASSES) as c:
                def split(n, k, i, slot, first, last):
                    if slot < 2:
                        dve.wait_ge(a_hi, c * (FT - KEPT) + (k + 1))
                        dve.tensor_tensor(v.lo[:, slot], act_t[:, ds(k, 1)].rearrange("p a n -> p (a n)"), v.hi[:, slot].bitcast(F32),
                                          ALU.subtract).then_inc(a_lo, 1)

                over_chunks(dve, c, split)
                dve.wait_ge(x_loaded, 16)
                dve.wait_ge(used, c * FT + (FT + CREDIT))
                for m in range(COLS):
                    for g in range(NG):
                        x = xT[:, ds(c * COLS + m, 1), g * GRP:(g + 1) * GRP].rearrange("p a n -> p (a n)")
                        dve.tensor_tensor(x, x, ps[:, m * NG + g, 0:GRP], ALU.add).then_inc(pass_out, 1)
                for m in range(COLS):
                    dve.drain()
                    add_squares(dve, xT[:, ds(c * COLS + m, 1)].rearrange("p a n -> p (a n)"), sq)
            dve.drain().then_inc(S["squared"], 1)


def finish(nc, t, v, act_t, xT, sq, S):
    with ExitStack() as scope:
        ps = v.ps
        rstd = act_t[:, 2]
        SLOTS = 4
        rows = act_t[:, 3:3 + SLOTS, 0:D]
        y_ready, y_turned, y_copied = v.sem("y_ready"), v.sem("y_turned"), v.sem("y_copied")
        y_stored = [v.sem(f"y_stored{i}") for i in range(SLOTS)]

        block = scope.enter_context(nc.Block())

        @block.vector
        def _(dve):
            dve.wait_ge(S["rstd"], 1)
            for cols in (slice(0, SEQ // 2), slice(SEQ // 2, TOK)):
                for k in range(KC):
                    ins = dve.scalar_tensor_tensor(out=xT[:, k, cols], in0=xT[:, k, cols], scalar=v.norms[:, k, 2:3],
                                                   in1=rstd[:, cols], op0=ALU.mult, op1=ALU.mult)
                ins.then_inc(y_ready, 1)

        @block.tensor
        def _(pe):
            norm_pe(pe, v, S, sq[:, 1])
            pe.wait_ge(S["rstd"], 1)

            def turn(first, i, width):
                for k in range(KC):
                    mm = pe.transpose(ps[0:width, 2 * i + k // 4, (k % 4) * P:(k % 4 + 1) * P],
                                      xT[:, k, ds(first, width)], v.ident[:])
                mm.then_inc(y_turned, 1)

            pe.wait_ge(y_ready, 1)
            for i in range(SLOTS):
                turn(i * P, i, P)
            pe.wait_ge(y_ready, 2)
            for n in range(SLOTS, NBLK + 1):
                pe.wait_ge(y_copied, n - SLOTS + 1)
                turn(n * P, n % SLOTS, P if n < NBLK else DEC)

        @block.scalar
        def _(act):
            norm_rstd(act, v, S, rstd)
            for n in range(NBLK + 1):
                i, width = n % SLOTS, P if n < NBLK else DEC
                act.wait_ge(y_turned, n + 1)
                if n >= SLOTS:
                    act.wait_ge(y_stored[i], 16 * (n // SLOTS))
                act.activation(rows[0:width, i], ps[0:width, 2 * i:2 * i + 2].rearrange("p a n -> p (a n)"), ACT.Copy).then_inc(y_copied, 1)

        @block.sync
        def _(sp):
            for n in range(NBLK + 1):
                i = n % SLOTS
                sp.wait_ge(y_copied, n + 1)
                if n < NBLK:
                    sp.dma_start(t["y_prompt"][0, n * P:(n + 1) * P], rows[:, i]).then_inc(y_stored[i], 16)
                else:
                    sp.dma_start(t["y_sample"].rearrange("b a d -> (b a) d"), rows[0:DEC, i]).then_inc(y_stored[i], 16)
            for i in range(SLOTS):
                sp.wait_ge(y_stored[i], 16 * (2 + (i == 0)))


INPUTS = ["x_prompt", "x_sample", "cache_k", "cache_v", "cache_logf", "state_gdn", "state_gdn_conv",
          "state_ffn_conv", "page_table", "norm_mix", "w_in", "b_forget", "gdn_a_log", "gdn_dt_bias",
          "w_gdn_conv", "gdn_out_norm", "w_out", "norm_ffn", "w_up", "w_ffn_conv", "b_ffn_conv", "w_down",
          "norm_final"]
OUTPUTS = [("y_prompt", (1, SEQ, D)), ("y_sample", (DEC, 1, D)),
           ("new_k_prompt", (1, 1, SEQ, FH, FD)), ("new_v_prompt", (1, 1, SEQ, FH, FD)),
           ("new_logf_prompt", (1, 1, SEQ, FH)), ("new_gdn_prompt", (1, 1, GH, GD, GD)),
           ("new_gdn_conv_prompt", (1, 1, TAPS - 1, 3 * GW)), ("new_ffn_conv_prompt", (1, 1, FTAPS - 1, FFN)),
           ("new_k_sample", (1, DEC, 1, FH, FD)), ("new_v_sample", (1, DEC, 1, FH, FD)),
           ("new_logf_sample", (1, DEC, 1, FH)), ("new_gdn_sample", (1, DEC, GH, GD, GD)),
           ("new_gdn_conv_sample", (1, DEC, TAPS - 1, 3 * GW)), ("new_ffn_conv_sample", (1, DEC, FTAPS - 1, FFN))]


def kernel(**inputs):
    import numpy as np
    import concourse.bacc as bacc
    from concourse import mybir as mb
    from concourse.bass_utils import run_bass_kernel_spmd

    nc = bacc.Bacc("TRN2", target_bir_lowering=False, num_devices=1)
    arrays, t = {}, {}
    for name in INPUTS:
        a = np.ascontiguousarray(inputs[name])
        arrays[f"in_{name}"] = a
        t[name] = nc.dram_tensor(f"in_{name}", a.shape, mb.dt.from_np(a.dtype), kind="ExternalInput").ap()
    for name, shape in OUTPUTS:
        t[name] = nc.dram_tensor(f"out_{name}", shape, mb.dt.float32, kind="ExternalOutput").ap()
    program(nc, t)
    r = run_bass_kernel_spmd(nc, [arrays], core_ids=[0])
    return tuple(r.results[0][f"out_{name}"] for name, _ in OUTPUTS)
```
